# Optimizing a Trainium2 kernel written in Bass

```python
import math
import jax, jax.numpy as jnp
from jax import lax
import numpy as np

D_MODEL = 1024
BATCH = 1
SEQ = 256
DEPTH = 2

N_EVEN = (DEPTH + 1) // 2
N_ODD = DEPTH // 2
BLOCK = 128
EPS = 1e-6

MLA_HEADS = 8
MLA_NOPE = 64
MLA_ROPE = 32
MLA_V = 64
MLA_Q_RANK = 256
MLA_KV_RANK = 128
ROPE_THETA = 10000.0

DIL_HEADS = 8
DIL_HD = 64
DIL_PATTERNS = ((128, 1), (512, 4), (2048, 16))

DIFF_HEADS = 4
DIFF_HD = 64

SB_HEADS = 8
SB_HD = 64

REL_BUCKETS = 32
REL_MAX_DIST = 2048
REL_MAPS = 8

D_FF = 2816
N_EXPERTS = 8
TOP_K = 2
D_FF_EXPERT = 3584

MLA_IN = MLA_Q_RANK + MLA_KV_RANK + MLA_ROPE
EVEN_IN = MLA_IN + 3 * DIL_HEADS * DIL_HD
EVEN_MIX = MLA_HEADS * MLA_V + DIL_HEADS * DIL_HD
DIFF_W = DIFF_HEADS * 2 * DIFF_HD
ODD_IN = 3 * DIFF_W + 3 * SB_HEADS * SB_HD
ODD_MIX = DIFF_W + SB_HEADS * SB_HD

kernel_name = 'hybrid_mla_dilated_diff_stickbreak_moe'

F32 = jnp.float32

def rmsnorm(x, g):
    xf = x.astype(F32)
    y = xf * lax.rsqrt(jnp.mean(xf * xf, axis=-1, keepdims=True) + EPS) * g.astype(F32)
    return y.astype(x.dtype)

def ada_modulation(c, w, b):
    m = jax.nn.silu(c) @ w + b
    shift, scale, gate = jnp.split(m, 3, axis=-1)
    return shift, scale, gate

def modulate(h, shift, scale):
    return h * (1 + scale[:, None, :]) + shift[:, None, :]

def rope(x, pos):
    half = x.shape[-1] // 2
    freqs = ROPE_THETA ** (-jnp.arange(half, dtype=F32) / half)
    ang = pos.astype(F32)[:, None] * freqs[None, :]
    cos = jnp.cos(ang)[:, None, :]
    sin = jnp.sin(ang)[:, None, :]
    x1 = x[..., :half].astype(F32)
    x2 = x[..., half:].astype(F32)
    return jnp.concatenate([x1 * cos - x2 * sin, x1 * sin + x2 * cos], axis=-1).astype(x.dtype)

def t5_bucket(dist):
    max_exact = REL_BUCKETS // 2
    d = jnp.maximum(dist, 1).astype(F32)
    log_b = max_exact + (jnp.log(d / max_exact) / math.log(REL_MAX_DIST / max_exact)
                         * (REL_BUCKETS - max_exact)).astype(jnp.int32)
    log_b = jnp.minimum(log_b, REL_BUCKETS - 1)
    return jnp.where(dist < max_exact, dist, log_b)

def to_query_blocks(t):
    b, s = t.shape[:2]
    t = t.reshape((b, s // BLOCK, BLOCK) + t.shape[2:])
    return jnp.moveaxis(t, 1, 0)

def from_query_blocks(t):
    t = jnp.moveaxis(t, 0, 1)
    return t.reshape((t.shape[0], t.shape[1] * t.shape[2]) + t.shape[3:])

def mla_attention(q_nope, q_rope, k_nope, k_rope, v):
    s_len = q_nope.shape[1]
    scale = (MLA_NOPE + MLA_ROPE) ** -0.5
    kpos = jnp.arange(s_len)

    def block(args):
        qn, qr, bi = args
        qpos = bi * BLOCK + jnp.arange(BLOCK)
        s = (jnp.einsum('bqhd,bkhd->bhqk', qn, k_nope, preferred_element_type=F32)
             + jnp.einsum('bqhr,bkr->bhqk', qr, k_rope, preferred_element_type=F32)) * scale
        s = jnp.where(kpos[None, :] <= qpos[:, None], s, -jnp.inf)
        p = jax.nn.softmax(s, axis=-1)
        return jnp.einsum('bhqk,bkhd->bqhd', p.astype(v.dtype), v)

    nb = s_len // BLOCK
    o = lax.map(block, (to_query_blocks(q_nope), to_query_blocks(q_rope), jnp.arange(nb)))
    return from_query_blocks(o)

def dilated_attention(q, k, v, rel_bias):
    b, s_len, h, dh = q.shape
    scale = dh ** -0.5
    outs, lses = [], []
    for window, dil in DIL_PATTERNS:
        nw = window // dil
        sub_len = s_len // dil
        pad = (-sub_len) % BLOCK
        nb = (sub_len + pad) // BLOCK

        def to_blocks(t):
            t = t.reshape(b, sub_len, dil, h, dh)
            t = jnp.pad(t, ((0, 0), (0, pad), (0, 0), (0, 0), (0, 0)))
            return t.reshape(b, nb, BLOCK, dil, h, dh)

        def with_prev(t):
            prev = jnp.pad(t, ((0, 0), (1, 0), (0, 0), (0, 0), (0, 0), (0, 0)))[:, :-1]
            return jnp.concatenate([prev, t], axis=2)

        qb = to_blocks(q)
        kk = with_prev(to_blocks(k))
        vv = with_prev(to_blocks(v))
        qi = jnp.arange(BLOCK)
        kj = jnp.arange(2 * BLOCK)
        rel = BLOCK + qi[:, None] - kj[None, :]
        band = (rel >= 0) & (rel <= nw)
        blk = jnp.arange(nb)
        valid = band[None] & (((blk[:, None] - 1) * BLOCK + kj[None, :]) >= 0)[:, None, :]
        bias = rel_bias[t5_bucket(jnp.maximum(rel, 0) * dil)]
        bias = jnp.transpose(bias, (2, 0, 1)).astype(F32)
        sc = jnp.einsum('bnqrhd,bnkrhd->bnrhqk', qb, kk, preferred_element_type=F32) * scale + bias
        sc = jnp.where(valid[None, :, None, None], sc, -jnp.inf)
        m = jnp.max(sc, axis=-1, keepdims=True)
        e = jnp.exp(sc - m)
        den = jnp.sum(e, axis=-1, keepdims=True)
        o = jnp.einsum('bnrhqk,bnkrhd->bnqrhd', (e / den).astype(v.dtype), vv, preferred_element_type=F32)
        lse = (m + jnp.log(den))[..., 0]
        o = o.reshape(b, nb * BLOCK, dil, h, dh)[:, :sub_len].reshape(b, s_len, h, dh)
        lse = jnp.transpose(lse, (0, 1, 4, 2, 3)).reshape(b, nb * BLOCK, dil, h)[:, :sub_len].reshape(b, s_len, h)
        outs.append(o)
        lses.append(lse)
    wts = jax.nn.softmax(jnp.stack(lses, axis=-1), axis=-1)
    out = jnp.einsum('bshg,bshgd->bshd', wts, jnp.stack(outs, axis=3))
    return out.astype(q.dtype)

def diff_attention(q, k, v, lam, rel_bias):
    s_len = q.shape[1]
    scale = DIFF_HD ** -0.5
    kpos = jnp.arange(s_len)

    def block(args):
        qb, bi = args
        qpos = bi * BLOCK + jnp.arange(BLOCK)
        dist = qpos[:, None] - kpos[None, :]
        bias = rel_bias[t5_bucket(jnp.maximum(dist, 0))].reshape(BLOCK, s_len, DIFF_HEADS, 2)
        bias = jnp.transpose(bias, (2, 3, 0, 1)).astype(F32)
        s = jnp.einsum('bqhmd,bkhmd->bhmqk', qb, k, preferred_element_type=F32) * scale + bias
        s = jnp.where(dist >= 0, s, -jnp.inf)
        p = jax.nn.softmax(s, axis=-1)
        a = p[:, :, 0] - lam * p[:, :, 1]
        return jnp.einsum('bhqk,bkhd->bqhd', a.astype(v.dtype), v)

    nb = s_len // BLOCK
    o = lax.map(block, (to_query_blocks(q), jnp.arange(nb)))
    return from_query_blocks(o)

def stick_breaking_attention(q, k, v):
    s_len = q.shape[1]
    scale = SB_HD ** -0.5
    kpos = jnp.arange(s_len)

    def block(args):
        qb, bi = args
        qpos = bi * BLOCK + jnp.arange(BLOCK)
        strict = kpos[None, :] < qpos[:, None]
        z = jnp.einsum('bqhd,bkhd->bhqk', qb, k, preferred_element_type=F32) * scale
        log_1m = jnp.where(strict, jax.nn.log_sigmoid(-z), 0.0)
        after = lax.cumsum(log_1m, axis=3, reverse=True) - log_1m
        w = jnp.where(strict, jnp.exp(jax.nn.log_sigmoid(z) + after), 0.0)
        return jnp.einsum('bhqk,bkhd->bqhd', w.astype(v.dtype), v)

    nb = s_len // BLOCK
    o = lax.map(block, (to_query_blocks(q), jnp.arange(nb)))
    return from_query_blocks(o)

def even_mixer(h, rel_bias, w_in, q_norm_g, w_uq, kv_norm_g, w_ukv, w_out):
    b, s_len, _ = h.shape
    pos = jnp.arange(s_len)
    proj = h @ w_in
    cq, ckv, kr, qkv = jnp.split(proj, [MLA_Q_RANK, MLA_Q_RANK + MLA_KV_RANK, MLA_IN], axis=-1)
    q = (rmsnorm(cq, q_norm_g) @ w_uq).reshape(b, s_len, MLA_HEADS, MLA_NOPE + MLA_ROPE)
    q_nope = q[..., :MLA_NOPE]
    q_rope = rope(q[..., MLA_NOPE:], pos)
    kv = (rmsnorm(ckv, kv_norm_g) @ w_ukv).reshape(b, s_len, MLA_HEADS, MLA_NOPE + MLA_V)
    k_nope = kv[..., :MLA_NOPE]
    v_a = kv[..., MLA_NOPE:]
    k_rope = rope(kr[:, :, None, :], pos)[:, :, 0]
    o_a = mla_attention(q_nope, q_rope, k_nope, k_rope, v_a)
    qkv = qkv.reshape(b, s_len, 3, DIL_HEADS, DIL_HD)
    o_b = dilated_attention(qkv[:, :, 0], qkv[:, :, 1], qkv[:, :, 2], rel_bias)
    o = jnp.concatenate([o_a.reshape(b, s_len, -1), o_b.reshape(b, s_len, -1)], axis=-1)
    return o @ w_out

def odd_mixer(h, layer, rel_bias, w_in, lq1, lk1, lq2, lk2, sub_g, w_out):
    b, s_len, _ = h.shape
    proj = h @ w_in
    qc, kc, vc, sb = jnp.split(proj, [DIFF_W, 2 * DIFF_W, 3 * DIFF_W], axis=-1)
    lam_init = 0.8 - 0.6 * math.exp(-0.3 * layer)
    lam = (jnp.exp(jnp.sum(lq1.astype(F32) * lk1.astype(F32)))
           - jnp.exp(jnp.sum(lq2.astype(F32) * lk2.astype(F32))) + lam_init)
    qd = qc.reshape(b, s_len, DIFF_HEADS, 2, DIFF_HD)
    kd = kc.reshape(b, s_len, DIFF_HEADS, 2, DIFF_HD)
    vd = vc.reshape(b, s_len, DIFF_HEADS, 2 * DIFF_HD)
    o_c = diff_attention(qd, kd, vd, lam, rel_bias)
    o_c = rmsnorm(o_c, sub_g) * (1 - lam_init)
    sb = sb.reshape(b, s_len, 3, SB_HEADS, SB_HD)
    o_d = stick_breaking_attention(sb[:, :, 0], sb[:, :, 1], sb[:, :, 2])
    o = jnp.concatenate([o_c.reshape(b, s_len, -1), o_d.reshape(b, s_len, -1)], axis=-1)
    return o @ w_out

def swiglu(t, w_gate, w_up, w_down):
    return (jax.nn.silu(t @ w_gate) * (t @ w_up)) @ w_down

def moe(h, router_w, router_b, w_gate, w_up, w_down):
    b, s_len, d = h.shape
    t = h.reshape(-1, d)
    logits = jnp.dot(t, router_w, preferred_element_type=F32) + router_b.astype(F32)
    top_val, top_idx = lax.top_k(logits, TOP_K)
    top_w = jax.nn.softmax(top_val, axis=-1)
    gates = jnp.sum(jax.nn.one_hot(top_idx, N_EXPERTS, dtype=F32) * top_w[..., None], axis=1)
    out = jnp.zeros_like(t)
    for e in range(N_EXPERTS):
        out = out + gates[:, e:e + 1].astype(t.dtype) * swiglu(t, w_gate[e], w_up[e], w_down[e])
    return out.reshape(b, s_len, d)

def setup_inputs(seed: int = 0) -> dict:
    key = jax.random.key(seed)
    keys = jax.random.split(key, 40)
    counter = [0]

    def nxt():
        k = keys[counter[0]]
        counter[0] += 1
        return k

    def nrm(shape, scale):
        return jax.random.normal(nxt(), shape, F32) * scale

    def gain(shape):
        return 1.0 + 0.05 * jax.random.normal(nxt(), shape, F32)

    d = D_MODEL
    inp = {}
    inp['x'] = nrm((BATCH, SEQ, d), 1.0)
    inp['c'] = nrm((BATCH, d), 1.0)
    inp['rel_bias'] = nrm((REL_BUCKETS, REL_MAPS), 0.2)
    inp['ada_mix_w'] = nrm((DEPTH, d, 3 * d), d ** -0.5)
    inp['ada_mix_b'] = nrm((DEPTH, 3 * d), 0.01)
    inp['mix_pre_g'] = gain((DEPTH, d))
    inp['mix_post_g'] = gain((DEPTH, d))
    inp['ada_ffn_w'] = nrm((DEPTH, d, 3 * d), d ** -0.5)
    inp['ada_ffn_b'] = nrm((DEPTH, 3 * d), 0.01)
    inp['ffn_pre_g'] = gain((DEPTH, d))
    inp['ffn_post_g'] = gain((DEPTH, d))
    inp['e_w_in'] = nrm((N_EVEN, d, EVEN_IN), d ** -0.5)
    inp['e_q_norm_g'] = gain((N_EVEN, MLA_Q_RANK))
    inp['e_w_uq'] = nrm((N_EVEN, MLA_Q_RANK, MLA_HEADS * (MLA_NOPE + MLA_ROPE)), MLA_Q_RANK ** -0.5)
    inp['e_kv_norm_g'] = gain((N_EVEN, MLA_KV_RANK))
    inp['e_w_ukv'] = nrm((N_EVEN, MLA_KV_RANK, MLA_HEADS * (MLA_NOPE + MLA_V)), MLA_KV_RANK ** -0.5)
    inp['e_w_out'] = nrm((N_EVEN, EVEN_MIX, d), EVEN_MIX ** -0.5)
    inp['ffn_w_gate'] = nrm((N_EVEN, d, D_FF), d ** -0.5)
    inp['ffn_w_up'] = nrm((N_EVEN, d, D_FF), d ** -0.5)
    inp['ffn_w_down'] = nrm((N_EVEN, D_FF, d), D_FF ** -0.5)
    inp['o_w_in'] = nrm((N_ODD, d, ODD_IN), d ** -0.5)
    inp['diff_lq1'] = nrm((N_ODD, DIFF_HD), 0.1)
    inp['diff_lk1'] = nrm((N_ODD, DIFF_HD), 0.1)
    inp['diff_lq2'] = nrm((N_ODD, DIFF_HD), 0.1)
    inp['diff_lk2'] = nrm((N_ODD, DIFF_HD), 0.1)
    inp['diff_sub_g'] = gain((N_ODD, 2 * DIFF_HD))
    inp['o_w_out'] = nrm((N_ODD, ODD_MIX, d), ODD_MIX ** -0.5)
    inp['router_w'] = nrm((N_ODD, d, N_EXPERTS), d ** -0.5)
    inp['router_b'] = nrm((N_ODD, N_EXPERTS), 0.01)
    inp['moe_w_gate'] = nrm((N_ODD, N_EXPERTS, d, D_FF_EXPERT), d ** -0.5)
    inp['moe_w_up'] = nrm((N_ODD, N_EXPERTS, d, D_FF_EXPERT), d ** -0.5)
    inp['moe_w_down'] = nrm((N_ODD, N_EXPERTS, D_FF_EXPERT, d), D_FF_EXPERT ** -0.5)
    return inp

def reference(x, c, rel_bias, ada_mix_w, ada_mix_b, mix_pre_g, mix_post_g, ada_ffn_w, ada_ffn_b,
              ffn_pre_g, ffn_post_g, e_w_in, e_q_norm_g, e_w_uq, e_kv_norm_g, e_w_ukv, e_w_out,
              ffn_w_gate, ffn_w_up, ffn_w_down, o_w_in, diff_lq1, diff_lk1, diff_lq2, diff_lk2,
              diff_sub_g, o_w_out, router_w, router_b, moe_w_gate, moe_w_up, moe_w_down):
    for layer in range(DEPTH):
        i = layer // 2
        shift, scale, gate = ada_modulation(c, ada_mix_w[layer], ada_mix_b[layer])
        h = modulate(rmsnorm(x, mix_pre_g[layer]), shift, scale)
        if layer % 2 == 0:
            y = even_mixer(h, rel_bias, e_w_in[i], e_q_norm_g[i], e_w_uq[i], e_kv_norm_g[i],
                           e_w_ukv[i], e_w_out[i])
        else:
            y = odd_mixer(h, layer, rel_bias, o_w_in[i], diff_lq1[i], diff_lk1[i], diff_lq2[i],
                          diff_lk2[i], diff_sub_g[i], o_w_out[i])
        x = x + gate[:, None, :] * rmsnorm(y, mix_post_g[layer])
        shift, scale, gate = ada_modulation(c, ada_ffn_w[layer], ada_ffn_b[layer])
        h = modulate(rmsnorm(x, ffn_pre_g[layer]), shift, scale)
        if layer % 2 == 0:
            y = swiglu(h, ffn_w_gate[i], ffn_w_up[i], ffn_w_down[i])
        else:
            y = moe(h, router_w[i], router_b[i], moe_w_gate[i], moe_w_up[i], moe_w_down[i])
        x = x + gate[:, None, :] * rmsnorm(y, ffn_post_g[layer])
    return x


_drawn_inputs = setup_inputs


def setup_inputs(seed=0):
    import zlib

    import numpy as np

    out = dict(_drawn_inputs(seed))
    spreads = {}
    factors = {'ada_ffn_b': 3.416,
     'e_q_norm_g': 6.786,
     'diff_lq1': 2.847,
     'diff_lk1': 8.0,
     'router_b': 6.657}
    for name, (base, spread) in spreads.items():
        noise = np.random.default_rng([zlib.crc32(name.encode()), seed]).standard_normal(out[name].shape)
        drawn = base * np.exp(spread * noise) if base else spread * noise
        out[name] = __import__('jax').numpy.asarray(drawn.astype(out[name].dtype))
    for name, factor in factors.items():
        out[name] = (out[name] * factor).astype(out[name].dtype)
    return out
```

```python
import math
from contextlib import ExitStack

import numpy as np

import concourse.bass as bass
from concourse import mybir

F32 = mybir.dt.float32
F32R = mybir.dt.float32r
I32 = mybir.dt.int32
U32 = mybir.dt.uint32
ACT = mybir.ActivationFunctionType
ALU = mybir.AluOpType
AX = mybir.AxisListType

P = 128
D = 1024
S = 256
KT = D // P
EPS = 1e-6
HD = 64
MLA_H, DIL_H, DIFF_H, SB_H = 8, 8, 4, 8
NOPE, ROPE = 64, 32
QK = NOPE + ROPE
Q_RANK, KV_RANK = 256, 128
MLA_IN = Q_RANK + KV_RANK + ROPE
D_FF, D_FFE, NE = 2816, 3584, 8
FB = 256
RING = 6
UNIT = 2048
UCOL = UNIT // KT
LAM_INIT = 0.8 - 0.6 * math.exp(-0.3 * 1)
NEG = -1e30
TRI = S + P

ADA_UNITS = 12
EVEN_IN0 = ADA_UNITS
EVEN_OUT0 = EVEN_IN0 + 10
DENSE0 = EVEN_OUT0 + 4
DENSE_NB = D_FF // FB
ODD_IN0 = DENSE0 + 3 * DENSE_NB
ODD_OUT0 = ODD_IN0 + 12
MOE0 = ODD_OUT0 + 4
MOE_NB = D_FFE // FB
CREDIT = 8


def shape_constants():
    f32 = np.float32
    k, m = np.arange(P)[:, None], np.arange(P)[None, :]
    c = {"ident": (k == m).astype(f32), "ones": np.ones((P, P), f32)}
    c["neg_suffix"] = -(k >= m).astype(f32)
    c["neg_ones"] = -np.ones((P, P), f32)
    c["before"] = (k < m).astype(f32)
    q, j = np.arange(P)[:, None], np.arange(S)[None, :]
    causal = np.where(j <= q + P, 0.0, NEG)
    c["causal"] = np.concatenate([causal, causal[:, P:]], 1).astype(f32)
    strict0 = np.where(np.arange(P)[:, None] < np.arange(S)[None, :], 0.0, NEG)
    c["strict"] = np.concatenate([strict0, strict0[:, :P]], 1).astype(f32)
    c["strict01"] = (c["strict"] == 0).astype(f32)
    c["iota"] = np.broadcast_to(np.arange(S, dtype=f32), (P, S)).copy()
    half = ROPE // 2
    freqs = (f32(10000.0) ** (-np.arange(half, dtype=f32) / f32(half))).astype(f32)
    ang = (np.arange(S, dtype=f32)[:, None] * freqs[None, :]).astype(f32)
    cos, sin, rot = np.zeros((P, S), f32), np.zeros((P, S), f32), np.zeros((P, ROPE), f32)
    for r in range(ROPE):
        cos[NOPE + r], sin[NOPE + r] = np.cos(ang[:, r % half]), np.sin(ang[:, r % half])
        rot[NOPE + (r + half if r < half else r - half), r] = -1.0 if r < half else 1.0
    c["cos"], c["sin"], c["rot"] = cos, sin, rot
    dist = 255 - np.arange(TRI)
    d = np.maximum(dist, 1).astype(f32)
    log_b = 16 + (np.log(d / f32(16)) / f32(math.log(2048 / 16)) * f32(16)).astype(np.int32)
    bucket = np.where(dist < 16, np.maximum(dist, 0), np.minimum(log_b, 31))
    hot = (np.arange(32)[:, None] == bucket[None, :]) & (dist >= 0)[None, :]
    count = ((dist >= 0) & (dist <= 128)).astype(int) + ((dist >= 0) & (dist % 4 == 0)) + ((dist >= 0) & (dist % 16 == 0))
    dil = np.where(count > 0, np.log(np.maximum(count, 1).astype(np.float64)), NEG)
    dif = np.where(dist >= 0, 0.0, NEG)
    c["bias_hot"] = np.stack([np.vstack([hot, x[None]]) for x in (dil, dif)]).astype(f32)
    return c


_INS = ["x", "rel_bias", "e_w_in", "e_w_uq", "e_w_ukv", "e_w_out",
        "ffn_w_gate", "ffn_w_up", "ffn_w_down", "o_w_in", "diff_lq1", "diff_lk1", "diff_lq2", "diff_lk2",
        "o_w_out", "router_b", "moe_w_gate", "moe_w_up", "moe_w_down"]


def build(nc, A, out):
    ctx = ExitStack()

    def sb(name, shape, dt=F32, scope=None):
        return (scope or ctx).enter_context(nc.sbuf_tensor(name, shape, dt))

    def sem(name):
        return ctx.enter_context(nc.semaphore(name))

    ring = [sb(f"ring{i}", [P, UNIT]) for i in range(RING)]
    k_ident, k_ones = sb("k_ident", [P, P]), sb("k_ones", [P, P])
    k_neg_suffix, k_neg_ones, k_before = sb("k_neg_suffix", [P, P]), sb("k_neg_ones", [P, P]), sb("k_before", [P, P])
    k_causal, k_strict, k_iota = sb("k_causal", [P, TRI]), sb("k_strict", [P, TRI]), sb("k_iota", [P, S])
    k_strict01 = sb("k_strict01", [P, TRI])
    k_cos, k_sin, k_rot = sb("k_cos", [P, S]), sb("k_sin", [P, S]), sb("k_rot", [P, ROPE])
    x_sb = sb("x_sb", [P, 2, D])
    y_sb = sb("y_sb", [P, 2, D])
    xn = sb("xn", [P, 2, D])
    hT = sb("hT", [P, KT, S])
    gate_row = sb("gate_row", [P, D])
    post_row = sb("post_row", [P, D])
    ada_bg = sb("ada_bg", [P, 3 * D])
    ada_w2 = [sb(f"ada_w{i}", [P, D]) for i in range(2)]
    c_col, c_silu = sb("c_col", [P, KT]), sb("c_silu", [P, KT])
    ada_b_col, pre_col = sb("ada_b_col", [P, 4, 16]), sb("pre_col", [P, 4, KT])
    mod_scale, mod_shift = sb("mod_scale", [P, 4, KT]), sb("mod_shift", [P, 4, KT])
    ssq, rs_v, rs_l, rs_t, rs_r = (sb(n, [P, 2]) for n in ("ssq", "rs_v", "rs_l", "rs_t", "rs_r"))
    vec_g = sb("vec_g", [P, 4])
    rw_sb, rb_row = sb("rw_sb", [P, KT, NE]), sb("rb_row", [P, NE])
    lam_in, lam_p = sb("lam_in", [P, 4, HD]), sb("lam_p", [P, 2, HD])
    lam_s, lam_e, lam, sub_scaled = sb("lam_s", [P, 2]), sb("lam_e", [P, 2]), sb("lam", [P, 1]), sb("sub_scaled", [P, 1])

    at = ExitStack()
    ada_fg = sb("ada_fg", [P, 3 * D], scope=at)
    qT, kT = sb("qT", [P, 8, S], scope=at), sb("kT", [P, 8, S], scope=at)
    qT2, kT2 = sb("qT2", [P, 4, S], scope=at), sb("kT2", [P, 4, S], scope=at)
    v1, v2 = sb("v1", [P, 2, 512], scope=at), sb("v2", [P, 2, 512], scope=at)
    oT = sb("oT", [P, 8, S], scope=at)
    latT = sb("latT", [P, 4, S], scope=at)
    lat_sq, lat_v = (y_sb[:, c, :].rearrange("p (i t) -> p i t", i=4) for c in range(2))
    lat_t, lat_r = (xn[:, c, :].rearrange("p (i t) -> p i t", i=4) for c in range(2))
    rope_t = ada_fg[:, 0:8 * S].rearrange("p (h t) -> p h t", h=8)
    bias = sb("bias", [P, 8, TRI], scope=at)
    bias_w = sb("bias_w", [33, 8], scope=at)
    hT_flat = hT[:].rearrange("p k t -> p (k t)")
    bias_hot = hT_flat[0:33, 0:2 * TRI].rearrange("p (m i) -> p m i", m=2)
    bias_v = hT_flat[0:8, 2 * TRI:4 * TRI].rearrange("p (m i) -> p m i", m=2)
    sc = sb("sc", [P, 2, 2, TRI], scope=at)
    pr = sb("pr", [P, 2, 2, TRI], scope=at)
    pt = sb("pt", [P, 2, TRI], scope=at)
    nmax, den, rden = (sb(n, [P, 2, 2, 2], scope=at) for n in ("nmax", "den", "rden"))
    at.close()

    ff = ExitStack()
    w_hi = [sb(f"w_hi{i}", [P, UNIT], F32R, ff) for i in range(3)]
    w_lo = [sb(f"w_lo{i}", [P, UNIT], F32R, ff) for i in range(3)]
    x_hi, x_lo = sb("x_hi", [P, KT, S], F32R, ff), sb("x_lo", [P, KT, S], F32R, ff)
    g_silu, prod = sb("g_silu", [P, 2, FB], scope=ff), sb("prod", [P, 2, FB], scope=ff)
    h_hi, h_lo = sb("h_hi", [P, 2, FB], F32R, ff), sb("h_lo", [P, 2, FB], F32R, ff)
    x_tok = sb("x_tok", [P, KT, P], scope=ff)
    pick, pick_g = sb("pick", [P, 2, S], scope=ff), sb("pick_g", [P, 2, S], scope=ff)
    pick_gT = sb("pick_gT", [P, 2, S], scope=ff)
    y_tok = hT_flat.rearrange("p (c d) -> p c d", c=2)
    r_log, r_m0, r_m1, r_mask = (sb(n, [P, 2, NE], scope=ff) for n in ("r_log", "r_m0", "r_m1", "r_mask"))
    r_max, r_idxf = sb("r_max", [P, 2, 8], scope=ff), sb("r_idxf", [P, 2, 8], scope=ff)
    r_idx = sb("r_idx", [P, 2, 8], U32, ff)
    r_e, r_w0, r_w1 = sb("r_e", [P, 2], scope=ff), sb("r_w0", [P, 2], scope=ff), sb("r_w1", [P, 2], scope=ff)
    slot_of, gate_of = sb("slot_of", [P, 2, 12], scope=ff), sb("gate_of", [P, 2, 12], scope=ff)
    two_chunks = sb("two_chunks", [1, 12], I32, ff)
    ff.close()

    ps = ctx.enter_context(nc.psum_tensor("ps", [P, 8, 512], F32))
    bias_dram = nc.dram_tensor("bias_dram", (2, 8, P, TRI), F32, kind="Internal").ap()

    landed = [sem(f"landed{i}") for i in range(RING)]
    consts_in, x_in, rows_in = sem("consts_in"), sem("x_in"), sem("rows_in")
    c_ready = sem("c_ready")
    ada_unit_used, even_unit_used, odd_unit_used = sem("ada_unit_used"), sem("even_unit_used"), sem("odd_unit_used")
    ada_fg_ready, ada_bg_step, ada_bg_ready = sem("ada_fg_ready"), sem("ada_bg_step"), sem("ada_bg_ready")
    ada_bg_in = [sem(f"ada_bg_in{i}") for i in range(2)]
    mod_ps, mod_used, mod_ready, gate_used = sem("mod_ps"), sem("mod_used"), sem("mod_ready"), sem("gate_used")
    gate_biased = sem("gate_biased")
    rs_var, rs_ln, rs_exp, ssq_ready, rs_done = sem("rs_var"), sem("rs_ln"), sem("rs_exp"), sem("ssq_ready"), sem("rs_done")
    xn_dve, xn_act, xT_ps, hT_dve, hT_act = sem("xn_dve"), sem("xn_act"), sem("xT_ps"), sem("hT_dve"), sem("hT_act")
    dve_chain, act_chain = sem("dve_chain"), sem("act_chain")
    bias_ps, bias_sb, bias_out, bias_in, bias_free = sem("bias_ps"), sem("bias_sb"), sem("bias_out"), sem("bias_in"), sem("bias_free")
    knope_ps, proj_dve, proj_act = sem("knope_ps"), sem("proj_dve"), sem("proj_act")
    lat_act, lat_ps, lat_ready, rot_ps, rope_ready = sem("lat_act"), sem("lat_ps"), sem("lat_ready"), sem("rot_ps"), sem("rope_ready")
    s_ps, s_free, s_max, p_exp, p_ready, pT_ps, pT_sb, o_ps, o_sb = (
        sem(n) for n in ("s_ps", "s_free", "s_max", "p_exp", "p_ready", "pT_ps", "pT_sb", "o_ps", "o_sb"))
    z_ps, z_ln, z_sp, a_ps, a_sb, w_sb, so_ps, so_sb = (
        sem(n) for n in ("z_ps", "z_ln", "z_sp", "a_ps", "a_sb", "w_sb", "so_ps", "so_sb"))
    dn_sq, dn_ps, dn_done, lam_sum, lam_exp = sem("dn_sq"), sem("dn_ps"), sem("dn_done"), sem("lam_sum"), sem("lam_exp")
    yo_ps, y_dve, y_act, y_sq = sem("yo_ps"), sem("y_dve"), sem("y_act"), sem("y_sq")
    x_new, out_done = sem("x_new"), sem("out_done")
    router_ps, router_sub, router_exp, router_mask, pos_ps, route_ready = (
        sem(n) for n in ("router_ps", "router_sub", "router_exp", "router_mask", "pos_ps", "route_ready"))

    class FfnSems:
        def __init__(self, name):
            self.x_hi, self.x_lo = ([sem(f"{name}_{n}{c}") for c in range(2)] for n in ("x_hi", "x_lo"))
            self.w_hi, self.w_lo, self.half_used = (sem(f"{name}_{n}") for n in ("w_hi", "w_lo", "half_used"))
            self.gu, self.silu, self.prod, self.hT_ps, self.h_hi, self.h_lo, self.down = (
                [sem(f"{name}_{n}{c}") for c in range(2)]
                for n in ("gu", "silu", "prod", "hT_ps", "h_hi", "h_lo", "down"))

    dense_s, moe_s = FfnSems("dense"), FfnSems("moe")
    pick_ready, pick_g_ready, pick_gT_ps, pick_gT_sb = sem("pick_ready"), sem("pick_g_ready"), sem("pick_gT_ps"), sem("pick_gT_sb")
    gath_ps, ytok_dve, ytok_act = ([sem(f"{n}{c}") for c in range(2)] for n in ("gath_ps", "ytok_dve", "ytok_act"))
    x_tok_dve, x_tok_act, x_tok_dve1, x_tok_act1 = (sem(n) for n in ("x_tok_dve", "x_tok_act", "x_tok_dve1", "x_tok_act1"))
    x_tok_mul = [sem(f"x_tok_mul{c}") for c in range(2)]
    scat_ps, y_added = sem("scat_ps"), sem("y_added")

    class Chain:
        def __init__(self, eng, s):
            self.eng, self.s, self.n = eng, s, 0

        def mark(self, ins):
            self.n += 1
            return ins.then_inc(self.s, 1)

        def wait(self):
            self.eng.wait_ge(self.s, self.n)

        def link(self, ins):
            self.mark(ins)
            self.wait()

    class Unit:
        def __init__(self, n):
            self.n, self.slot = n, ring[n % RING]

        def wait(self, eng, more_uses=0):
            eng.wait_ge(landed[self.n % RING], 32 * (self.n // RING + 1) + 32 * more_uses)

    def with_second(eng, flag, work, skipped):
        if flag is None:
            work()
            return
        with eng.If(flag > 0):
            work()
        with eng.Else():
            for s in skipped:
                eng.sem_inc(s, 1)

    rs_count = {"dve": 0, "act": 0}

    def rsqrt_act(v, l, r):
        rs_count["act"] += 1
        nc.scalar.wait_ge(rs_var, rs_count["act"])
        nc.scalar.activation(l, v, ACT.Ln).then_inc(rs_ln, 1)
        nc.scalar.wait_ge(rs_ln, rs_count["act"])
        nc.scalar.activation(r, l, ACT.Exp, scale=-0.5).then_inc(rs_exp, 1)

    def rsqrt_dve(dve, chain, sums, v, t, r):
        rs_count["dve"] += 1
        for squares, n, mean in sums:
            last = nc.vector.tensor_scalar(mean, squares, 1.0 / n, EPS, ALU.mult, ALU.add)
        last.then_inc(rs_var, 1)
        dve.wait_ge(rs_var, rs_count["dve"])
        dve.wait_ge(rs_exp, rs_count["dve"])
        chain.link(nc.vector.tensor_tensor(t, r, r, ALU.mult))
        chain.link(nc.vector.tensor_tensor(t, t, v, ALU.mult))
        chain.link(nc.vector.tensor_scalar(t, t, -0.5, 1.5, ALU.mult, ALU.add))
        nc.vector.tensor_tensor(r, r, t, ALU.mult).then_inc(rs_done, 1)
        dve.wait_ge(rs_done, rs_count["dve"])

    CONST_LOADS = [(c_col[:], A["c_cols"])]
    for name, dst in (("ident", k_ident), ("ones", k_ones), ("neg_suffix", k_neg_suffix), ("neg_ones", k_neg_ones),
                      ("before", k_before), ("causal", k_causal), ("strict", k_strict), ("strict01", k_strict01),
                      ("iota", k_iota), ("cos", k_cos), ("sin", k_sin), ("rot", k_rot), ("ada_b_cols", ada_b_col),
                      ("pre_cols", pre_col), ("vec_cols", vec_g), ("router_cols", rw_sb)):
        CONST_LOADS.append((dst[:], A[name]))
    CONST_LOADS += [
        (bias_hot, A["bias_hot"].rearrange("m b i -> b m i")),
        (bias_w[0:32, :], A["rel_bias"]), (bias_w[32:33, :], A["ones"][0:1, 0:8]),
        (rb_row[:], A["router_b"].partition_broadcast(P)),
    ]
    for i, name in enumerate(("diff_lq1", "diff_lk1", "diff_lq2", "diff_lk2")):
        CONST_LOADS.append((lam_in[:, i, :], A[name].partition_broadcast(P)))
    N_CONSTS = 16 * len(CONST_LOADS)

    block = ctx.enter_context(nc.Block())

    w_in, wo_in = A["e_w_in"][0], A["o_w_in"][0]

    def cols(w, c0, n=UCOL):
        return w.rearrange("(k p) n -> p k n", p=P)[:, :, c0:c0 + n]

    @block.sync
    def _(sp):
        sp.dma_start(x_sb[:], A["x"][0].rearrange("(c p) d -> p c d", p=P)).then_inc(x_in, 16)

        def slot_free(n):
            old = n - RING
            if old < 0:
                return
            for lo, hi, s in ((0, EVEN_IN0, ada_unit_used), (EVEN_IN0, DENSE0, even_unit_used),
                              (ODD_IN0, MOE0, odd_unit_used)):
                if lo <= old < hi:
                    sp.wait_ge(s, old - lo + 1)
                elif hi <= old:
                    pass
            if DENSE0 <= old < ODD_IN0:
                sp.wait_ge(dense_s.w_lo, CREDIT + old - DENSE0 + 1)

        def load(n, src, k):
            slot_free(n)
            w = src.shape[-1]
            dst = ring[n % RING][:, 0:k * w].rearrange("p (k n) -> p k n", k=k)
            for a in (0, k // 2):
                b = a + k // 2
                sp.dma_start(dst[:, a:b, :], src[:, a:b, :]).then_inc(landed[n % RING], 16)

        for u in range(ADA_UNITS):
            g, kp = u // 4, u % 4
            src = A["ada_w"][0].rearrange("(k p) n -> p k n", p=P)[:, 2 * kp:2 * kp + 2, g * D:(g + 1) * D]
            load(u, src, 2)

        mla = cols(w_in, 0, MLA_IN)
        load(EVEN_IN0, mla[:, 0:4, :], 4)
        load(EVEN_IN0 + 1, mla[:, 4:8, :], 4)
        for i in range(6):
            load(EVEN_IN0 + 2 + i, cols(w_in, MLA_IN + i * UCOL), KT)
        load(EVEN_IN0 + 8, A["e_w_uq"][0].rearrange("(k p) n -> p k n", p=P), 2)
        load(EVEN_IN0 + 9, A["e_w_ukv"][0].rearrange("p (k n) -> p k n", k=2), 2)
        for i in range(4):
            load(EVEN_OUT0 + i, cols(A["e_w_out"][0], i * UCOL), KT)

        def ffn_loads(u0, nb, w_gate, w_up, w_down, lo_done, e=None):
            more = 0 if e is None else e * (3 * nb)
            gate = w_gate.rearrange("o (k p) f -> (o p) k f", p=P)
            up = w_up.rearrange("o (k p) f -> (o p) k f", p=P)
            down = w_down.rearrange("o (g k p) d -> (o p) g k d", p=P, k=2)

            def free(idx, it):
                sp.wait_ge(lo_done, more + it * 6 + (CREDIT + idx + 1 - RING))

            def gate_up(idx, b, half, it=0):
                r = ring[(u0 + idx) % RING][:].rearrange("p (k n) -> p k n", k=4)
                s = landed[(u0 + idx) % RING]
                c0 = b * FB
                k0 = 4 * half
                src_g, src_u = gate[:, k0:k0 + 4, bass.ds(c0, FB)], up[:, k0:k0 + 4, bass.ds(c0, FB)]
                free(idx, it)
                sp.dma_start(r[:, :, 0:FB], src_g).then_inc(s, 16)
                sp.dma_start(r[:, :, FB:2 * FB], src_u).then_inc(s, 16)

            def down_rows(idx, b, it=0):
                r = ring[(u0 + idx) % RING][:].rearrange("p (k n) -> p k n", k=2)
                s = landed[(u0 + idx) % RING]
                src = down[:, bass.ds(b, 1), :, :].rearrange("p o k d -> p (o k) d")
                free(idx, it)
                for k in range(2):
                    sp.dma_start(r[:, k:k + 1, :], src[:, k:k + 1, :]).then_inc(s, 16)

            def step(s, idx, it=0):
                gate_up(idx, s + 1, 0, it)
                gate_up(idx + 1, s + 1, 1, it)
                down_rows(idx + 2, s, it)

            gate_up(0, 0, 0)
            gate_up(1, 0, 1)
            step(0, 2)
            turns = (nb - 2) // 2
            with sp.Fori(0, turns) as it:
                step(2 * it + 1, 5, it)
                step(2 * it + 2, 8, it)
            for s in range(1 + 2 * turns, nb - 1):
                step(s, 2 + 3 * s)
            down_rows(3 * nb - 1, nb - 1)

        sp.wait_ge(even_unit_used, DENSE0 - EVEN_IN0)
        ffn_loads(DENSE0, DENSE_NB, A["ffn_w_gate"], A["ffn_w_up"], A["ffn_w_down"], dense_s.w_lo)

        for i in range(12):
            load(ODD_IN0 + i, cols(wo_in, i * UCOL), KT)
        for i in range(4):
            load(ODD_OUT0 + i, cols(A["o_w_out"][0], i * UCOL), KT)

        sp.wait_ge(odd_unit_used, MOE0 - ODD_IN0)
        with sp.Fori(0, NE) as e:
            ex = [A[n][0][bass.ds(e, 1)] for n in ("moe_w_gate", "moe_w_up", "moe_w_down")]
            ffn_loads(MOE0, MOE_NB, *ex, moe_s.w_lo, e)

        sp.wait_ge(x_new, 8)
        sp.dma_start(out[0].rearrange("(c p) d -> p c d", p=P), x_sb[:]).then_inc(out_done, 16)
        sp.wait_ge(out_done, 16)

    @block.gpsimd
    def _(pool):
        pool.wait_ge(c_ready, 1)
        ada_w_k = A["ada_w"].rearrange("m (k p) n -> m p k n", p=P)
        PIECES = 3 * KT
        with pool.Fori(0, 3) as i:
            pool.wait_ge(mod_used, i + 1)
            for n in range(PIECES + 1):
                if n < PIECES:
                    g, k = n // KT, n % KT
                    src = ada_w_k[bass.ds(i + 1, 1), :, k:k + 1, g * D:(g + 1) * D].rearrange("m p k n -> (m p) (k n)")
                    if n >= 2:
                        pool.wait_ge(ada_bg_step, 2 * PIECES * i + 2 * (n - 1))
                    nc.gpsimd.dma_start(ada_w2[n % 2][:], src).then_inc(ada_bg_in[n % 2], 16)
                if n >= 1:
                    m = n - 1
                    g, k = m // KT, m % KT
                    acc = ada_bg[:, g * D:(g + 1) * D]
                    pool.wait_ge(ada_bg_in[m % 2], 8 * PIECES * i + 16 * (m // 2 + 1))
                    w = ada_w2[m % 2][:]
                    ck = c_silu[:, k:k + 1].to_broadcast([P, D])
                    if k == 0:
                        nc.gpsimd.tensor_tensor(acc, w, ck, ALU.mult).then_inc(ada_bg_step, 2)
                    else:
                        nc.gpsimd.tensor_tensor(w, w, ck, ALU.mult).then_inc(ada_bg_step, 1)
                        pool.wait_ge(ada_bg_step, 2 * PIECES * i + 2 * m + 1)
                        nc.gpsimd.tensor_tensor(acc, acc, w, ALU.add).then_inc(ada_bg_step, 1)
                    pool.wait_ge(ada_bg_step, 2 * PIECES * i + 2 * m + 2)
            pool.sem_inc(ada_bg_ready, 1)

    @block.tensor
    def _(pe):
        mm = nc.tensor.matmul
        for f in (dense_s, moe_s):
            for s in (f.half_used, *f.gu, *f.hT_ps, *f.down):
                pe.sem_inc(s, CREDIT)
        for s in (pick_gT_ps, scat_ps, *gath_ps):
            pe.sem_inc(s, CREDIT)

        def modulation(m):
            acc = ada_fg if m == 0 else ada_bg
            if m == 0:
                pe.wait_ge(ada_fg_ready, 1)
            else:
                pe.wait_ge(ada_bg_ready, m)
            for j in range(16):
                last = mm(ps[:, 0, j:j + 1], acc[:, j * P:(j + 1) * P], k_ones[:, 0:1], start=True, stop=True)
            for n in range(2):
                last = mm(ps[:, 1 + n, :], k_ones[:], acc[:, 2 * D + n * 512:2 * D + (n + 1) * 512], start=True, stop=True)
            last.then_inc(mod_used, 1)

        def transposes(m):
            pe.wait_ge(xn_dve, m + 1)
            pe.wait_ge(xn_act, m + 1)
            for j in range(KT):
                for c in range(2):
                    o = (j % 2) * S + c * P
                    last = nc.tensor.transpose(ps[:, 3 + j // 2, o:o + P], xn[:, c, j * P:(j + 1) * P], k_ident[:])
            last.then_inc(xT_ps, 1)

        def wait_hT(m):
            pe.wait_ge(hT_dve, m + 1)
            pe.wait_ge(hT_act, m + 1)

        def unit(n, k):
            u = Unit(n)
            u.wait(pe)
            return u.slot[:].rearrange("p (k n) -> p k n", k=k)

        def features(n, bank):
            w = unit(n, KT)
            for i in range(2):
                for k in range(KT):
                    last = mm(ps[:, bank, i * S:(i + 1) * S], w[:, k, i * P:(i + 1) * P], hT[:, k, :],
                              start=(k == 0), stop=(k == KT - 1))
            return last

        def tokens(n, bank, lhs):
            w = unit(n, KT)
            for c in range(2):
                for k in range(KT):
                    last = mm(ps[:, bank, c * UCOL:(c + 1) * UCOL], lhs[:, k, c * P:(c + 1) * P], w[:, k, :],
                              start=(k == 0), stop=(k == KT - 1))
            return last

        pe.wait_ge(consts_in, N_CONSTS)
        for v in range(2):
            last = mm(ps[0:8, v, 0:TRI], bias_w[:], bias_hot[:, v, :], start=True, stop=True)
        last.then_inc(bias_ps, 1)
        transposes(0)
        pe.wait_ge(bias_sb, 1)
        modulation(0)
        wait_hT(0)

        for h in range(2):
            w = Unit(EVEN_IN0 + h)
            w.wait(pe)
            wv = w.slot[:, 0:4 * MLA_IN].rearrange("p (k n) -> p k n", k=4)
            for k in range(4):
                kt = 4 * h + k
                for i in range(3):
                    mm(ps[:, i, 0:S], wv[:, k, i * P:(i + 1) * P], hT[:, kt, :], start=(kt == 0), stop=(kt == KT - 1))
                last = mm(ps[NOPE:QK, 3, 0:S], wv[:, k, 3 * P:3 * P + ROPE], hT[:, kt, :], start=(kt == 0), stop=(kt == KT - 1))
            last.then_inc(even_unit_used, 1)
        for i in range(4):
            features(EVEN_IN0 + 2 + i, 4 + i).then_inc(even_unit_used, 1)
        pe.wait_ge(lat_act, 1)
        for i in range(2):
            tokens(EVEN_IN0 + 6 + i, i, hT).then_inc(even_unit_used, 1)
        mm(ps[:, 2, 0:S], k_ones[:], lat_sq[:, 0, :], start=True, stop=False)
        mm(ps[:, 2, 0:S], k_ones[:], lat_sq[:, 1, :], start=False, stop=True)
        mm(ps[:, 2, S:2 * S], k_ones[:], lat_sq[:, 2, :], start=True, stop=True).then_inc(lat_ps, 1)
        wq = Unit(EVEN_IN0 + 8)
        wq.wait(pe)
        wqv = wq.slot[:, 0:2 * MLA_H * QK].rearrange("p (k n) -> p k n", k=2)
        pe.wait_ge(lat_ready, 1)
        pe.wait_ge(proj_dve, 2)
        pe.wait_ge(proj_act, 2)
        for h in range(MLA_H):
            for k in range(2):
                last = mm(ps[0:QK, 4 + h // 2, (h % 2) * S:(h % 2 + 1) * S], wqv[:, k, h * QK:(h + 1) * QK], latT[:, k, :],
                          start=(k == 0), stop=(k == 1))
        last.then_inc(even_unit_used, 1)
        wkv = Unit(EVEN_IN0 + 9)
        wkv.wait(pe)
        wkvv = wkv.slot[:, 0:MLA_H * 2 * HD].rearrange("p (h n) -> p h n", h=MLA_H)
        pe.wait_ge(proj_dve, 3)
        pe.wait_ge(proj_act, 3)
        for h in range(MLA_H):
            last = mm(ps[0:NOPE, h // 2, (h % 2) * S:(h % 2 + 1) * S], wkvv[:, h, 0:NOPE], latT[:, 2, :], start=True, stop=True)
        last.then_inc(knope_ps, 1)
        pe.wait_ge(proj_dve, 5)
        pe.wait_ge(proj_act, 5)
        for i in range(4):
            mm(ps[NOPE:QK, 4 + i, :], k_rot[NOPE:QK, :], qT[NOPE:QK, 2 * i:2 * i + 2, :], start=True, stop=True)
        mm(ps[NOPE:QK, 0, 0:S], k_rot[NOPE:QK, :], latT[NOPE:QK, 3, :], start=True, stop=True).then_inc(rot_ps, 1)
        for c in range(2):
            last = mm(ps[:, 1 + c, :], latT[:, 2, c * P:(c + 1) * P], wkvv[:, :, NOPE:2 * HD], start=True, stop=True)
        last.then_inc(even_unit_used, 1)

        def softmax_head(i, maps, n_maps):
            b0 = (i % 2) * n_maps
            if i >= first_head[0] + 2:
                pe.wait_ge(s_free, i - 1)
            for m, (q, k) in enumerate(maps):
                mm(ps[:, b0 + m, 0:S], q[:, P:S], k[:, 0:S], start=True, stop=True)
                last = mm(ps[:, b0 + m, S:TRI], q[:, 0:P], k[:, 0:P], start=True, stop=True)
            last.then_inc(s_ps, 1)

        def transpose_head(i, bank):
            pe.wait_ge(p_ready, i + 1)
            if i >= first_head[0] + 2:
                pe.wait_ge(pT_sb, i - 1)
            p = pr[:, i % 2, 0, :]
            for src, dst in ((0, P), (P, S), (S, 0)):
                last = nc.tensor.transpose(ps[:, bank + i % 2, dst:dst + P], p[:, src:src + P], k_ident[:])
            last.then_inc(pT_ps, 1)

        def values(i, bank, rows, v, signal=True):
            pe.wait_ge(pT_sb, i + 1)
            if i >= first_head[0] + 2:
                pe.wait_ge(o_sb, i - 1)
            o = ps[rows, bank + i % 2, :]
            mm(o[:, 0:S], v[:, 0, :], pt[:, i % 2, 0:S], start=True, stop=False)
            mm(o[:, P:S], v[:, 1, :], pt[:, i % 2, S:TRI], start=False, stop=True).then_inc(o_ps, 1)

        first_head = [0]
        pe.wait_ge(proj_dve, 6)
        pe.wait_ge(proj_act, 6)
        pe.wait_ge(rope_ready, 1)

        def even_maps(i):
            if i < DIL_H:
                r = slice(64 * (i % 2), 64 * (i % 2) + HD)
                return [(qT2[r, i // 2, :], kT2[r, i // 2, :])]
            return [(qT[0:QK, i - DIL_H, :], kT[0:QK, i - DIL_H, :])]

        H0 = DIL_H + MLA_H
        for i in range(H0 + 2):
            if i < H0:
                softmax_head(i, even_maps(i), 1)
            if 1 <= i <= H0:
                transpose_head(i - 1, 2)
            if i >= 2:
                h = i - 2
                v = v2 if h < DIL_H else v1
                values(h, 4, slice(64 * (h % 2), 64 * (h % 2) + HD), v[:, :, (h % 8) * HD:(h % 8 + 1) * HD])

        def out_projection(u0, used):
            for n in range(4):
                tokens(u0 + n, n, oT).then_inc(used, 1)
        pe.wait_ge(o_sb, H0)
        out_projection(EVEN_OUT0, even_unit_used)

        pe.wait_ge(y_dve, 1)
        pe.wait_ge(y_act, 1)
        modulation(1)
        transposes(1)

        def ffn(f, u0, nb, flag=None, e=None, between=None, y_free=None):
            blk0 = 0 if e is None else e * nb
            un0 = 0 if e is None else e * (3 * nb)

            def w_ready(un):
                pe.wait_ge(f.w_hi, un + (CREDIT + 1))
                pe.wait_ge(f.w_lo, un + (CREDIT + 1))

            def gate_up(un, blk):
                def chunk(c):
                    pe.wait_ge(f.prod[c], blk + CREDIT)
                    for k in range(KT):
                        t = k // 4
                        if k % 4 == 0:
                            w_ready(un + t)
                        wh = w_hi[t][:, (k % 4) * 512:(k % 4 + 1) * 512]
                        wl = w_lo[t][:, (k % 4) * 512:(k % 4 + 1) * 512]
                        xh, xl = x_hi[:, k, c * P:(c + 1) * P], x_lo[:, k, c * P:(c + 1) * P]
                        mm(ps[:, c, :], xh, wh, start=(k == 0), stop=False)
                        mm(ps[:, c, :], xl, wh, start=False, stop=False)
                        last = mm(ps[:, c, :], xh, wl, start=False, stop=(k == KT - 1))
                        if c == 0 and k == 3:
                            last.then_inc(f.half_used, 1)
                    return last
                with_second(pe, flag, lambda: chunk(1).then_inc(f.gu[1], 1), [f.gu[1]])
                chunk(0).then_inc(f.gu[0], 1)

            def hidden_T(blk):
                def chunk(c):
                    pe.wait_ge(f.prod[c], blk + (CREDIT + 1))
                    pe.wait_ge(f.h_lo[c], blk + CREDIT)
                    for i in range(2):
                        last = nc.tensor.transpose(ps[:, 2 + c, i * P:(i + 1) * P], prod[:, c, i * P:(i + 1) * P], k_ident[:])
                    last.then_inc(f.hT_ps[c], 1)
                with_second(pe, flag, lambda: chunk(1), [f.hT_ps[1]])
                chunk(0)

            def down(un, blk, first=False, final=False):
                if first and y_free:
                    y_free()
                def chunk(c):
                    pe.wait_ge(f.h_hi[c], blk + (CREDIT + 1))
                    pe.wait_ge(f.h_lo[c], blk + (CREDIT + 1))
                    w_ready(un)
                    for i in range(2):
                        hh, hl = h_hi[:, c, i * P:(i + 1) * P], h_lo[:, c, i * P:(i + 1) * P]
                        for n in range(2):
                            o = ps[:, 4 + 2 * c + n, :]
                            wh = w_hi[2][:, i * D + n * 512:i * D + (n + 1) * 512]
                            wl = w_lo[2][:, i * D + n * 512:i * D + (n + 1) * 512]
                            mm(o, hh, wh, start=(first and i == 0), stop=False, skip_group_check=True)
                            mm(o, hl, wh, start=False, stop=False, skip_group_check=True)
                            last = mm(o, hh, wl, start=False, stop=(final and i == 1), skip_group_check=True)
                    return last
                with_second(pe, flag, lambda: chunk(1).then_inc(f.down[1], 1), [f.down[1]])
                chunk(0).then_inc(f.down[0], 1)

            def step(s, idx, it=0, first=False):
                gate_up(un0 + 6 * it + idx, blk0 + s + 1)
                down(un0 + 6 * it + idx + 2, blk0 + s, first)
                hidden_T(blk0 + s + 1)

            gate_up(un0, blk0)
            if between:
                between()
            hidden_T(blk0)
            step(0, 2, first=True)
            turns = (nb - 2) // 2
            with pe.Fori(0, turns) as it:
                step(2 * it + 1, 5, it)
                step(2 * it + 2, 8, it)
            for s in range(1 + 2 * turns, nb - 1):
                step(s, 2 + 3 * s)
            return lambda: down(un0 + 3 * nb - 1, blk0 + nb - 1, final=True)

        pe.wait_ge(dense_s.x_hi[0], CREDIT + 1)
        pe.wait_ge(dense_s.x_lo[0], CREDIT + 1)
        ffn(dense_s, DENSE0, DENSE_NB)()
        pe.wait_ge(y_dve, 2)
        pe.wait_ge(y_act, 2)
        modulation(2)
        transposes(2)
        wait_hT(2)

        for i in range(12):
            bank = i % 8
            if i >= 8:
                pe.wait_ge(proj_dve, 6 + (i - 8) // 2 + 1)
                pe.wait_ge(proj_act, 6 + (i - 8) // 2 + 1)
            (tokens(ODD_IN0 + i, bank, hT) if i in (4, 5, 10, 11) else features(ODD_IN0 + i, bank)).then_inc(odd_unit_used, 1)
        pe.wait_ge(proj_dve, 12)
        pe.wait_ge(proj_act, 12)

        first_head[0] = H0
        for j in range(DIFF_H + 2):
            i = H0 + j
            if j < DIFF_H:
                softmax_head(i, [(qT[64 * m:64 * m + HD, j, :], kT[64 * m:64 * m + HD, j, :]) for m in range(2)], 2)
            if 1 <= j <= DIFF_H:
                transpose_head(i - 1, 4)
            if j >= 2:
                values(i - 2, 6, slice(0, P), v1[:, :, (j - 2) * P:(j - 1) * P])
        pe.wait_ge(dn_sq, DIFF_H)
        pe.wait_ge(pT_sb, H0 + DIFF_H)
        for i in range(2):
            last = mm(ps[:, 4 + i, :], k_ones[:], lat_sq[:, 2 * i:2 * i + 2, :], start=True, stop=True)
        last.then_inc(dn_ps, 1)

        def sb_qk(h):
            r = slice(64 * (h % 2), 64 * (h % 2) + HD)
            return qT2[r, h // 2, :], kT2[r, h // 2, :]

        for i in range(SB_H + 2):
            if i < SB_H:
                if i >= 2:
                    pe.wait_ge(z_sp, i - 1)
                q, k = sb_qk(i)
                mm(ps[:, i % 2, 0:S], k[:, 0:P], q[:, 0:S], start=True, stop=True)
                mm(ps[:, i % 2, S:TRI], k[:, P:S], q[:, P:S], start=True, stop=True).then_inc(z_ps, 1)
            if 1 <= i <= SB_H:
                h = i - 1
                q, k = sb_qk(h)
                sp_h = sc[:, h % 2, 0, :]
                o = ps[:, 2 + h % 2, :]
                if h >= 2:
                    pe.wait_ge(a_sb, h - 1)
                mm(o[:, 0:S], k[:, 0:P], q[:, 0:S], start=True, stop=False)
                pe.wait_ge(z_sp, h + 1)
                mm(o[:, 0:S], k_neg_suffix[:], sp_h[:, 0:S], start=False, stop=False)
                mm(o[:, P:S], k_neg_ones[:], sp_h[:, S:TRI], start=False, stop=True)
                mm(o[:, S:TRI], k[:, P:S], q[:, P:S], start=True, stop=False)
                mm(o[:, S:TRI], k_neg_suffix[:], sp_h[:, S:TRI], start=False, stop=True).then_inc(a_ps, 1)
            if i >= 2:
                h = i - 2
                pe.wait_ge(w_sb, h + 1)
                if h >= 2:
                    pe.wait_ge(so_sb, h - 1)
                o = ps[64 * (h % 2):64 * (h % 2) + HD, 6 + h % 2, :]
                w, v = pr[:, h % 2, 0, :], v2[:, :, h * HD:(h + 1) * HD]
                mm(o[:, 0:S], v[:, 0, :], w[:, 0:S], start=True, stop=False)
                mm(o[:, P:S], v[:, 1, :], w[:, S:TRI], start=False, stop=True).then_inc(so_ps, 1)

        pe.wait_ge(so_sb, SB_H)
        pe.wait_ge(dn_done, 1)
        out_projection(ODD_OUT0, odd_unit_used)
        pe.wait_ge(y_dve, 3)
        pe.wait_ge(y_act, 3)
        modulation(3)
        transposes(3)
        wait_hT(3)

        for c in range(2):
            for k in range(KT):
                last = mm(ps[:, 0, c * NE:(c + 1) * NE], hT[:, k, c * P:(c + 1) * P], rw_sb[:, k, :], start=(k == 0), stop=(k == KT - 1))
        last.then_inc(router_ps, 1)
        pe.wait_ge(router_mask, 1)
        mm(ps[:, 1, 0:NE], k_before[:], r_mask[:, 0, :], start=True, stop=True)
        mm(ps[:, 1, NE:2 * NE], k_ones[:], r_mask[:, 0, :], start=True, stop=False)
        mm(ps[:, 1, NE:2 * NE], k_before[:], r_mask[:, 1, :], start=False, stop=True)
        mm(ps[:, 1, 2 * NE:3 * NE], k_ones[:], r_mask[:, 0, :], start=True, stop=False)
        mm(ps[:, 1, 2 * NE:3 * NE], k_ones[:], r_mask[:, 1, :], start=False, stop=True).then_inc(pos_ps, 1)

        def gather(s):
            for j in range(KT):
                for c in range(2):
                    last = mm(ps[:, j // 4, (j % 4) * P:(j % 4 + 1) * P], xn[:, c, j * P:(j + 1) * P],
                              pick[:, c, s * P:(s + 1) * P], start=(c == 0), stop=(c == 1))
            last.then_inc(gath_ps[s], 1)

        def gather_second(flag, n):
            def work():
                pe.wait_ge(x_tok_dve, n + 1)
                pe.wait_ge(x_tok_act, n + 1)
                gather(1)
            with_second(pe, flag, work, [gath_ps[1]])

        def pick_gates_T(n):
            pe.wait_ge(pick_g_ready, n + 1)
            for s in range(2):
                for c in range(2):
                    last = nc.tensor.transpose(ps[:, 2, s * S + c * P:s * S + (c + 1) * P], pick_g[:, c, s * P:(s + 1) * P], k_ident[:])
            last.then_inc(pick_gT_ps, 1)

        def scatter(flag, n):
            pe.wait_ge(pick_gT_sb, n + 1)
            for s in (ytok_dve[0], ytok_act[0]):
                pe.wait_ge(s, n + (CREDIT + 1))

            def out(chunks):
                for c in range(2):
                    for half in range(2):
                        for s in chunks:
                            last = mm(ps[:, 4 + 2 * c + half, :], pick_gT[:, s, c * P:(c + 1) * P],
                                      y_tok[:, s, half * 512:(half + 1) * 512], start=(s == chunks[0]), stop=(s == chunks[-1]))
                last.then_inc(scat_ps, 1)

            with pe.If(flag > 0):
                for s in (ytok_dve[1], ytok_act[1]):
                    pe.wait_ge(s, n + (CREDIT + 1))
                out([0, 1])
            with pe.Else():
                out([0])

        def flag_at(i):
            return pe.value_load(two_chunks[0:1, i], min_val=0, max_val=1)

        pe.wait_ge(route_ready, 1)
        pe.wait_ge(pick_ready, 1)
        gather(0)
        gather_second(flag_at(slice(1, 2)), 0)
        with pe.Fori(0, NE) as e:
            last_flag, flag, next_flag = (flag_at(bass.ds(e + i, 1)) for i in range(3))
            pe.wait_ge(moe_s.h_lo[0], e * MOE_NB + CREDIT)
            pick_gates_T(e)
            for s in (moe_s.x_hi[0], moe_s.x_lo[0], moe_s.x_hi[1], moe_s.x_lo[1]):
                pe.wait_ge(s, e + (CREDIT + 1))
            last_down = ffn(moe_s, MOE0, MOE_NB, flag, e, between=lambda: scatter(last_flag, e),
                            y_free=lambda: pe.wait_ge(y_added, e + 2))
            pe.wait_ge(pick_ready, e + 2)
            gather(0)
            last_down()
            gather_second(next_flag, e + 1)
        pe.wait_ge(moe_s.h_lo[0], NE * MOE_NB + CREDIT)
        pick_gates_T(NE)
        scatter(flag_at(slice(NE, NE + 1)), NE)

    @block.scalar
    def _(act):
        chain = Chain(act, act_chain)
        do = nc.scalar.activation
        for f in (dense_s, moe_s):
            for s in (f.w_hi, *f.silu, *f.h_hi, *f.x_hi):
                act.sem_inc(s, CREDIT)
        for s in ytok_act:
            act.sem_inc(s, CREDIT)

        for dst, src in CONST_LOADS:
            act.dma_start(dst, src).then_inc(consts_in, 16)

        def load_rows(m):
            act.dma_start(gate_row[:], A["ada_b"][m:m + 1, 2 * D:3 * D].partition_broadcast(P)).then_inc(rows_in, 16)
            act.dma_start(post_row[:], A["post_g"][m:m + 1, :].partition_broadcast(P)).then_inc(rows_in, 16)

        def sum_squares(src):
            for c in range(2):
                last = do(xn[:, c, :], src[:, c, :], ACT.Square, accum_out=ssq[:, c:c + 1])
            last.then_inc(ssq_ready, 1)
            rsqrt_act(rs_v[:], rs_l[:], rs_r[:])

        def prenorm(m):
            sum_squares(x_sb)
            act.wait_ge(rs_done, rs_count["act"])
            do(xn[:, 1, :], x_sb[:, 1, :], ACT.Copy, scale=rs_r[:, 1:2]).then_inc(xn_act, 1)

        def modulated(m):
            act.wait_ge(xT_ps, m + 1)
            act.wait_ge(mod_ready, m + 1)
            for j in (2, 3, 6, 7):
                last = do(hT[:, j, :], ps[:, 3 + j // 2, (j % 2) * S:(j % 2 + 1) * S], ACT.Identity,
                          scale=mod_scale[:, m, j:j + 1], bias=mod_shift[:, m, j:j + 1])
            last.then_inc(hT_act, 1)

        def bias_tiles(v):
            src = bias_dram[v, 0, 0, :]
            for dst0, src0, n in ((0, P - 1, S), (S, 2 * P - 1, P)):
                skew = bass.AP(src.tensor, src.offset + src0, [[TRI - 1, P], [P * TRI, 8], [1, n]])
                act.dma_start(bias[:, :, dst0:dst0 + n], skew).then_inc(bias_in, 16)

        act.wait_ge(consts_in, N_CONSTS)
        do(c_silu[:], c_col[:], ACT.Silu).then_inc(c_ready, 1)
        load_rows(0)
        act.wait_ge(x_in, 16)
        prenorm(0)
        act.wait_ge(bias_ps, 1)
        do(bias_v, ps[0:8, 0:2, 0:TRI], ACT.Copy).then_inc(bias_sb, 1)
        act.wait_ge(bias_sb, 1)
        for v in range(2):
            copies = bias_v[:, v, :].unsqueeze(1).to_broadcast([8, P, TRI])
            act.dma_start(bias_dram[v], copies).then_inc(bias_out, 16)
        act.wait_ge(bias_out, 32)
        bias_tiles(0)
        modulated(0)

        act.wait_ge(even_unit_used, 2)
        for i in range(3):
            do(latT[:, i, :], ps[:, i, 0:S], ACT.Copy)
            last = do(lat_sq[:, i, :], ps[:, i, 0:S], ACT.Square)
        last.then_inc(lat_act, 1)
        act.wait_ge(even_unit_used, 4)
        do(qT2[:, 2:4, :], ps[:, 5, :], ACT.Copy).then_inc(proj_act, 1)
        act.wait_ge(even_unit_used, 6)
        do(kT2[:, 2:4, :], ps[:, 7, :], ACT.Copy).then_inc(proj_act, 1)
        act.wait_ge(even_unit_used, 8)
        do(v2[:, :, S:2 * S], ps[:, 1, :], ACT.Copy).then_inc(proj_act, 1)
        rsqrt_act(lat_v[:, 0:2, :], lat_t[:, 2:4, :], lat_r[:, 0:2, :])
        act.wait_ge(even_unit_used, 9)
        do(qT[0:QK, 4:8, :], ps[0:QK, 6:8, :], ACT.Copy).then_inc(proj_act, 1)
        act.wait_ge(knope_ps, 1)
        do(kT[0:NOPE, 4:8, :], ps[0:NOPE, 2:4, :], ACT.Copy).then_inc(proj_act, 1)
        act.wait_ge(even_unit_used, 10)
        do(v1[:, 1, :], ps[:, 2, :], ACT.Copy).then_inc(proj_act, 1)

        SEG = ((0, S), (S, TRI))

        def exps(i, maps):
            act.wait_ge(s_max, i + 1)
            for m in range(maps):
                for g, (a, b) in enumerate(SEG):
                    last = do(pr[:, i % 2, m, a:b], sc[:, i % 2, m, a:b], ACT.Exp, bias=nmax[:, i % 2, m, g:g + 1],
                              accum_out=den[:, i % 2, m, g:g + 1])
            last.then_inc(p_exp, 1)

        def pT_copy(i, bank):
            act.wait_ge(pT_ps, i + 1)
            do(pt[:, i % 2, :], ps[:, bank + i % 2, 0:TRI], ACT.Copy).then_inc(pT_sb, 1)

        H0 = DIL_H + MLA_H
        for i in range(H0 + 2):
            if i < H0:
                exps(i, 1)
            if 1 <= i <= H0:
                pT_copy(i - 1, 2)
            if i >= 2:
                h = i - 2
                act.wait_ge(o_ps, h + 1)
                rows = slice(64 * (h % 2), 64 * (h % 2) + HD)
                chunk = 4 + h // 2 if h < DIL_H else (h - DIL_H) // 2
                do(oT[rows, chunk, :], ps[rows, 4 + h % 2, 0:S], ACT.Copy).then_inc(o_sb, 1)

        def out_half(used, n0):
            for n in (1, 3):
                act.wait_ge(used, n0 + n + 1)
                last = do(y_sb[:, :, n * UCOL:(n + 1) * UCOL], ps[:, n, :], ACT.Copy)
            last.then_inc(y_act, 1)

        def residual(m):
            sum_squares(y_sb)
            act.wait_ge(x_new, 2 * (m + 1))

        def next_input(m):
            act.wait_ge(y_dve, m)
            act.wait_ge(y_act, m)
            residual(m - 1)
            load_rows(m)
            prenorm(m)
            modulated(m)

        out_half(even_unit_used, 10)
        next_input(1)

        def ffn(f, u0, nb, flag=None, e=None, between=None):
            blk0 = 0 if e is None else e * nb
            uses = 0 if e is None else e * (3 * nb // RING)

            def hi(t, idx, blk, it=0):
                Unit(u0 + idx).wait(act, uses + it)
                act.wait_ge((f.half_used, f.gu[0], f.down[0])[t], blk + CREDIT)
                do(w_hi[t][:], ring[(u0 + idx) % RING][:], ACT.Copy).then_inc(f.w_hi, 1)

            def silu(blk):
                def chunk(c):
                    act.wait_ge(f.gu[c], blk + (CREDIT + 1))
                    act.wait_ge(f.prod[c], blk + CREDIT)
                    do(g_silu[:, c, :], ps[:, c, 0:FB], ACT.Silu).then_inc(f.silu[c], 1)
                with_second(act, flag, lambda: chunk(1), [f.silu[1]])
                chunk(0)

            def hidden(blk):
                def chunk(c):
                    act.wait_ge(f.hT_ps[c], blk + (CREDIT + 1))
                    act.wait_ge(f.down[c], blk + CREDIT)
                    do(h_hi[:, c, :], ps[:, 2 + c, 0:FB], ACT.Copy).then_inc(f.h_hi[c], 1)
                with_second(act, flag, lambda: chunk(1), [f.h_hi[1]])
                chunk(0)

            def step(s, idx, it=0):
                hi(0, idx, blk0 + s + 1, it)
                silu(blk0 + s)
                hi(1, idx + 1, blk0 + s + 1, it)
                hidden(blk0 + s)
                hi(2, idx + 2, blk0 + s, it)

            hi(0, 0, blk0)
            hi(1, 1, blk0)
            if between:
                between()
            step(0, 2)
            turns = (nb - 2) // 2
            with act.Fori(0, turns) as it:
                step(2 * it + 1, 5, it)
                step(2 * it + 2, 8, it)
            for s in range(1 + 2 * turns, nb - 1):
                step(s, 2 + 3 * s)
            silu(blk0 + nb - 1)
            hidden(blk0 + nb - 1)
            hi(2, 3 * nb - 1, blk0 + nb - 1)

        act.wait_ge(hT_dve, 2)
        act.wait_ge(hT_act, 2)
        do(x_hi[:], hT[:], ACT.Copy).then_inc(dense_s.x_hi[0], 1)
        ffn(dense_s, DENSE0, DENSE_NB)
        act.wait_ge(dense_s.down[0], CREDIT + DENSE_NB)
        act.wait_ge(dense_s.down[1], CREDIT + DENSE_NB)
        do(y_sb[:, 1, :], ps[:, 6:8, :], ACT.Copy).then_inc(y_act, 1)
        bias_tiles(1)
        next_input(2)

        for i in range(1, 12, 2):
            act.wait_ge(odd_unit_used, i + 1)
            bank = ps[:, i % 8, :]
            if i in (5, 11):
                do((v1 if i == 5 else v2)[:, :, S:2 * S], bank, ACT.Copy).then_inc(proj_act, 1)
            else:
                dst = {1: qT, 3: kT, 7: qT2, 9: kT2}[i]
                do(dst[:, 2:4, :], bank, ACT.Copy, scale=HD ** -0.5 if i == 7 else 1.0).then_inc(proj_act, 1)
        act.wait_ge(lam_sum, 1)
        do(lam_e[:], lam_s[:], ACT.Exp).then_inc(lam_exp, 1)

        for j in range(DIFF_H + 2):
            i = H0 + j
            if j < DIFF_H:
                exps(i, 2)
            if 1 <= j <= DIFF_H:
                pT_copy(i - 1, 4)
            if j >= 2:
                h = j - 2
                act.wait_ge(o_ps, H0 + h + 1)
                do(latT[:, h, :], ps[:, 6 + h % 2, 0:S], ACT.Copy).then_inc(o_sb, 1)
                act.wait_ge(o_sb, H0 + h + 1)
                do(lat_sq[:, h, :], latT[:, h, :], ACT.Square).then_inc(dn_sq, 1)
        rsqrt_act(lat_v[:, 0:4, :], lat_t[:, 0:4, :], lat_r[:, 0:4, :])

        for i in range(SB_H + 2):
            if i < SB_H:
                t = sc[:, i % 2, 1, :]
                act.wait_ge(z_ps, i + 1)
                if i >= 2:
                    act.wait_ge(z_sp, i - 1)
                chain.link(do(t, ps[:, i % 2, 0:TRI], ACT.Abs))
                chain.link(do(t, t, ACT.Exp, scale=-1.0))
                do(t, t, ACT.Ln, bias=1.0).then_inc(z_ln, 1)
            if 1 <= i <= SB_H:
                h = i - 1
                act.wait_ge(a_sb, h + 1)
                if h >= 2:
                    act.wait_ge(so_ps, h - 1)
                do(pr[:, h % 2, 0, :], pr[:, h % 2, 1, :], ACT.Exp).then_inc(w_sb, 1)
            if i >= 2:
                h = i - 2
                act.wait_ge(so_ps, h + 1)
                rows = slice(64 * (h % 2), 64 * (h % 2) + HD)
                do(oT[rows, 4 + h // 2, :], ps[rows, 6 + h % 2, 0:S], ACT.Copy).then_inc(so_sb, 1)

        out_half(odd_unit_used, 12)
        next_input(3)

        act.wait_ge(router_sub, 1)
        do(r_e[:], r_e[:], ACT.Exp).then_inc(router_exp, 1)

        def gathered(s, n):
            own, other = ((x_tok_act, x_tok_dve), (x_tok_act1, x_tok_dve1))[s]
            act.wait_ge(gath_ps[s], n + (CREDIT + 1))
            act.wait_ge(moe_s.x_lo[0], n + (CREDIT + s))
            act.wait_ge(moe_s.x_lo[1], n + CREDIT)
            for j in range(4, KT):
                last = do(x_tok[:, j, :], ps[:, 1, (j - 4) * P:(j - 3) * P], ACT.Identity,
                          scale=mod_scale[:, 3, j:j + 1], bias=mod_shift[:, 3, j:j + 1])
            last.then_inc(own, 1)
            act.wait_ge(own, n + 1)
            act.wait_ge(other, n + 1)
            do(x_hi[:, :, s * P:(s + 1) * P], x_tok[:], ACT.Copy).then_inc(moe_s.x_hi[s], 1)

        def gathered_second(flag, n):
            with_second(act, flag, lambda: gathered(1, n), [x_tok_act1, moe_s.x_hi[1]])

        def last_outputs(flag, n):
            act.wait_ge(pick_gT_ps, n + (CREDIT + 1))
            act.wait_ge(scat_ps, n + CREDIT)
            do(pick_gT[:], ps[:, 2, :], ACT.Copy).then_inc(pick_gT_sb, 1)

            def chunk(c):
                act.wait_ge(moe_s.down[c], n * MOE_NB + CREDIT)
                do(y_tok[:, c, 512:D], ps[:, 5 + 2 * c, :], ACT.Copy).then_inc(ytok_act[c], 1)
            with_second(act, flag, lambda: chunk(1), [ytok_act[1]])
            chunk(0)

        def flag_at(i):
            return act.value_load(two_chunks[0:1, i], min_val=0, max_val=1)

        act.wait_ge(route_ready, 1)
        gathered(0, 0)
        gathered_second(flag_at(slice(1, 2)), 0)
        with act.Fori(0, NE) as e:
            last_flag, flag, next_flag = (flag_at(bass.ds(e + i, 1)) for i in range(3))
            ffn(moe_s, MOE0, MOE_NB, flag, e, between=lambda: last_outputs(last_flag, e))
            gathered(0, e + 1)
            gathered_second(next_flag, e + 1)
        last_outputs(flag_at(slice(NE, NE + 1)), NE)
        act.wait_ge(y_added, NE + 2)
        residual(3)

    @block.vector
    def _(dve):
        chain = Chain(dve, dve_chain)
        v = nc.vector
        for f in (dense_s, moe_s):
            for s in (f.w_lo, *f.prod, *f.h_lo, *f.x_lo):
                dve.sem_inc(s, CREDIT)
        for s in ytok_dve:
            dve.sem_inc(s, CREDIT)

        def normalise(m):
            dve.wait_ge(ssq_ready, ssq_count[0] + 1)
            ssq_count[0] += 1
            rsqrt_dve(dve, chain, [(ssq[:], D, rs_v[:])], rs_v[:], rs_t[:], rs_r[:])

        ssq_count = [0]

        def prenorm(m):
            normalise(m)
            v.tensor_scalar(xn[:, 0, :], x_sb[:, 0, :], rs_r[:, 0:1], None, ALU.mult).then_inc(xn_dve, 1)

        def modulation(m):
            dve.wait_ge(mod_used, m + 1)
            v.tensor_tensor(mod_shift[:, m, :], ps[:, 0, 0:KT], ada_b_col[:, m, 0:KT], ALU.add)
            chain.link(v.tensor_tensor(mod_scale[:, m, :], ps[:, 0, KT:2 * KT], ada_b_col[:, m, KT:2 * KT], ALU.add))
            v.scalar_tensor_tensor(out=mod_scale[:, m, :], in0=mod_scale[:, m, :], scalar=1.0, in1=pre_col[:, m, :],
                                   op0=ALU.add, op1=ALU.mult).then_inc(mod_ready, 1)
            dve.wait_ge(rows_in, 32 * (m + 1))
            chain.link(v.tensor_tensor(gate_row[:], ps[:, 1:3, :].rearrange("p b n -> p (b n)"), gate_row[:], ALU.add))
            chain.link(v.tensor_tensor(gate_row[:], gate_row[:], post_row[:], ALU.mult))

        def modulated(m):
            dve.wait_ge(xT_ps, m + 1)
            dve.wait_ge(mod_ready, m + 1)
            for j in (0, 1, 4, 5):
                last = v.tensor_scalar(hT[:, j, :], ps[:, 3 + j // 2, (j % 2) * S:(j % 2 + 1) * S],
                                       mod_scale[:, m, j:j + 1], mod_shift[:, m, j:j + 1], ALU.mult, ALU.add)
            last.then_inc(hT_dve, 1)

        dve.wait_ge(consts_in, N_CONSTS)
        dve.wait_ge(x_in, 16)
        prenorm(0)

        dve.wait_ge(c_ready, 1)
        for u in range(ADA_UNITS):
            g, kp = u // 4, u % 4
            un = Unit(u)
            un.wait(dve)
            acc = ada_fg[:, g * D:(g + 1) * D]
            for i in range(2):
                k = 2 * kp + i
                w = un.slot[:, i * D:(i + 1) * D]
                if k == 0:
                    ins = v.tensor_scalar(acc, w, c_silu[:, k:k + 1], None, ALU.mult)
                else:
                    ins = v.scalar_tensor_tensor(out=acc, in0=w, scalar=c_silu[:, k:k + 1], in1=acc, op0=ALU.mult, op1=ALU.add)
                if u == ADA_UNITS - 1 and i == 1:
                    ins.then_inc(ada_fg_ready, 1)
                elif i == 1:
                    ins.then_inc(ada_unit_used, 1)
                    dve.wait_ge(ada_unit_used, u + 1)
                else:
                    chain.link(ins)
        dve.wait_ge(ada_fg_ready, 1)
        dve.sem_inc(ada_unit_used, 1)
        modulation(0)
        dve.wait_ge(bias_out, 32)
        modulated(0)

        dve.wait_ge(even_unit_used, 2)
        chain.link(v.tensor_copy(latT[NOPE:QK, 3, :], ps[NOPE:QK, 3, 0:S]))
        dve.wait_ge(even_unit_used, 3)
        v.tensor_copy(qT2[:, 0:2, :], ps[:, 4, :]).then_inc(proj_dve, 1)
        dve.wait_ge(even_unit_used, 5)
        v.tensor_copy(kT2[:, 0:2, :], ps[:, 6, :]).then_inc(proj_dve, 1)
        dve.wait_ge(even_unit_used, 7)
        v.tensor_copy(v2[:, :, 0:S], ps[:, 0, :]).then_inc(proj_dve, 1)
        dve.wait_ge(lat_act, 1)
        dve.wait_ge(lat_ps, 1)
        rsqrt_dve(dve, chain, [(ps[:, 2, 0:S], Q_RANK, lat_v[:, 0, :]), (ps[:, 2, S:2 * S], KV_RANK, lat_v[:, 1, :])],
                  lat_v[:, 0:2, :], lat_t[:, 0:2, :], lat_r[:, 0:2, :])
        for i in range(3):
            last = v.scalar_tensor_tensor(out=latT[:, i, :], in0=latT[:, i, :], scalar=vec_g[:, i:i + 1], in1=lat_r[:, i // 2, :],
                                          op0=ALU.mult, op1=ALU.mult)
        last.then_inc(lat_ready, 1)
        dve.wait_ge(even_unit_used, 9)
        v.tensor_copy(qT[0:QK, 0:4, :], ps[0:QK, 4:6, :]).then_inc(proj_dve, 1)
        dve.wait_ge(knope_ps, 1)
        v.tensor_copy(kT[0:NOPE, 0:4, :], ps[0:NOPE, 0:2, :]).then_inc(proj_dve, 1)
        dve.wait_ge(even_unit_used, 10)
        v.tensor_copy(v1[:, 0, :], ps[:, 1, :]).then_inc(proj_dve, 1)
        R = slice(NOPE, QK)
        sin8 = k_sin[R, :].unsqueeze(1).to_broadcast([ROPE, MLA_H, S])
        cos8 = k_cos[R, :].unsqueeze(1).to_broadcast([ROPE, MLA_H, S])
        dve.wait_ge(rot_ps, 1)
        v.tensor_tensor(lat_v[R, 2, :], latT[R, 3, :], k_cos[R, :], ALU.mult)
        v.tensor_tensor(rope_t[R], ps[R, 4:8, :].rearrange("p b (h t) -> p (b h) t", h=2), sin8, ALU.mult)
        chain.link(v.tensor_tensor(lat_v[R, 3, :], ps[R, 0, 0:S], k_sin[R, :], ALU.mult))
        v.tensor_tensor(kT[R], lat_v[R, 2, :].unsqueeze(1).to_broadcast([ROPE, MLA_H, S]),
                        lat_v[R, 3, :].unsqueeze(1).to_broadcast([ROPE, MLA_H, S]), ALU.add)
        chain.link(v.tensor_tensor(qT[R], qT[R], cos8, ALU.mult))
        v.tensor_tensor(qT[R], qT[R], rope_t[R], ALU.add).then_inc(rope_ready, 1)

        SEG = ((0, S), (S, TRI))
        H0 = DIL_H + MLA_H

        def scores(i, b0, biases, scale, first):
            dve.wait_ge(s_ps, i + 1)
            if i >= first + 2:
                dve.wait_ge(p_exp, i - 1)
            for m, b in enumerate(biases):
                last = v.scalar_tensor_tensor(out=sc[:, i % 2, m, :], in0=ps[:, b0 + m, 0:TRI], scalar=scale, in1=b,
                                              op0=ALU.mult, op1=ALU.add)
            last.then_inc(s_free, 1)
            dve.wait_ge(s_free, i + 1)
            for m in range(len(biases)):
                for g, (a, b) in enumerate(SEG):
                    last = v.tensor_reduce(nmax[:, i % 2, m, g:g + 1], sc[:, i % 2, m, a:b], AX.X, ALU.max, negate=True)
            last.then_inc(s_max, 1)

        def normalised(i):
            dve.wait_ge(p_exp, i + 1)
            r = rden[:, i % 2, 0, :]
            chain.link(v.reciprocal(r, den[:, i % 2, 0, :]))
            for g, (a, b) in enumerate(SEG):
                last = v.tensor_scalar(pr[:, i % 2, 0, a:b], pr[:, i % 2, 0, a:b], r[:, g:g + 1], None, ALU.mult)
            last.then_inc(p_ready, 1)

        for i in range(H0 + 1):
            if i < H0:
                if i == 0:
                    dve.wait_ge(bias_in, 32)
                b = bias[:, i, :] if i < DIL_H else k_causal[:]
                scores(i, i % 2, [b], (HD if i < DIL_H else QK) ** -0.5, 0)
            if i >= 1:
                normalised(i - 1)

        def out_half(used, n0):
            for n in (0, 2):
                dve.wait_ge(used, n0 + n + 1)
                last = v.tensor_copy(y_sb[:, :, n * UCOL:(n + 1) * UCOL], ps[:, n, :])
            last.then_inc(y_dve, 1)

        def residual(m):
            normalise(m)
            for c in range(2):
                chain.mark(v.scalar_tensor_tensor(out=y_sb[:, c, :], in0=y_sb[:, c, :], scalar=rs_r[:, c:c + 1], in1=gate_row[:],
                                                  op0=ALU.mult, op1=ALU.mult))
            chain.wait()
            for c in range(2):
                v.tensor_tensor(x_sb[:, c, :], x_sb[:, c, :], y_sb[:, c, :], ALU.add).then_inc(x_new, 1)
            dve.wait_ge(x_new, 2 * (m + 1))

        def next_input(m):
            dve.wait_ge(y_dve, m)
            dve.wait_ge(y_act, m)
            residual(m - 1)
            prenorm(m)
            modulation(m)
            modulated(m)

        out_half(even_unit_used, 10)
        next_input(1)

        def ffn(f, u0, nb, flag=None, e=None, between=None, added=None):
            blk0 = 0 if e is None else e * nb
            un0 = 0 if e is None else e * (3 * nb)

            def lo(t, idx, it=0):
                dve.wait_ge(f.w_hi, un0 + 6 * it + (idx + CREDIT + 1))
                v.tensor_tensor(w_lo[t][:], ring[(u0 + idx) % RING][:], w_hi[t][:].bitcast(F32), ALU.subtract).then_inc(f.w_lo, 1)

            def product(blk):
                def chunk(c):
                    dve.wait_ge(f.silu[c], blk + (CREDIT + 1))
                    dve.wait_ge(f.hT_ps[c], blk + CREDIT)
                    v.tensor_tensor(prod[:, c, :], ps[:, c, FB:2 * FB], g_silu[:, c, :], ALU.mult).then_inc(f.prod[c], 1)
                with_second(dve, flag, lambda: chunk(1), [f.prod[1]])
                chunk(0)

            def hidden(blk):
                def chunk(c):
                    dve.wait_ge(f.h_hi[c], blk + (CREDIT + 1))
                    v.tensor_tensor(h_lo[:, c, :], ps[:, 2 + c, 0:FB], h_hi[:, c, :].bitcast(F32), ALU.subtract).then_inc(f.h_lo[c], 1)
                with_second(dve, flag, lambda: chunk(1), [f.h_lo[1]])
                chunk(0)

            def step(s, idx, it=0, added=None):
                lo(0, idx, it)
                product(blk0 + s)
                lo(1, idx + 1, it)
                if added:
                    added()
                hidden(blk0 + s)
                lo(2, idx + 2, it)

            lo(0, 0)
            lo(1, 1)
            if between:
                between()
            step(0, 2, added=added)
            turns = (nb - 2) // 2
            with dve.Fori(0, turns) as it:
                step(2 * it + 1, 5, it)
                step(2 * it + 2, 8, it)
            for s in range(1 + 2 * turns, nb - 1):
                step(s, 2 + 3 * s)
            product(blk0 + nb - 1)
            hidden(blk0 + nb - 1)
            lo(2, 3 * nb - 1)

        dve.wait_ge(dense_s.x_hi[0], CREDIT + 1)
        v.tensor_tensor(x_lo[:], hT[:], x_hi[:].bitcast(F32), ALU.subtract).then_inc(dense_s.x_lo[0], 1)
        ffn(dense_s, DENSE0, DENSE_NB)
        dve.wait_ge(dense_s.down[0], CREDIT + DENSE_NB)
        v.tensor_copy(y_sb[:, 0, :], ps[:, 4:6, :].rearrange("p b n -> p (b n)")).then_inc(y_dve, 1)
        next_input(2)

        for i in range(0, 12, 2):
            dve.wait_ge(odd_unit_used, i + 1)
            bank = ps[:, i % 8, :]
            if i in (4, 10):
                v.tensor_copy((v1 if i == 4 else v2)[:, :, 0:S], bank).then_inc(proj_dve, 1)
            elif i == 6:
                v.tensor_scalar(qT2[:, 0:2, :], bank, HD ** -0.5, None, ALU.mult).then_inc(proj_dve, 1)
            else:
                v.tensor_copy({0: qT, 2: kT, 8: kT2}[i][:, 0:2, :], bank).then_inc(proj_dve, 1)
        chain.link(v.tensor_tensor(lam_p[:], lam_in[:, 0::2, :], lam_in[:, 1::2, :], ALU.mult))
        v.tensor_reduce(lam_s[:], lam_p[:], AX.X, ALU.add).then_inc(lam_sum, 1)
        dve.wait_ge(lam_exp, 1)
        v.tensor_scalar(sub_scaled[:], vec_g[:, 3:4], 1.0 - LAM_INIT, None, ALU.mult)
        chain.link(v.scalar_tensor_tensor(out=lam[:], in0=lam_e[:, 0:1], scalar=LAM_INIT, in1=lam_e[:, 1:2],
                                          op0=ALU.add, op1=ALU.subtract))

        def difference(i):
            dve.wait_ge(p_exp, i + 1)
            chain.link(v.reciprocal(rden[:, i % 2, :, :], den[:, i % 2, :, :]))
            chain.link(v.tensor_scalar(rden[:, i % 2, 1, :], rden[:, i % 2, 1, :], lam[:], None, ALU.mult))
            for g, (a, b) in enumerate(SEG):
                chain.mark(v.tensor_scalar(pr[:, i % 2, 1, a:b], pr[:, i % 2, 1, a:b], rden[:, i % 2, 1, g:g + 1], None, ALU.mult))
            chain.wait()
            for g, (a, b) in enumerate(SEG):
                last = v.scalar_tensor_tensor(out=pr[:, i % 2, 0, a:b], in0=pr[:, i % 2, 0, a:b], scalar=rden[:, i % 2, 0, g:g + 1],
                                              in1=pr[:, i % 2, 1, a:b], op0=ALU.mult, op1=ALU.subtract)
            last.then_inc(p_ready, 1)

        dve.wait_ge(bias_in, 64)
        for j in range(DIFF_H + 1):
            i = H0 + j
            if j < DIFF_H:
                scores(i, 2 * (i % 2), [bias[:, 2 * j, :], bias[:, 2 * j + 1, :]], HD ** -0.5, H0)
            if j >= 1:
                difference(i - 1)
        dve.wait_ge(dn_ps, 1)
        rsqrt_dve(dve, chain, [(ps[:, 4:6, :].rearrange("p b (h t) -> p (b h) t", h=2), 2 * HD, lat_v[:, 0:4, :])],
                  lat_v[:, 0:4, :], lat_t[:, 0:4, :], lat_r[:, 0:4, :])
        v.scalar_tensor_tensor(out=oT[:, 0:4, :], in0=latT[:, 0:4, :], scalar=sub_scaled[:], in1=lat_r[:, 0:4, :],
                               op0=ALU.mult, op1=ALU.mult).then_inc(dn_done, 1)

        for i in range(SB_H + 1):
            if i < SB_H:
                dve.wait_ge(z_ln, i + 1)
                if i >= 2:
                    dve.wait_ge(a_ps, i - 1)
                chain.link(v.scalar_tensor_tensor(out=sc[:, i % 2, 0, :], in0=ps[:, i % 2, 0:TRI], scalar=0.0, in1=sc[:, i % 2, 1, :],
                                                  op0=ALU.max, op1=ALU.add))
                v.tensor_tensor(sc[:, i % 2, 0, :], sc[:, i % 2, 0, :], k_strict01[:], ALU.mult).then_inc(z_sp, 1)
            if i >= 1:
                h = i - 1
                dve.wait_ge(a_ps, h + 1)
                if h >= 2:
                    dve.wait_ge(w_sb, h - 1)
                v.tensor_tensor(pr[:, h % 2, 1, :], ps[:, 2 + h % 2, 0:TRI], k_strict[:], ALU.add).then_inc(a_sb, 1)

        out_half(odd_unit_used, 12)
        next_input(3)

        dve.wait_ge(router_ps, 1)
        v.memset(slot_of[:], 0.0)
        v.memset(gate_of[:], 0.0)
        v.memset(two_chunks[:], 0)
        v.memset(y_sb[:], 0.0).then_inc(y_added, 1)
        dve.wait_ge(y_added, 1)
        chain.link(v.tensor_tensor(r_log[:], ps[:, 0, 0:2 * NE].rearrange("p (c n) -> p c n", c=2),
                                   rb_row[:].unsqueeze(1).to_broadcast([P, 2, NE]), ALU.add))
        for c in range(2):
            chain.mark(v.max(r_max[:, c, :], r_log[:, c, :]))
        chain.wait()
        for c in range(2):
            chain.mark(v.max_index(r_idx[:, c, :], r_max[:, c, :], r_log[:, c, :]))
        v.tensor_tensor(r_e[:], r_max[:, :, 1], r_max[:, :, 0], ALU.subtract).then_inc(router_sub, 1)
        chain.wait()
        chain.link(v.tensor_copy(r_idxf[:], r_idx[:]))
        for c in range(2):
            for m, mask in enumerate((r_m0, r_m1)):
                chain.mark(v.tensor_scalar(mask[:, c, :], k_iota[:, 0:NE], r_idxf[:, c, m:m + 1], None, ALU.is_equal))
        chain.wait()
        v.tensor_tensor(r_mask[:], r_m0[:], r_m1[:], ALU.add).then_inc(router_mask, 1)
        dve.wait_ge(router_exp, 1)
        chain.link(v.tensor_scalar(r_w0[:], r_e[:], 1.0, None, ALU.add))
        chain.link(v.reciprocal(r_w0[:], r_w0[:]))
        chain.link(v.tensor_tensor(r_w1[:], r_e[:], r_w0[:], ALU.mult))
        for c in range(2):
            chain.mark(v.tensor_scalar(r_m0[:, c, :], r_m0[:, c, :], r_w0[:, c:c + 1], None, ALU.mult))
        chain.wait()
        for c in range(2):
            chain.mark(v.scalar_tensor_tensor(out=gate_of[:, c, 1:1 + NE], in0=r_m1[:, c, :], scalar=r_w1[:, c:c + 1], in1=r_m0[:, c, :],
                                              op0=ALU.mult, op1=ALU.add))
        chain.wait()
        dve.wait_ge(router_mask, 1)
        dve.wait_ge(pos_ps, 1)
        chain.mark(v.scalar_tensor_tensor(out=slot_of[:, :, 1:1 + NE], in0=ps[:, 1, 0:2 * NE].rearrange("p (c n) -> p c n", c=2),
                                          scalar=1.0, in1=r_mask[:], op0=ALU.add, op1=ALU.mult))
        chain.mark(v.tensor_scalar(two_chunks[0:1, 1:1 + NE], ps[0:1, 1, 2 * NE:3 * NE], P + 0.5, None, ALU.is_gt))
        chain.wait()
        v.tensor_scalar(slot_of[:], slot_of[:], -1.0, None, ALU.add).then_inc(route_ready, 1)
        dve.wait_ge(route_ready, 1)

        def picks(col):
            for c in range(2):
                last = v.tensor_scalar(pick[:, c, :], k_iota[:], slot_of[:, c, col], None, ALU.is_equal)
            last.then_inc(pick_ready, 1)

        def last_picks(n, col):
            dve.wait_ge(pick_gT_ps, n + CREDIT)
            for c in range(2):
                last = v.tensor_scalar(pick_g[:, c, :], k_iota[:], slot_of[:, c, col], gate_of[:, c, col], ALU.is_equal, ALU.mult)
            last.then_inc(pick_g_ready, 1)

        def gathered(s, n):
            own, other = ((x_tok_dve, x_tok_act), (x_tok_dve1, x_tok_act1))[s]
            dve.wait_ge(gath_ps[s], n + (CREDIT + 1))
            dve.wait_ge(moe_s.x_lo[0], n + (CREDIT + s))
            dve.wait_ge(moe_s.x_lo[1], n + CREDIT)
            t = x_tok[:, 0:4, :]
            v.tensor_tensor(t, ps[:, 0, :].rearrange("p (j n) -> p j n", j=4), mod_scale[:, 3, 0:4].unsqueeze(2).to_broadcast([P, 4, P]),
                            ALU.mult).then_inc(x_tok_mul[s], 1)
            dve.wait_ge(x_tok_mul[s], n + 1)
            v.tensor_tensor(t, t, mod_shift[:, 3, 0:4].unsqueeze(2).to_broadcast([P, 4, P]), ALU.add).then_inc(own, 1)
            dve.wait_ge(own, n + 1)
            dve.wait_ge(other, n + 1)
            dve.wait_ge(moe_s.x_hi[s], n + (CREDIT + 1))
            v.tensor_tensor(x_lo[:, :, s * P:(s + 1) * P], x_tok[:], x_hi[:, :, s * P:(s + 1) * P].bitcast(F32),
                            ALU.subtract).then_inc(moe_s.x_lo[s], 1)

        def gathered_second(flag, n):
            with_second(dve, flag, lambda: gathered(1, n), [x_tok_mul[1], x_tok_dve1, moe_s.x_lo[1]])

        def last_outputs(flag, n):
            def chunk(c):
                dve.wait_ge(moe_s.down[c], n * MOE_NB + CREDIT)
                dve.wait_ge(scat_ps, n + CREDIT)
                v.tensor_copy(y_tok[:, c, 0:512], ps[:, 4 + 2 * c, :]).then_inc(ytok_dve[c], 1)
            with_second(dve, flag, lambda: chunk(1), [ytok_dve[1]])
            chunk(0)

        def add_scattered(n):
            dve.wait_ge(scat_ps, n + (CREDIT + 1))
            dve.wait_ge(y_added, n + 1)
            for c in range(2):
                last = v.tensor_tensor(y_sb[:, c, :], ps[:, 4 + 2 * c:6 + 2 * c, :].rearrange("p b n -> p (b n)"), y_sb[:, c, :], ALU.add)
            last.then_inc(y_added, 1)

        def flag_at(i):
            return dve.value_load(two_chunks[0:1, i], min_val=0, max_val=1)

        picks(slice(1, 2))
        gathered(0, 0)
        gathered_second(flag_at(slice(1, 2)), 0)
        with dve.Fori(0, NE) as e:
            last_flag, flag, next_flag = (flag_at(bass.ds(e + i, 1)) for i in range(3))
            last_picks(e, bass.ds(e, 1))
            picks(bass.ds(e + 2, 1))
            ffn(moe_s, MOE0, MOE_NB, flag, e, between=lambda: last_outputs(last_flag, e), added=lambda: add_scattered(e))
            gathered(0, e + 1)
            gathered_second(next_flag, e + 1)
        last_picks(NE, slice(NE, NE + 1))
        last_outputs(flag_at(slice(NE, NE + 1)), NE)
        add_scattered(NE)
        dve.wait_ge(y_added, NE + 2)
        residual(3)

    ctx.close()


def kernel(**inputs):
    import concourse.bacc as bacc
    from concourse.bass_utils import run_bass_kernel_spmd

    nc = bacc.Bacc("TRN2", target_bir_lowering=False, num_devices=1)
    arrays = {name: np.ascontiguousarray(inputs[name]) for name in _INS}
    for name, mix, ffn in (("ada_w", "ada_mix_w", "ada_ffn_w"), ("ada_b", "ada_mix_b", "ada_ffn_b"),
                           ("pre_g", "mix_pre_g", "ffn_pre_g"), ("post_g", "mix_post_g", "ffn_post_g")):
        a, b = np.asarray(inputs[mix]), np.asarray(inputs[ffn])
        arrays[name] = np.stack([a[0], b[0], a[1], b[1]])
    def columns(a, lead=0):
        a = np.asarray(a)
        a = a.reshape(a.shape[:lead] + (a.shape[lead] // P, P) + a.shape[lead + 1:])
        return np.ascontiguousarray(np.moveaxis(a, lead + 1, 0))

    arrays["c_cols"] = columns(inputs["c"][0])
    arrays["ada_b_cols"] = columns(arrays["ada_b"][:, 0:2 * D], 1)
    arrays["pre_cols"] = columns(arrays["pre_g"], 1)
    arrays["vec_cols"] = np.concatenate([columns(inputs[n][0]) for n in ("e_q_norm_g", "e_kv_norm_g", "diff_sub_g")], 1)
    arrays["router_cols"] = columns(inputs["router_w"][0])
    del arrays["pre_g"]
    arrays.update(shape_constants())
    aps = {}
    for name, a in arrays.items():
        aps[name] = nc.dram_tensor(f"in_{name}", a.shape, mybir.dt.from_np(a.dtype), kind="ExternalInput").ap()
    out = nc.dram_tensor("out_0", (1, S, D), F32, kind="ExternalOutput").ap()
    build(nc, aps, out)
    r = run_bass_kernel_spmd(nc, [{f"in_{name}": a for name, a in arrays.items()}], core_ids=[0])
    return r.results[0]["out_0"]
```

```python
import math
from contextlib import ExitStack

import numpy as np

import concourse.bass as bass
from concourse import mybir

F32 = mybir.dt.float32
F32R = mybir.dt.float32r
I32 = mybir.dt.int32
U32 = mybir.dt.uint32
ACT = mybir.ActivationFunctionType
ALU = mybir.AluOpType
AX = mybir.AxisListType

P = 128
D = 1024
S = 256
KT = D // P
EPS = 1e-6
HD = 64
MLA_H, DIL_H, DIFF_H, SB_H = 8, 8, 4, 8
NOPE, ROPE = 64, 32
QK = NOPE + ROPE
Q_RANK, KV_RANK = 256, 128
MLA_IN = Q_RANK + KV_RANK + ROPE
D_FF, D_FFE, NE = 2816, 3584, 8
FB = 256
RING = 6
UNIT = 2048
UCOL = UNIT // KT
LAM_INIT = 0.8 - 0.6 * math.exp(-0.3 * 1)
NEG = -1e30
TRI = S + P

ADA_UNITS = 8
EVEN_IN0 = ADA_UNITS
GATE0 = EVEN_IN0 + 6
EVEN_UP0 = GATE0 + 4
EVEN_OUT0 = EVEN_UP0 + 4
DENSE0 = EVEN_OUT0 + 4
DENSE_NB = D_FF // FB
ODD_IN0 = DENSE0 + 3 * DENSE_NB
ODD_OUT0 = ODD_IN0 + 12
MOE0 = ODD_OUT0 + 4
MOE_NB = D_FFE // FB
PIECES = 3 * KT
ACT_PIECES = 15
CREDIT = 8


def shape_constants():
    f32 = np.float32
    k, m = np.arange(P)[:, None], np.arange(P)[None, :]
    c = {"ident": (k == m).astype(f32), "ones": np.ones((P, P), f32)}
    c["neg_suffix"] = -(k >= m).astype(f32)
    c["neg_ones"] = -np.ones((P, P), f32)
    c["before"] = (k < m).astype(f32)
    q, j = np.arange(P)[:, None], np.arange(S)[None, :]
    causal = np.where(j <= q + P, 0.0, NEG)
    c["causal"] = np.concatenate([causal, causal[:, P:]], 1).astype(f32)
    strict0 = np.where(np.arange(P)[:, None] < np.arange(S)[None, :], 0.0, NEG)
    c["strict"] = np.concatenate([strict0, strict0[:, :P]], 1).astype(f32)
    c["strict01"] = (c["strict"] == 0).astype(f32)
    c["iota"] = np.broadcast_to(np.arange(S, dtype=f32), (P, S)).copy()
    half = ROPE // 2
    freqs = (f32(10000.0) ** (-np.arange(half, dtype=f32) / f32(half))).astype(f32)
    ang = (np.arange(S, dtype=f32)[:, None] * freqs[None, :]).astype(f32)
    cos, sin, rot = np.zeros((P, S), f32), np.zeros((P, S), f32), np.zeros((P, ROPE), f32)
    for r in range(ROPE):
        cos[NOPE + r], sin[NOPE + r] = np.cos(ang[:, r % half]), np.sin(ang[:, r % half])
        rot[NOPE + (r + half if r < half else r - half), r] = -1.0 if r < half else 1.0
    c["cos"], c["sin"], c["rot"] = cos, sin, rot
    dist = 255 - np.arange(TRI)
    d = np.maximum(dist, 1).astype(f32)
    log_b = 16 + (np.log(d / f32(16)) / f32(math.log(2048 / 16)) * f32(16)).astype(np.int32)
    bucket = np.where(dist < 16, np.maximum(dist, 0), np.minimum(log_b, 31))
    hot = (np.arange(32)[:, None] == bucket[None, :]) & (dist >= 0)[None, :]
    count = ((dist >= 0) & (dist <= 128)).astype(int) + ((dist >= 0) & (dist % 4 == 0)) + ((dist >= 0) & (dist % 16 == 0))
    dil = np.where(count > 0, np.log(np.maximum(count, 1).astype(np.float64)), NEG)
    dif = np.where(dist >= 0, 0.0, NEG)
    c["bias_hot"] = np.stack([np.vstack([hot, x[None]]) for x in (dil, dif)]).astype(f32)
    return c


_INS = ["x", "rel_bias", "e_w_in", "e_w_uq", "e_w_ukv", "e_w_out",
        "ffn_w_gate", "ffn_w_up", "ffn_w_down", "o_w_in", "diff_lq1", "diff_lk1", "diff_lq2", "diff_lk2",
        "o_w_out", "router_b", "moe_w_gate", "moe_w_up", "moe_w_down"]


def build(nc, A, out):
    ctx = ExitStack()

    def sb(name, shape, dt=F32, scope=None):
        return (scope or ctx).enter_context(nc.sbuf_tensor(name, shape, dt))

    def sem(name):
        return ctx.enter_context(nc.semaphore(name))

    ring = [sb(f"ring{i}", [P, UNIT]) for i in range(RING)]
    k_ident, k_ones = sb("k_ident", [P, P]), sb("k_ones", [P, P])
    k_neg_suffix, k_neg_ones, k_before = sb("k_neg_suffix", [P, P]), sb("k_neg_ones", [P, P]), sb("k_before", [P, P])
    k_causal, k_strict, k_iota = sb("k_causal", [P, TRI]), sb("k_strict", [P, TRI]), sb("k_iota", [P, S])
    k_strict01 = sb("k_strict01", [P, TRI])
    k_cos, k_sin, k_rot = sb("k_cos", [P, S]), sb("k_sin", [P, S]), sb("k_rot", [P, ROPE])
    x_sb = sb("x_sb", [P, 2, D])
    y_sb = sb("y_sb", [P, 2, D])
    xn = sb("xn", [P, 2, D])
    hT = sb("hT", [P, KT, S])
    gate_row = sb("gate_row", [P, D])
    post_row = sb("post_row", [P, D])
    ada_bg = sb("ada_bg", [P, 3 * D])
    ada_w2 = [sb(f"ada_w{i}", [P, D]) for i in range(2)]
    c_col, c_silu = sb("c_col", [P, KT]), sb("c_silu", [P, KT])
    ada_b_col, pre_col = sb("ada_b_col", [P, 4, 16]), sb("pre_col", [P, 4, KT])
    mod_scale, mod_shift = sb("mod_scale", [P, 4, KT]), sb("mod_shift", [P, 4, KT])
    ssq, rs_v, rs_t, rs_r = (sb(n, [P, 2]) for n in ("ssq", "rs_v", "rs_t", "rs_r"))
    y_ssq, table = sb("y_ssq", [P, 2, 4]), sb("table", [P, 1])
    vec_g = sb("vec_g", [P, 4])
    rw_sb, rb_row = sb("rw_sb", [P, KT, NE]), sb("rb_row", [P, NE])
    lam_in, lam_p = sb("lam_in", [P, 4, HD]), sb("lam_p", [P, 2, HD])
    lam_s, lam_e, lam, sub_scaled = sb("lam_s", [P, 2]), sb("lam_e", [P, 2]), sb("lam", [P, 1]), sb("sub_scaled", [P, 1])

    at = ExitStack()
    ada_fg = sb("ada_fg", [P, 3 * D], scope=at)
    qT, kT = sb("qT", [P, 8, S], scope=at), sb("kT", [P, 8, S], scope=at)
    qT2, kT2 = sb("qT2", [P, 4, S], scope=at), sb("kT2", [P, 4, S], scope=at)
    v1, v2 = sb("v1", [P, 2, 512], scope=at), sb("v2", [P, 2, 512], scope=at)
    oT = sb("oT", [P, 8, S], scope=at)
    latT = sb("latT", [P, 4, S], scope=at)
    lat_sq, lat_v = (y_sb[:, c, :].rearrange("p (i t) -> p i t", i=4) for c in range(2))
    lat_t, lat_r = (xn[:, c, :].rearrange("p (i t) -> p i t", i=4) for c in range(2))
    rope_t = ada_fg[:, 0:8 * S].rearrange("p (h t) -> p h t", h=8)
    bias = sb("bias", [P, 8, TRI], scope=at)
    bias_w = sb("bias_w", [33, 8], scope=at)
    hT_flat = hT[:].rearrange("p k t -> p (k t)")
    sc = sb("sc", [P, 2, 2, TRI], scope=at)
    bias_hot, bias_v = sc[0:33, 0, :, :], sc[0:8, 1, :, :]
    pr = sb("pr", [P, 2, 2, TRI], scope=at)
    pt = sb("pt", [P, 2, TRI], scope=at)
    nmax, den, rden = (sb(n, [P, 2, 2, 2], scope=at) for n in ("nmax", "den", "rden"))
    at.close()

    ff = ExitStack()
    w_hi = [sb(f"w_hi{i}", [P, UNIT], F32R, ff) for i in range(3)]
    w_lo = [sb(f"w_lo{i}", [P, UNIT], F32R, ff) for i in range(3)]
    x_hi, x_lo = sb("x_hi", [P, KT, S], F32R, ff), sb("x_lo", [P, KT, S], F32R, ff)
    g_silu, prod = sb("g_silu", [P, 2, FB], scope=ff), sb("prod", [P, 2, FB], scope=ff)
    h_hi, h_lo = sb("h_hi", [P, 2, FB], F32R, ff), sb("h_lo", [P, 2, FB], F32R, ff)
    x_tok = sb("x_tok", [P, KT, P], scope=ff)
    pick, pick_g = sb("pick", [P, 2, S], scope=ff), sb("pick_g", [P, 2, S], scope=ff)
    pick_gT = sb("pick_gT", [P, 2, S], scope=ff)
    y_tok = hT_flat.rearrange("p (c d) -> p c d", c=2)
    r_log, r_m0, r_m1, r_mask = (sb(n, [P, 2, NE], scope=ff) for n in ("r_log", "r_m0", "r_m1", "r_mask"))
    r_max, r_idxf = sb("r_max", [P, 2, 8], scope=ff), sb("r_idxf", [P, 2, 8], scope=ff)
    r_idx = sb("r_idx", [P, 2, 8], U32, ff)
    r_e, r_w0, r_w1 = sb("r_e", [P, 2], scope=ff), sb("r_w0", [P, 2], scope=ff), sb("r_w1", [P, 2], scope=ff)
    slot_of, gate_of = sb("slot_of", [P, 2, 12], scope=ff), sb("gate_of", [P, 2, 12], scope=ff)
    two_chunks = sb("two_chunks", [1, 12], I32, ff)
    ff.close()

    ps = ctx.enter_context(nc.psum_tensor("ps", [P, 8, 512], F32))
    MOD_BANK, GATE_BANK, XT_BANK = (0, 5, 1, 5), (6, 6, 2, 6), (4, 0, 4, 0)
    bias_dram = nc.dram_tensor("bias_dram", (2, 8, P, TRI), F32, kind="Internal").ap()

    landed = [sem(f"landed{i}") for i in range(RING)]
    consts_in, x_in, rows_in = sem("consts_in"), sem("x_in"), sem("rows_in")
    c_ready = sem("c_ready")
    ada_unit_used, even_unit_used, odd_unit_used = sem("ada_unit_used"), sem("even_unit_used"), sem("odd_unit_used")
    ada_fg_ready, ada_bg_step, ada_bg_ready = sem("ada_fg_ready"), sem("ada_bg_step"), sem("ada_bg_ready")
    ada_bg_in = [sem(f"ada_bg_in{i}") for i in range(2)]
    mod_ps, mod_used, mod_ready, gate_ps, gate_sb = (sem(n) for n in ("mod_ps", "mod_used", "mod_ready", "gate_ps", "gate_sb"))
    c_in, early_in, ada_multiplied = sem("c_in"), sem("early_in"), sem("ada_multiplied")
    rs_var, rs_sqrt, ssq_ready, rs_done = sem("rs_var"), sem("rs_sqrt"), sem("ssq_ready"), sem("rs_done")
    xn_dve, xn_act, xT_ps, hT_dve, hT_act = sem("xn_dve"), sem("xn_act"), sem("xT_ps"), sem("hT_dve"), sem("hT_act")
    dve_chain, act_chain = sem("dve_chain"), sem("act_chain")
    bias_ps, bias_sb, bias_out, bias_in = sem("bias_ps"), sem("bias_sb"), sem("bias_out"), sem("bias_in")
    knope_ps, proj_dve, proj_act = sem("knope_ps"), sem("proj_dve"), sem("proj_act")
    lat_act, lat_ps, lat_ready, rot_ps, rope_ready = sem("lat_act"), sem("lat_ps"), sem("lat_ready"), sem("rot_ps"), sem("rope_ready")
    s_ps, s_free, s_max, p_exp, p_ready, pT_ps, pT_sb, o_ps, o_sb = (
        sem(n) for n in ("s_ps", "s_free", "s_max", "p_exp", "p_ready", "pT_ps", "pT_sb", "o_ps", "o_sb"))
    z_ps, z_ln, z_sp, a_ps, a_sb, w_sb, so_ps, so_sb = (
        sem(n) for n in ("z_ps", "z_ln", "z_sp", "a_ps", "a_sb", "w_sb", "so_ps", "so_sb"))
    dn_sq, dn_ps, dn_done, lam_sum, lam_exp = sem("dn_sq"), sem("dn_ps"), sem("dn_done"), sem("lam_sum"), sem("lam_exp")
    y_gated, y_squared, y_half = sem("y_gated"), sem("y_squared"), sem("y_half")
    x_new, out_done = sem("x_new"), sem("out_done")
    router_ps, router_sub, router_exp, router_mask, pos_ps, route_ready = (
        sem(n) for n in ("router_ps", "router_sub", "router_exp", "router_mask", "pos_ps", "route_ready"))

    class FfnSems:
        def __init__(self, name):
            self.x_hi, self.x_lo = ([sem(f"{name}_{n}{c}") for c in range(2)] for n in ("x_hi", "x_lo"))
            self.w_hi, self.w_lo, self.half_used = (sem(f"{name}_{n}") for n in ("w_hi", "w_lo", "half_used"))
            self.gu, self.silu, self.prod, self.hT_ps, self.h_hi, self.h_lo, self.down = (
                [sem(f"{name}_{n}{c}") for c in range(2)]
                for n in ("gu", "silu", "prod", "hT_ps", "h_hi", "h_lo", "down"))

    dense_s, moe_s = FfnSems("dense"), FfnSems("moe")
    pick_ready, pick_g_ready, pick_gT_ps, pick_gT_sb = sem("pick_ready"), sem("pick_g_ready"), sem("pick_gT_ps"), sem("pick_gT_sb")
    gath_ps, ytok_dve, ytok_act = ([sem(f"{n}{c}") for c in range(2)] for n in ("gath_ps", "ytok_dve", "ytok_act"))
    x_tok_dve, x_tok_act, x_tok_dve1, x_tok_act1 = (sem(n) for n in ("x_tok_dve", "x_tok_act", "x_tok_dve1", "x_tok_act1"))
    x_tok_mul = [sem(f"x_tok_mul{c}") for c in range(2)]
    scat_ps, y_added = sem("scat_ps"), sem("y_added")

    class Chain:
        def __init__(self, eng, s):
            self.eng, self.s, self.n = eng, s, 0

        def mark(self, ins):
            self.n += 1
            return ins.then_inc(self.s, 1)

        def wait(self):
            self.eng.wait_ge(self.s, self.n)

        def link(self, ins):
            self.mark(ins)
            self.wait()

    class Unit:
        def __init__(self, n):
            self.n, self.slot = n, ring[n % RING]

        def wait(self, eng, more_uses=0):
            eng.wait_ge(landed[self.n % RING], 32 * (self.n // RING + 1) + 32 * more_uses)

    def with_second(eng, flag, work, skipped):
        if flag is None:
            work()
            return
        with eng.If(flag > 0):
            work()
        with eng.Else():
            for s in skipped:
                eng.sem_inc(s, 1)

    def bias_tiles(eng, v):
        src = bias_dram[v, 0, 0, :]
        for dst0, src0, n in ((0, P - 1, S), (S, 2 * P - 1, P)):
            skew = bass.AP(src.tensor, src.offset + src0, [[TRI - 1, P], [P * TRI, 8], [1, n]])
            eng.dma_start(bias[:, :, dst0:dst0 + n], skew).then_inc(bias_in, 16)

    rs_count = {"dve": 0, "act": 0}

    def rsqrt_act(v, r):
        rs_count["act"] += 1
        nc.scalar.wait_ge(rs_var, rs_count["act"])
        nc.scalar.activation(r, v, ACT.Sqrt).then_inc(rs_sqrt, 1)

    def rsqrt_dve(dve, chain, sums, v, t, r):
        rs_count["dve"] += 1
        for squares, n, mean in sums:
            last = nc.vector.tensor_scalar(mean, squares, 1.0 / n, EPS, ALU.mult, ALU.add)
        last.then_inc(rs_var, 1)
        dve.wait_ge(rs_var, rs_count["dve"])
        dve.wait_ge(rs_sqrt, rs_count["dve"])
        chain.link(nc.vector.reciprocal(r, r))
        chain.link(nc.vector.tensor_tensor(t, r, r, ALU.mult))
        chain.link(nc.vector.tensor_tensor(t, t, v, ALU.mult))
        chain.link(nc.vector.tensor_scalar(t, t, -0.5, 1.5, ALU.mult, ALU.add))
        nc.vector.tensor_tensor(r, r, t, ALU.mult).then_inc(rs_done, 1)
        dve.wait_ge(rs_done, rs_count["dve"])

    EARLY_LOADS = [(k_ident[:], A["ident"]), (k_ones[:], A["ones"]), (ada_b_col[:], A["ada_b_cols"]), (pre_col[:], A["pre_cols"])]
    CONST_LOADS = []
    for name, dst in (("neg_suffix", k_neg_suffix), ("neg_ones", k_neg_ones),
                      ("before", k_before), ("causal", k_causal), ("strict", k_strict), ("strict01", k_strict01),
                      ("iota", k_iota), ("cos", k_cos), ("sin", k_sin), ("rot", k_rot), ("vec_cols", vec_g), ("router_cols", rw_sb)):
        CONST_LOADS.append((dst[:], A[name]))
    EARLY_LOADS += [
        (bias_hot, A["bias_hot"].rearrange("m b i -> b m i")),
        (bias_w[0:32, :], A["rel_bias"]), (bias_w[32:33, :], A["ones"][0:1, 0:8]),
    ]
    CONST_LOADS += [
        (rb_row[:], A["router_b"].partition_broadcast(P)),
    ]
    for i, name in enumerate(("diff_lq1", "diff_lk1", "diff_lq2", "diff_lk2")):
        CONST_LOADS.append((lam_in[:, i, :], A[name].partition_broadcast(P)))
    N_EARLY = 16 * len(EARLY_LOADS)
    N_CONSTS = 16 * len(CONST_LOADS)

    block = ctx.enter_context(nc.Block())

    w_in, wo_in = A["e_w_in"][0], A["o_w_in"][0]

    def cols(w, c0, n=UCOL):
        return w.rearrange("(k p) n -> p k n", p=P)[:, :, c0:c0 + n]

    @block.sync
    def _(sp):
        sp.dma_start(c_col[:], A["c_cols"]).then_inc(c_in, 16)

        def slot_free(n):
            old = n - RING
            if old < 0:
                return
            for lo, hi, s, before in ((0, EVEN_IN0, ada_unit_used, 0), (EVEN_IN0, GATE0, even_unit_used, 0),
                                      (GATE0, EVEN_UP0, ada_unit_used, ADA_UNITS), (EVEN_UP0, DENSE0, even_unit_used, 6),
                                      (ODD_IN0, MOE0, odd_unit_used, 0)):
                if lo <= old < hi:
                    sp.wait_ge(s, before + old - lo + 1)
            if DENSE0 <= old < ODD_IN0:
                sp.wait_ge(dense_s.w_lo, CREDIT + old - DENSE0 + 1)

        def load(n, src, k):
            slot_free(n)
            w = src.shape[-1]
            dst = ring[n % RING][:, 0:k * w].rearrange("p (k n) -> p k n", k=k)
            for a in (0, k // 2):
                b = a + k // 2
                sp.dma_start(dst[:, a:b, :], src[:, a:b, :]).then_inc(landed[n % RING], 16)

        def ada(n, u):
            g, kp = u // 4, u % 4
            src = A["ada_w"][0].rearrange("(k p) n -> p k n", p=P)[:, 2 * kp:2 * kp + 2, g * D:(g + 1) * D]
            load(n, src, 2)

        for u in range(ADA_UNITS):
            ada(u, u)
            if u == 2:
                sp.dma_start(x_sb[:], A["x"][0].rearrange("(c p) d -> p c d", p=P)).then_inc(x_in, 16)

        mla = cols(w_in, 0, MLA_IN)
        load(EVEN_IN0, mla[:, 0:4, :], 4)
        load(EVEN_IN0 + 1, mla[:, 4:8, :], 4)
        for i in range(4):
            load(EVEN_IN0 + 2 + i, cols(w_in, MLA_IN + i * UCOL), KT)
        for i in range(4):
            ada(GATE0 + i, ADA_UNITS + i)
        load(EVEN_UP0, A["e_w_uq"][0].rearrange("(k p) n -> p k n", p=P), 2)
        load(EVEN_UP0 + 1, A["e_w_ukv"][0].rearrange("p (k n) -> p k n", k=2), 2)
        for i in range(2):
            load(EVEN_UP0 + 2 + i, cols(w_in, MLA_IN + (4 + i) * UCOL), KT)
        sp.wait_ge(bias_sb, 1)
        for i in range(2):
            copies = bias_v[:, i, :].unsqueeze(1).to_broadcast([8, P, TRI])
            sp.dma_start(bias_dram[i], copies).then_inc(bias_out, 16)
        sp.wait_ge(bias_out, 32)
        bias_tiles(sp, 0)
        for i in range(4):
            load(EVEN_OUT0 + i, cols(A["e_w_out"][0], i * UCOL), KT)

        def ffn_loads(u0, nb, w_gate, w_up, w_down, lo_done, older, e=None):
            more = 0 if e is None else e * (3 * nb)
            gate = w_gate.rearrange("o (k p) f -> (o p) k f", p=P)
            up = w_up.rearrange("o (k p) f -> (o p) k f", p=P)
            down = w_down.rearrange("o (g k p) d -> (o p) g k d", p=P, k=2)

            def free(idx, it):
                sp.wait_ge(lo_done, more + it * 6 + (CREDIT + idx + 1 - RING))

            def gate_up(idx, b, half, it=0):
                r = ring[(u0 + idx) % RING][:].rearrange("p (k n) -> p k n", k=4)
                s = landed[(u0 + idx) % RING]
                c0 = b * FB
                k0 = 4 * half
                src_g, src_u = gate[:, k0:k0 + 4, bass.ds(c0, FB)], up[:, k0:k0 + 4, bass.ds(c0, FB)]
                free(idx, it)
                sp.dma_start(r[:, :, 0:FB], src_g).then_inc(s, 16)
                sp.dma_start(r[:, :, FB:2 * FB], src_u).then_inc(s, 16)

            def down_rows(idx, b, it=0):
                r = ring[(u0 + idx) % RING][:].rearrange("p (k n) -> p k n", k=2)
                s = landed[(u0 + idx) % RING]
                src = down[:, bass.ds(b, 1), :, :].rearrange("p o k d -> p (o k) d")
                free(idx, it)
                for k in range(2):
                    sp.dma_start(r[:, k:k + 1, :], src[:, k:k + 1, :]).then_inc(s, 16)

            def step(s, idx, it=0):
                gate_up(idx, s + 1, 0, it)
                gate_up(idx + 1, s + 1, 1, it)
                down_rows(idx + 2, s, it)

            older(1)
            gate_up(0, 0, 0)
            older(2)
            gate_up(1, 0, 1)
            older(6)
            step(0, 2)
            turns = (nb - 2) // 2
            with sp.Fori(0, turns) as it:
                step(2 * it + 1, 5, it)
                step(2 * it + 2, 8, it)
            for s in range(1 + 2 * turns, nb - 1):
                step(s, 2 + 3 * s)
            down_rows(3 * nb - 1, nb - 1)

        ffn_loads(DENSE0, DENSE_NB, A["ffn_w_gate"], A["ffn_w_up"], A["ffn_w_down"], dense_s.w_lo,
                  lambda i: sp.wait_ge(even_unit_used, 6 + DENSE0 - EVEN_UP0 - 6 + i))

        for i in range(12):
            load(ODD_IN0 + i, cols(wo_in, i * UCOL), KT)
        for i in range(4):
            load(ODD_OUT0 + i, cols(A["o_w_out"][0], i * UCOL), KT)

        with sp.Fori(0, NE) as e:
            ex = [A[n][0][bass.ds(e, 1)] for n in ("moe_w_gate", "moe_w_up", "moe_w_down")]
            ffn_loads(MOE0, MOE_NB, *ex, moe_s.w_lo, lambda i: sp.wait_ge(odd_unit_used, MOE0 - ODD_IN0 - 6 + i), e)

        for c in range(2):
            sp.wait_ge(x_new, 7 + c)
            sp.dma_start(out[0, c * P:(c + 1) * P, :], x_sb[:, c, :]).then_inc(out_done, 16)
        sp.wait_ge(out_done, 32)

    @block.gpsimd
    def _(pool):
        pool.wait_ge(c_ready, 1)
        ada_w_k = A["ada_w"].rearrange("m (k p) n -> m p k n", p=P)

        def sub_layer(m, i, by_act):
            for n in range(PIECES + 1):
                if n < PIECES:
                    g, k = n // KT, n % KT
                    src = ada_w_k[m, :, k:k + 1, g * D:(g + 1) * D].rearrange("m p k n -> (m p) (k n)")
                    if n >= 2:
                        pool.wait_ge(ada_bg_step, 2 * PIECES * i + 2 * (n - 1))
                    nc.gpsimd.dma_start(ada_w2[n % 2][:], src).then_inc(ada_bg_in[n % 2], 16)
                if n >= 1:
                    p = n - 1
                    g, k = p // KT, p % KT
                    acc = ada_bg[:, g * D:(g + 1) * D]
                    w = ada_w2[p % 2][:]
                    ck = c_silu[:, k:k + 1].to_broadcast([P, D])
                    done = 2 * PIECES * i + 2 * p
                    if p < by_act:
                        pool.wait_ge(ada_multiplied, p + 1)
                        if k == 0:
                            pool.sem_inc(ada_bg_step, 2)
                        else:
                            nc.gpsimd.tensor_tensor(acc, acc, w, ALU.add).then_inc(ada_bg_step, 2)
                    else:
                        pool.wait_ge(ada_bg_in[p % 2], 8 * PIECES * i + 16 * (p // 2 + 1))
                        if k == 0:
                            nc.gpsimd.tensor_tensor(acc, w, ck, ALU.mult).then_inc(ada_bg_step, 2)
                        else:
                            nc.gpsimd.tensor_tensor(w, w, ck, ALU.mult).then_inc(ada_bg_step, 1)
                            pool.wait_ge(ada_bg_step, done + 1)
                            nc.gpsimd.tensor_tensor(acc, acc, w, ALU.add).then_inc(ada_bg_step, 1)
                    pool.wait_ge(ada_bg_step, done + 2)
            pool.sem_inc(ada_bg_ready, 1)

        pool.wait_ge(mod_used, 1)
        sub_layer(slice(1, 2), 0, ACT_PIECES)
        with pool.Fori(0, 2) as i:
            pool.wait_ge(mod_used, i + 2)
            sub_layer(bass.ds(i + 2, 1), i + 1, 0)

    @block.tensor
    def _(pe):
        mm = nc.tensor.matmul
        for f in (dense_s, moe_s):
            for s in (f.half_used, *f.gu, *f.hT_ps, *f.down):
                pe.sem_inc(s, CREDIT)
        for s in (pick_gT_ps, scat_ps, *gath_ps):
            pe.sem_inc(s, CREDIT)

        def shift_scale(m):
            if m > 0:
                pe.wait_ge(ada_bg_ready, m)
            acc = ada_fg if m == 0 else ada_bg
            for j in range(16):
                if m == 0 and j % KT == 0:
                    pe.wait_ge(ada_fg_ready, j // KT + 1)
                last = mm(ps[:, MOD_BANK[m], j:j + 1], acc[:, j * P:(j + 1) * P], k_ones[:, 0:1], start=True, stop=True)
            last.then_inc(mod_ps, 1)
            if m == 0:
                pe.sem_inc(mod_used, 1)

        def gate(m):
            acc = ada_fg if m == 0 else ada_bg
            if m == 0:
                pe.wait_ge(ada_fg_ready, 3)
            for n in range(2):
                last = mm(ps[:, GATE_BANK[m] + n, :], k_ones[:], acc[:, 2 * D + n * 512:2 * D + (n + 1) * 512], start=True, stop=True)
            last.then_inc(gate_ps, 1)
            if m > 0:
                pe.wait_ge(gate_ps, m + 1)
                pe.sem_inc(mod_used, 1)

        def modulation(m):
            shift_scale(m)
            gate(m)

        def transposes(m):
            pe.wait_ge(xn_dve, m + 1)
            pe.wait_ge(xn_act, m + 1)
            for j in range(KT):
                for c in range(2):
                    o = (j % 2) * S + c * P
                    last = nc.tensor.transpose(ps[:, XT_BANK[m] + j // 2, o:o + P], xn[:, c, j * P:(j + 1) * P], k_ident[:])
            last.then_inc(xT_ps, 1)

        def wait_hT(m):
            pe.wait_ge(hT_dve, m + 1)
            pe.wait_ge(hT_act, m + 1)

        def unit(n, k):
            u = Unit(n)
            u.wait(pe)
            return u.slot[:].rearrange("p (k n) -> p k n", k=k)

        def features(n, bank):
            w = unit(n, KT)
            for i in range(2):
                for k in range(KT):
                    last = mm(ps[:, bank, i * S:(i + 1) * S], w[:, k, i * P:(i + 1) * P], hT[:, k, :],
                              start=(k == 0), stop=(k == KT - 1))
            return last

        def tokens(n, bank, lhs):
            w = unit(n, KT)
            for c in range(2):
                for k in range(KT):
                    last = mm(ps[:, bank, c * UCOL:(c + 1) * UCOL], lhs[:, k, c * P:(c + 1) * P], w[:, k, :],
                              start=(k == 0), stop=(k == KT - 1))
            return last

        pe.wait_ge(early_in, N_EARLY)
        for v in range(2):
            last = mm(ps[0:8, 1 + v, 0:TRI], bias_w[:], bias_hot[:, v, :], start=True, stop=True)
        last.then_inc(bias_ps, 1)
        transposes(0)
        shift_scale(0)
        pe.wait_ge(bias_sb, 1)
        wait_hT(0)
        pe.wait_ge(consts_in, N_CONSTS)

        for h in range(2):
            w = Unit(EVEN_IN0 + h)
            w.wait(pe)
            wv = w.slot[:, 0:4 * MLA_IN].rearrange("p (k n) -> p k n", k=4)
            for k in range(4):
                kt = 4 * h + k
                for i in range(3):
                    mm(ps[:, i, 0:S], wv[:, k, i * P:(i + 1) * P], hT[:, kt, :], start=(kt == 0), stop=(kt == KT - 1))
                last = mm(ps[NOPE:QK, 3, 0:S], wv[:, k, 3 * P:3 * P + ROPE], hT[:, kt, :], start=(kt == 0), stop=(kt == KT - 1))
            last.then_inc(even_unit_used, 1)
        for i in range(4):
            if i == 2:
                pe.wait_ge(lat_act, 1)
                mm(ps[:, 2, 0:S], k_ones[:], lat_sq[:, 0, :], start=True, stop=False)
                mm(ps[:, 2, 0:S], k_ones[:], lat_sq[:, 1, :], start=False, stop=True)
                mm(ps[:, 2, S:2 * S], k_ones[:], lat_sq[:, 2, :], start=True, stop=True).then_inc(lat_ps, 1)
            features(EVEN_IN0 + 2 + i, 4 + i).then_inc(even_unit_used, 1)
        wq = Unit(EVEN_UP0)
        wq.wait(pe)
        wqv = wq.slot[:, 0:2 * MLA_H * QK].rearrange("p (k n) -> p k n", k=2)
        pe.wait_ge(lat_ready, 1)
        pe.wait_ge(proj_dve, 2)
        pe.wait_ge(proj_act, 2)
        for h in range(MLA_H):
            for k in range(2):
                last = mm(ps[0:QK, 4 + h // 2, (h % 2) * S:(h % 2 + 1) * S], wqv[:, k, h * QK:(h + 1) * QK], latT[:, k, :],
                          start=(k == 0), stop=(k == 1))
        last.then_inc(even_unit_used, 1)
        wkv = Unit(EVEN_UP0 + 1)
        wkv.wait(pe)
        wkvv = wkv.slot[:, 0:MLA_H * 2 * HD].rearrange("p (h n) -> p h n", h=MLA_H)
        for h in range(MLA_H):
            last = mm(ps[0:NOPE, h // 2, (h % 2) * S:(h % 2 + 1) * S], wkvv[:, h, 0:NOPE], latT[:, 2, :], start=True, stop=True)
        last.then_inc(knope_ps, 1)
        pe.wait_ge(proj_dve, 4)
        pe.wait_ge(proj_act, 4)
        for i in range(4):
            mm(ps[NOPE:QK, 4 + i, :], k_rot[NOPE:QK, :], qT[NOPE:QK, 2 * i:2 * i + 2, :], start=True, stop=True)
        mm(ps[NOPE:QK, 0, 0:S], k_rot[NOPE:QK, :], latT[NOPE:QK, 3, :], start=True, stop=True).then_inc(rot_ps, 1)
        for c in range(2):
            last = mm(ps[:, 1 + c, :], latT[:, 2, c * P:(c + 1) * P], wkvv[:, :, NOPE:2 * HD], start=True, stop=True)
        last.then_inc(even_unit_used, 1)
        tokens(EVEN_UP0 + 2, 3, hT).then_inc(even_unit_used, 1)
        pe.wait_ge(proj_dve, 5)
        tokens(EVEN_UP0 + 3, 1, hT).then_inc(even_unit_used, 1)

        def softmax_head(i, maps, n_maps):
            b0 = (i % 2) * n_maps
            if i >= first_head[0] + 2:
                pe.wait_ge(s_free, i - 1)
            for m, (q, k) in enumerate(maps):
                mm(ps[:, b0 + m, 0:S], q[:, P:S], k[:, 0:S], start=True, stop=True)
                last = mm(ps[:, b0 + m, S:TRI], q[:, 0:P], k[:, 0:P], start=True, stop=True)
            last.then_inc(s_ps, 1)

        def transpose_head(i, bank):
            pe.wait_ge(p_ready, i + 1)
            if i >= first_head[0] + 2:
                pe.wait_ge(pT_sb, i - 1)
            p = pr[:, i % 2, 0, :]
            for src, dst in ((0, P), (P, S), (S, 0)):
                last = nc.tensor.transpose(ps[:, bank + i % 2, dst:dst + P], p[:, src:src + P], k_ident[:])
            last.then_inc(pT_ps, 1)

        def values(i, bank, rows, v, signal=True):
            pe.wait_ge(pT_sb, i + 1)
            if i >= first_head[0] + 2:
                pe.wait_ge(o_sb, i - 1)
            o = ps[rows, bank + i % 2, :]
            mm(o[:, 0:S], v[:, 0, :], pt[:, i % 2, 0:S], start=True, stop=False)
            mm(o[:, P:S], v[:, 1, :], pt[:, i % 2, S:TRI], start=False, stop=True).then_inc(o_ps, 1)

        first_head = [0]
        pe.wait_ge(proj_dve, 6)
        pe.wait_ge(proj_act, 6)
        pe.wait_ge(rope_ready, 1)

        def even_maps(i):
            if i < DIL_H:
                r = slice(64 * (i % 2), 64 * (i % 2) + HD)
                return [(qT2[r, i // 2, :], kT2[r, i // 2, :])]
            return [(qT[0:QK, i - DIL_H, :], kT[0:QK, i - DIL_H, :])]

        H0 = DIL_H + MLA_H
        for i in range(H0 + 3):
            if i < H0:
                softmax_head(i, even_maps(i), 1)
            if 2 <= i < H0 + 2:
                transpose_head(i - 2, 2)
            if i >= 3:
                h = i - 3
                v = v2 if h < DIL_H else v1
                values(h, 4, slice(64 * (h % 2), 64 * (h % 2) + HD), v[:, :, (h % 8) * HD:(h % 8 + 1) * HD])

        def out_projection(u0, used):
            for n in range(4):
                tokens(u0 + n, n, oT).then_inc(used, 1)
        pe.wait_ge(o_sb, H0)
        gate(0)
        shift_scale(1)
        out_projection(EVEN_OUT0, even_unit_used)
        pe.wait_ge(gate_sb, 1)
        gate(1)
        transposes(1)

        def ffn(f, u0, nb, flag=None, e=None, between=None, y_free=None):
            blk0 = 0 if e is None else e * nb
            un0 = 0 if e is None else e * (3 * nb)

            def w_ready(un):
                pe.wait_ge(f.w_hi, un + (CREDIT + 1))
                pe.wait_ge(f.w_lo, un + (CREDIT + 1))

            def gate_up(un, blk):
                def chunk(c):
                    pe.wait_ge(f.prod[c], blk + CREDIT)
                    for k in range(KT):
                        t = k // 4
                        if k % 4 == 0:
                            w_ready(un + t)
                        wh = w_hi[t][:, (k % 4) * 512:(k % 4 + 1) * 512]
                        wl = w_lo[t][:, (k % 4) * 512:(k % 4 + 1) * 512]
                        xh, xl = x_hi[:, k, c * P:(c + 1) * P], x_lo[:, k, c * P:(c + 1) * P]
                        mm(ps[:, c, :], xh, wh, start=(k == 0), stop=False)
                        mm(ps[:, c, :], xl, wh, start=False, stop=False)
                        last = mm(ps[:, c, :], xh, wl, start=False, stop=(k == KT - 1))
                        if c == 0 and k == 3:
                            last.then_inc(f.half_used, 1)
                    return last
                with_second(pe, flag, lambda: chunk(1).then_inc(f.gu[1], 1), [f.gu[1]])
                chunk(0).then_inc(f.gu[0], 1)

            def hidden_T(blk):
                def chunk(c):
                    pe.wait_ge(f.prod[c], blk + (CREDIT + 1))
                    pe.wait_ge(f.h_lo[c], blk + CREDIT)
                    for i in range(2):
                        last = nc.tensor.transpose(ps[:, 2 + c, i * P:(i + 1) * P], prod[:, c, i * P:(i + 1) * P], k_ident[:])
                    last.then_inc(f.hT_ps[c], 1)
                with_second(pe, flag, lambda: chunk(1), [f.hT_ps[1]])
                chunk(0)

            def down(un, blk, first=False, final=False):
                if first and y_free:
                    y_free()
                def chunk(c):
                    pe.wait_ge(f.h_hi[c], blk + (CREDIT + 1))
                    pe.wait_ge(f.h_lo[c], blk + (CREDIT + 1))
                    w_ready(un)
                    for i in range(2):
                        hh, hl = h_hi[:, c, i * P:(i + 1) * P], h_lo[:, c, i * P:(i + 1) * P]
                        for n in range(2):
                            o = ps[:, 4 + 2 * c + n, :]
                            wh = w_hi[2][:, i * D + n * 512:i * D + (n + 1) * 512]
                            wl = w_lo[2][:, i * D + n * 512:i * D + (n + 1) * 512]
                            mm(o, hh, wh, start=(first and i == 0), stop=False, skip_group_check=True)
                            mm(o, hl, wh, start=False, stop=False, skip_group_check=True)
                            last = mm(o, hh, wl, start=False, stop=(final and i == 1), skip_group_check=True)
                    return last
                with_second(pe, flag, lambda: chunk(1).then_inc(f.down[1], 1), [f.down[1]])
                chunk(0).then_inc(f.down[0], 1)

            def step(s, idx, it=0, first=False):
                gate_up(un0 + 6 * it + idx, blk0 + s + 1)
                down(un0 + 6 * it + idx + 2, blk0 + s, first)
                hidden_T(blk0 + s + 1)

            gate_up(un0, blk0)
            if between:
                between()
            hidden_T(blk0)
            step(0, 2, first=True)
            turns = (nb - 2) // 2
            with pe.Fori(0, turns) as it:
                step(2 * it + 1, 5, it)
                step(2 * it + 2, 8, it)
            for s in range(1 + 2 * turns, nb - 1):
                step(s, 2 + 3 * s)
            return lambda: down(un0 + 3 * nb - 1, blk0 + nb - 1, final=True)

        pe.wait_ge(dense_s.x_hi[0], CREDIT + 1)
        pe.wait_ge(dense_s.x_lo[0], CREDIT + 1)
        ffn(dense_s, DENSE0, DENSE_NB, y_free=lambda: pe.wait_ge(gate_sb, 2))()
        modulation(2)
        transposes(2)
        wait_hT(2)

        for i in range(12):
            bank = i % 8
            if i == 2:
                pe.wait_ge(gate_sb, 3)
            if i >= 8:
                pe.wait_ge(proj_dve, 6 + (i - 8) // 2 + 1)
                pe.wait_ge(proj_act, 6 + (i - 8) // 2 + 1)
            (tokens(ODD_IN0 + i, bank, hT) if i in (4, 5, 10, 11) else features(ODD_IN0 + i, bank)).then_inc(odd_unit_used, 1)
        pe.wait_ge(proj_dve, 12)
        pe.wait_ge(proj_act, 12)

        first_head[0] = H0
        for j in range(DIFF_H + 3):
            i = H0 + j
            if j < DIFF_H:
                softmax_head(i, [(qT[64 * m:64 * m + HD, j, :], kT[64 * m:64 * m + HD, j, :]) for m in range(2)], 2)
            if 2 <= j < DIFF_H + 2:
                transpose_head(i - 2, 4)
            if j >= 3:
                values(i - 3, 6, slice(0, P), v1[:, :, (j - 3) * P:(j - 2) * P])
        pe.wait_ge(dn_sq, DIFF_H)
        pe.wait_ge(pT_sb, H0 + DIFF_H)
        for i in range(2):
            last = mm(ps[:, 4 + i, :], k_ones[:], lat_sq[:, 2 * i:2 * i + 2, :], start=True, stop=True)
        last.then_inc(dn_ps, 1)

        def sb_qk(h):
            r = slice(64 * (h % 2), 64 * (h % 2) + HD)
            return qT2[r, h // 2, :], kT2[r, h // 2, :]

        for i in range(SB_H + 2):
            if i < SB_H:
                if i >= 2:
                    pe.wait_ge(z_sp, i - 1)
                q, k = sb_qk(i)
                mm(ps[:, i % 2, 0:S], k[:, 0:P], q[:, 0:S], start=True, stop=True)
                mm(ps[:, i % 2, S:TRI], k[:, P:S], q[:, P:S], start=True, stop=True).then_inc(z_ps, 1)
            if 1 <= i <= SB_H:
                h = i - 1
                q, k = sb_qk(h)
                sp_h = sc[:, h % 2, 0, :]
                o = ps[:, 2 + h % 2, :]
                if h >= 2:
                    pe.wait_ge(a_sb, h - 1)
                mm(o[:, 0:S], k[:, 0:P], q[:, 0:S], start=True, stop=False)
                pe.wait_ge(z_sp, h + 1)
                mm(o[:, 0:S], k_neg_suffix[:], sp_h[:, 0:S], start=False, stop=False)
                mm(o[:, P:S], k_neg_ones[:], sp_h[:, S:TRI], start=False, stop=True)
                mm(o[:, S:TRI], k[:, P:S], q[:, P:S], start=True, stop=False)
                mm(o[:, S:TRI], k_neg_suffix[:], sp_h[:, S:TRI], start=False, stop=True).then_inc(a_ps, 1)
            if i >= 2:
                h = i - 2
                pe.wait_ge(w_sb, h + 1)
                if h >= 2:
                    pe.wait_ge(so_sb, h - 1)
                o = ps[64 * (h % 2):64 * (h % 2) + HD, 6 + h % 2, :]
                w, v = pr[:, h % 2, 0, :], v2[:, :, h * HD:(h + 1) * HD]
                mm(o[:, 0:S], v[:, 0, :], w[:, 0:S], start=True, stop=False)
                mm(o[:, P:S], v[:, 1, :], w[:, S:TRI], start=False, stop=True).then_inc(so_ps, 1)

        pe.wait_ge(so_sb, SB_H)
        pe.wait_ge(dn_done, 1)
        shift_scale(3)
        out_projection(ODD_OUT0, odd_unit_used)
        gate(3)
        transposes(3)
        wait_hT(3)

        for c in range(2):
            for k in range(KT):
                last = mm(ps[:, 0, c * NE:(c + 1) * NE], hT[:, k, c * P:(c + 1) * P], rw_sb[:, k, :], start=(k == 0), stop=(k == KT - 1))
        last.then_inc(router_ps, 1)
        pe.wait_ge(router_mask, 1)
        mm(ps[:, 1, 0:NE], k_before[:], r_mask[:, 0, :], start=True, stop=True)
        mm(ps[:, 1, NE:2 * NE], k_ones[:], r_mask[:, 0, :], start=True, stop=False)
        mm(ps[:, 1, NE:2 * NE], k_before[:], r_mask[:, 1, :], start=False, stop=True)
        mm(ps[:, 1, 2 * NE:3 * NE], k_ones[:], r_mask[:, 0, :], start=True, stop=False)
        mm(ps[:, 1, 2 * NE:3 * NE], k_ones[:], r_mask[:, 1, :], start=False, stop=True).then_inc(pos_ps, 1)

        pe.wait_ge(gate_sb, 4)

        def gather(s):
            for j in range(KT):
                for c in range(2):
                    last = mm(ps[:, j // 4, (j % 4) * P:(j % 4 + 1) * P], xn[:, c, j * P:(j + 1) * P],
                              pick[:, c, s * P:(s + 1) * P], start=(c == 0), stop=(c == 1))
            last.then_inc(gath_ps[s], 1)

        def gather_second(flag, n):
            def work():
                pe.wait_ge(x_tok_dve, n + 1)
                pe.wait_ge(x_tok_act, n + 1)
                gather(1)
            with_second(pe, flag, work, [gath_ps[1]])

        def pick_gates_T(n):
            pe.wait_ge(pick_g_ready, n + 1)
            for s in range(2):
                for c in range(2):
                    last = nc.tensor.transpose(ps[:, 2, s * S + c * P:s * S + (c + 1) * P], pick_g[:, c, s * P:(s + 1) * P], k_ident[:])
            last.then_inc(pick_gT_ps, 1)

        def scatter(flag, n):
            pe.wait_ge(pick_gT_sb, n + 1)
            for s in (ytok_dve[0], ytok_act[0]):
                pe.wait_ge(s, n + (CREDIT + 1))

            def out(chunks):
                for c in range(2):
                    for half in range(2):
                        for s in chunks:
                            last = mm(ps[:, 4 + 2 * c + half, :], pick_gT[:, s, c * P:(c + 1) * P],
                                      y_tok[:, s, half * 512:(half + 1) * 512], start=(s == chunks[0]), stop=(s == chunks[-1]))
                last.then_inc(scat_ps, 1)

            with pe.If(flag > 0):
                for s in (ytok_dve[1], ytok_act[1]):
                    pe.wait_ge(s, n + (CREDIT + 1))
                out([0, 1])
            with pe.Else():
                out([0])

        def flag_at(i):
            return pe.value_load(two_chunks[0:1, i], min_val=0, max_val=1)

        pe.wait_ge(route_ready, 1)
        pe.wait_ge(pick_ready, 1)
        gather(0)
        gather_second(flag_at(slice(1, 2)), 0)
        with pe.Fori(0, NE) as e:
            last_flag, flag, next_flag = (flag_at(bass.ds(e + i, 1)) for i in range(3))
            pe.wait_ge(moe_s.h_lo[0], e * MOE_NB + CREDIT)
            pick_gates_T(e)
            for s in (moe_s.x_hi[0], moe_s.x_lo[0], moe_s.x_hi[1], moe_s.x_lo[1]):
                pe.wait_ge(s, e + (CREDIT + 1))
            last_down = ffn(moe_s, MOE0, MOE_NB, flag, e, between=lambda: scatter(last_flag, e),
                            y_free=lambda: pe.wait_ge(y_added, e + 2))
            pe.wait_ge(pick_ready, e + 2)
            gather(0)
            last_down()
            gather_second(next_flag, e + 1)
        pe.wait_ge(moe_s.h_lo[0], NE * MOE_NB + CREDIT)
        pick_gates_T(NE)
        scatter(flag_at(slice(NE, NE + 1)), NE)

    @block.scalar
    def _(act):
        chain = Chain(act, act_chain)
        do = nc.scalar.activation
        for f in (dense_s, moe_s):
            for s in (f.w_hi, *f.silu, *f.h_hi, *f.x_hi):
                act.sem_inc(s, CREDIT)
        for s in ytok_act:
            act.sem_inc(s, CREDIT)

        for dst, src in EARLY_LOADS:
            act.dma_start(dst, src).then_inc(early_in, 16)

        def load_rows(m):
            act.dma_start(gate_row[:], A["ada_b"][m:m + 1, 2 * D:3 * D].partition_broadcast(P)).then_inc(rows_in, 16)
            act.dma_start(post_row[:], A["post_g"][m:m + 1, :].partition_broadcast(P)).then_inc(rows_in, 16)

        def sqrt_table():
            do(table[:], k_ones[:, 0:1], ACT.Sqrt)

        def prenorm(m):
            for c in range(2):
                if m > 0:
                    act.wait_ge(x_new, 2 * (m - 1) + c + 1)
                last = do(xn[:, c, :], x_sb[:, c, :], ACT.Square, accum_out=ssq[:, c:c + 1])
            last.then_inc(ssq_ready, 1)
            rsqrt_act(rs_v[:], rs_r[:])
            act.wait_ge(rs_done, rs_count["act"])
            do(xn[:, 1, :], x_sb[:, 1, :], ACT.Copy, scale=rs_r[:, 1:2]).then_inc(xn_act, 1)

        def modulated(m):
            act.wait_ge(xT_ps, m + 1)
            act.wait_ge(mod_ready, m + 1)
            for j in (2, 3, 6, 7):
                last = do(hT[:, j, :], ps[:, XT_BANK[m] + j // 2, (j % 2) * S:(j % 2 + 1) * S], ACT.Identity,
                          scale=mod_scale[:, m, j:j + 1], bias=mod_shift[:, m, j:j + 1])
            last.then_inc(hT_act, 1)

        def multiply_pieces(a, b):
            for n in range(a, b):
                g, k = n // KT, n % KT
                act.wait_ge(ada_bg_in[n % 2], 16 * (n // 2 + 1))
                w = ada_w2[n % 2][:]
                do(ada_bg[:, g * D:(g + 1) * D] if k == 0 else w, w, ACT.Copy, scale=c_silu[:, k:k + 1]).then_inc(ada_multiplied, 1)

        act.wait_ge(c_in, 16)
        do(c_silu[:], c_col[:], ACT.Silu).then_inc(c_ready, 1)
        for dst, src in CONST_LOADS:
            act.dma_start(dst, src).then_inc(consts_in, 16)
        act.wait_ge(x_in, 16)
        prenorm(0)
        act.wait_ge(bias_ps, 1)
        do(bias_v, ps[0:8, 1:3, 0:TRI], ACT.Copy).then_inc(bias_sb, 1)
        modulated(0)
        load_rows(0)
        multiply_pieces(0, 4)

        act.wait_ge(even_unit_used, 2)
        for i in range(3):
            do(latT[:, i, :], ps[:, i, 0:S], ACT.Copy)
            last = do(lat_sq[:, i, :], ps[:, i, 0:S], ACT.Square)
        last.then_inc(lat_act, 1)
        multiply_pieces(4, 7)
        act.wait_ge(even_unit_used, 4)
        do(qT2[:, 2:4, :], ps[:, 5, :], ACT.Copy).then_inc(proj_act, 1)
        rsqrt_act(lat_v[:, 0:2, :], lat_r[:, 0:2, :])
        multiply_pieces(7, 10)
        act.wait_ge(even_unit_used, 6)
        do(kT2[:, 2:4, :], ps[:, 7, :], ACT.Copy).then_inc(proj_act, 1)
        multiply_pieces(10, 12)
        act.wait_ge(even_unit_used, 7)
        do(qT[0:QK, 4:8, :], ps[0:QK, 6:8, :], ACT.Copy).then_inc(proj_act, 1)
        act.wait_ge(knope_ps, 1)
        do(kT[0:NOPE, 4:8, :], ps[0:NOPE, 2:4, :], ACT.Copy).then_inc(proj_act, 1)
        act.wait_ge(even_unit_used, 8)
        do(v1[:, 1, :], ps[:, 2, :], ACT.Copy).then_inc(proj_act, 1)
        multiply_pieces(12, ACT_PIECES)
        act.wait_ge(even_unit_used, 10)
        do(v2[:, :, S:2 * S], ps[:, 1, :], ACT.Copy).then_inc(proj_act, 1)

        SEG = ((0, S), (S, TRI))

        def exps(i, maps):
            act.wait_ge(s_max, i + 1)
            if i >= 2:
                act.wait_ge(pT_ps, i - 1)
            for m in range(maps):
                for g, (a, b) in enumerate(SEG):
                    last = do(pr[:, i % 2, m, a:b], sc[:, i % 2, m, a:b], ACT.Exp, bias=nmax[:, i % 2, m, g:g + 1],
                              accum_out=den[:, i % 2, m, g:g + 1])
            last.then_inc(p_exp, 1)

        def pT_copy(i, bank):
            act.wait_ge(pT_ps, i + 1)
            do(pt[:, i % 2, :], ps[:, bank + i % 2, 0:TRI], ACT.Copy).then_inc(pT_sb, 1)

        H0 = DIL_H + MLA_H
        for i in range(H0 + 3):
            if i < H0:
                exps(i, 1)
            if 2 <= i < H0 + 2:
                pT_copy(i - 2, 2)
            if i >= 3:
                h = i - 3
                act.wait_ge(o_ps, h + 1)
                rows = slice(64 * (h % 2), 64 * (h % 2) + HD)
                chunk = 4 + h // 2 if h < DIL_H else (h - DIL_H) // 2
                do(oT[rows, chunk, :], ps[rows, 4 + h % 2, 0:S], ACT.Copy).then_inc(o_sb, 1)

        def out_squares(used, n0, after=None):
            sqrt_table()
            for n in range(4):
                act.wait_ge(used, n0 + n + 1)
                for c in range(2):
                    last = do(xn[:, c, n * UCOL:(n + 1) * UCOL], ps[:, n, c * UCOL:(c + 1) * UCOL], ACT.Square,
                              accum_out=y_ssq[:, c, n:n + 1])
                last.then_inc(y_squared, 1)
                if after:
                    after(n)
            rsqrt_act(rs_v[:], rs_r[:])

        def next_input(m):
            act.wait_ge(y_gated, m)
            load_rows(m)
            prenorm(m)
            modulated(m)


        def ffn(f, u0, nb, flag=None, e=None, between=None):
            blk0 = 0 if e is None else e * nb
            uses = 0 if e is None else e * (3 * nb // RING)

            def hi(t, idx, blk, it=0):
                Unit(u0 + idx).wait(act, uses + it)
                act.wait_ge((f.half_used, f.gu[0], f.down[0])[t], blk + CREDIT)
                do(w_hi[t][:], ring[(u0 + idx) % RING][:], ACT.Copy).then_inc(f.w_hi, 1)

            def silu(blk):
                def chunk(c):
                    act.wait_ge(f.gu[c], blk + (CREDIT + 1))
                    act.wait_ge(f.prod[c], blk + CREDIT)
                    do(g_silu[:, c, :], ps[:, c, 0:FB], ACT.Silu).then_inc(f.silu[c], 1)
                with_second(act, flag, lambda: chunk(1), [f.silu[1]])
                chunk(0)

            def hidden(blk):
                def chunk(c):
                    act.wait_ge(f.hT_ps[c], blk + (CREDIT + 1))
                    act.wait_ge(f.down[c], blk + CREDIT)
                    do(h_hi[:, c, :], ps[:, 2 + c, 0:FB], ACT.Copy).then_inc(f.h_hi[c], 1)
                with_second(act, flag, lambda: chunk(1), [f.h_hi[1]])
                chunk(0)

            def step(s, idx, it=0):
                hi(0, idx, blk0 + s + 1, it)
                silu(blk0 + s)
                hi(1, idx + 1, blk0 + s + 1, it)
                hidden(blk0 + s)
                hi(2, idx + 2, blk0 + s, it)

            if e is not None:
                hi(0, 0, blk0)
                hi(1, 1, blk0)
            if between:
                between()
            step(0, 2)
            turns = (nb - 2) // 2
            with act.Fori(0, turns) as it:
                step(2 * it + 1, 5, it)
                step(2 * it + 2, 8, it)
            for s in range(1 + 2 * turns, nb - 1):
                step(s, 2 + 3 * s)
            silu(blk0 + nb - 1)
            hidden(blk0 + nb - 1)
            hi(2, 3 * nb - 1, blk0 + nb - 1)

        def first_weights(n):
            if n < 2:
                Unit(DENSE0 + n).wait(act)
                do(w_hi[n][:], ring[(DENSE0 + n) % RING][:], ACT.Copy).then_inc(dense_s.w_hi, 1)

        out_squares(even_unit_used, 10, first_weights)
        next_input(1)
        act.wait_ge(hT_dve, 2)
        act.wait_ge(hT_act, 2)
        do(x_hi[:], hT[:], ACT.Copy).then_inc(dense_s.x_hi[0], 1)
        ffn(dense_s, DENSE0, DENSE_NB)
        sqrt_table()
        act.wait_ge(dense_s.down[0], CREDIT + DENSE_NB)
        act.wait_ge(dense_s.down[1], CREDIT + DENSE_NB)
        do(xn[:, 0, :], ps[:, 4:6, :], ACT.Square, accum_out=ssq[:, 0:1]).then_inc(y_squared, 1)
        act.wait_ge(y_half, 1)
        do(xn[:, 1, :], ps[:, 6:8, :], ACT.Square, accum_out=ssq[:, 1:2]).then_inc(ssq_ready, 1)
        rsqrt_act(rs_v[:], rs_r[:])
        bias_tiles(act, 1)
        next_input(2)

        for i in range(1, 12, 2):
            act.wait_ge(odd_unit_used, i + 1)
            bank = ps[:, i % 8, :]
            if i in (5, 11):
                do((v1 if i == 5 else v2)[:, :, S:2 * S], bank, ACT.Copy).then_inc(proj_act, 1)
            else:
                dst = {1: qT, 3: kT, 7: qT2, 9: kT2}[i]
                do(dst[:, 2:4, :], bank, ACT.Copy, scale=HD ** -0.5 if i == 7 else 1.0).then_inc(proj_act, 1)
        act.wait_ge(lam_sum, 1)
        do(lam_e[:], lam_s[:], ACT.Exp).then_inc(lam_exp, 1)

        for j in range(DIFF_H + 3):
            i = H0 + j
            if j < DIFF_H:
                exps(i, 2)
            if 2 <= j < DIFF_H + 2:
                pT_copy(i - 2, 4)
            if j >= 3:
                h = j - 3
                act.wait_ge(o_ps, H0 + h + 1)
                do(latT[:, h, :], ps[:, 6 + h % 2, 0:S], ACT.Copy).then_inc(o_sb, 1)
                act.wait_ge(o_sb, H0 + h + 1)
                do(lat_sq[:, h, :], latT[:, h, :], ACT.Square).then_inc(dn_sq, 1)
        rsqrt_act(lat_v[:, 0:4, :], lat_r[:, 0:4, :])

        for i in range(SB_H + 2):
            if i < SB_H:
                t = sc[:, i % 2, 1, :]
                act.wait_ge(z_ps, i + 1)
                if i >= 2:
                    act.wait_ge(z_sp, i - 1)
                chain.link(do(t, ps[:, i % 2, 0:TRI], ACT.Abs))
                chain.link(do(t, t, ACT.Exp, scale=-1.0))
                do(t, t, ACT.Ln, bias=1.0).then_inc(z_ln, 1)
            if 1 <= i <= SB_H:
                h = i - 1
                act.wait_ge(a_sb, h + 1)
                if h >= 2:
                    act.wait_ge(so_ps, h - 1)
                do(pr[:, h % 2, 0, :], pr[:, h % 2, 1, :], ACT.Exp).then_inc(w_sb, 1)
            if i >= 2:
                h = i - 2
                act.wait_ge(so_ps, h + 1)
                rows = slice(64 * (h % 2), 64 * (h % 2) + HD)
                do(oT[rows, 4 + h // 2, :], ps[rows, 6 + h % 2, 0:S], ACT.Copy).then_inc(so_sb, 1)

        out_squares(odd_unit_used, 12)
        next_input(3)

        act.wait_ge(router_sub, 1)
        do(r_e[:], r_e[:], ACT.Exp).then_inc(router_exp, 1)

        def gathered(s, n):
            own, other = ((x_tok_act, x_tok_dve), (x_tok_act1, x_tok_dve1))[s]
            act.wait_ge(gath_ps[s], n + (CREDIT + 1))
            act.wait_ge(moe_s.x_lo[0], n + (CREDIT + s))
            act.wait_ge(moe_s.x_lo[1], n + CREDIT)
            for j in range(4, KT):
                last = do(x_tok[:, j, :], ps[:, 1, (j - 4) * P:(j - 3) * P], ACT.Identity,
                          scale=mod_scale[:, 3, j:j + 1], bias=mod_shift[:, 3, j:j + 1])
            last.then_inc(own, 1)
            act.wait_ge(own, n + 1)
            act.wait_ge(other, n + 1)
            do(x_hi[:, :, s * P:(s + 1) * P], x_tok[:], ACT.Copy).then_inc(moe_s.x_hi[s], 1)

        def gathered_second(flag, n):
            with_second(act, flag, lambda: gathered(1, n), [x_tok_act1, moe_s.x_hi[1]])

        def last_outputs(flag, n):
            act.wait_ge(pick_gT_ps, n + (CREDIT + 1))
            act.wait_ge(scat_ps, n + CREDIT)
            do(pick_gT[:], ps[:, 2, :], ACT.Copy).then_inc(pick_gT_sb, 1)

            def chunk(c):
                act.wait_ge(moe_s.down[c], n * MOE_NB + CREDIT)
                do(y_tok[:, c, 512:D], ps[:, 5 + 2 * c, :], ACT.Copy).then_inc(ytok_act[c], 1)
            with_second(act, flag, lambda: chunk(1), [ytok_act[1]])
            chunk(0)

        def flag_at(i):
            return act.value_load(two_chunks[0:1, i], min_val=0, max_val=1)

        act.wait_ge(route_ready, 1)
        gathered(0, 0)
        gathered_second(flag_at(slice(1, 2)), 0)
        with act.Fori(0, NE) as e:
            last_flag, flag, next_flag = (flag_at(bass.ds(e + i, 1)) for i in range(3))
            ffn(moe_s, MOE0, MOE_NB, flag, e, between=lambda: last_outputs(last_flag, e))
            gathered(0, e + 1)
            gathered_second(next_flag, e + 1)
        last_outputs(flag_at(slice(NE, NE + 1)), NE)
        sqrt_table()
        act.wait_ge(y_added, NE + 2)
        for c in range(2):
            last = do(y_tok[:, c, :], y_sb[:, c, :], ACT.Square, accum_out=ssq[:, c:c + 1])
        last.then_inc(ssq_ready, 1)
        rsqrt_act(rs_v[:], rs_r[:])

    @block.vector
    def _(dve):
        chain = Chain(dve, dve_chain)
        v = nc.vector
        for f in (dense_s, moe_s):
            for s in (f.w_lo, *f.prod, *f.h_lo, *f.x_lo):
                dve.sem_inc(s, CREDIT)
        for s in ytok_dve:
            dve.sem_inc(s, CREDIT)

        def normalise(m, ready=False):
            if not ready:
                ssq_count[0] += 1
                dve.wait_ge(ssq_ready, ssq_count[0])
            rsqrt_dve(dve, chain, [(ssq[:], D, rs_v[:])], rs_v[:], rs_t[:], rs_r[:])

        ssq_count = [0]

        def prenorm(m):
            normalise(m)
            v.tensor_scalar(xn[:, 0, :], x_sb[:, 0, :], rs_r[:, 0:1], None, ALU.mult).then_inc(xn_dve, 1)

        def shift_scale(m):
            dve.wait_ge(mod_ps, m + 1)
            o = ps[:, MOD_BANK[m], :]
            v.tensor_tensor(mod_shift[:, m, :], o[:, 0:KT], ada_b_col[:, m, 0:KT], ALU.add)
            chain.link(v.tensor_tensor(mod_scale[:, m, :], o[:, KT:2 * KT], ada_b_col[:, m, KT:2 * KT], ALU.add))
            v.scalar_tensor_tensor(out=mod_scale[:, m, :], in0=mod_scale[:, m, :], scalar=1.0, in1=pre_col[:, m, :],
                                   op0=ALU.add, op1=ALU.mult).then_inc(mod_ready, 1)

        def gate(m):
            dve.wait_ge(gate_ps, m + 1)
            dve.wait_ge(rows_in, 32 * (m + 1))
            o = ps[:, GATE_BANK[m]:GATE_BANK[m] + 2, :].rearrange("p b n -> p (b n)")
            v.tensor_tensor(gate_row[:], o, gate_row[:], ALU.add).then_inc(gate_sb, 1)
            dve.wait_ge(gate_sb, m + 1)
            chain.link(v.tensor_tensor(gate_row[:], gate_row[:], post_row[:], ALU.mult))

        def modulated(m):
            dve.wait_ge(xT_ps, m + 1)
            dve.wait_ge(mod_ready, m + 1)
            for j in (0, 1, 4, 5):
                last = v.tensor_scalar(hT[:, j, :], ps[:, XT_BANK[m] + j // 2, (j % 2) * S:(j % 2 + 1) * S],
                                       mod_scale[:, m, j:j + 1], mod_shift[:, m, j:j + 1], ALU.mult, ALU.add)
            last.then_inc(hT_dve, 1)

        dve.wait_ge(c_ready, 1)
        def ada(n, u):
            g, kp = u // 4, u % 4
            un = Unit(n)
            un.wait(dve)
            acc = ada_fg[:, g * D:(g + 1) * D]
            for i in range(2):
                k = 2 * kp + i
                w = un.slot[:, i * D:(i + 1) * D]
                if k == 0:
                    ins = v.tensor_scalar(acc, w, c_silu[:, k:k + 1], None, ALU.mult)
                else:
                    ins = v.scalar_tensor_tensor(out=acc, in0=w, scalar=c_silu[:, k:k + 1], in1=acc, op0=ALU.mult, op1=ALU.add)
                if i == 0:
                    chain.link(ins)
            ins.then_inc(ada_unit_used, 1)
            dve.wait_ge(ada_unit_used, u + 1)
            if kp == 3:
                dve.sem_inc(ada_fg_ready, 1)

        for u in range(ADA_UNITS):
            if u == 4:
                prenorm(0)
            ada(u, u)
        dve.wait_ge(early_in, N_EARLY)
        shift_scale(0)
        modulated(0)
        dve.wait_ge(consts_in, N_CONSTS)

        dve.wait_ge(even_unit_used, 2)
        chain.link(v.tensor_copy(latT[NOPE:QK, 3, :], ps[NOPE:QK, 3, 0:S]))
        dve.wait_ge(even_unit_used, 3)
        v.tensor_copy(qT2[:, 0:2, :], ps[:, 4, :]).then_inc(proj_dve, 1)
        dve.wait_ge(lat_act, 1)
        dve.wait_ge(lat_ps, 1)
        rsqrt_dve(dve, chain, [(ps[:, 2, 0:S], Q_RANK, lat_v[:, 0, :]), (ps[:, 2, S:2 * S], KV_RANK, lat_v[:, 1, :])],
                  lat_v[:, 0:2, :], lat_t[:, 0:2, :], lat_r[:, 0:2, :])
        for i in range(3):
            last = v.scalar_tensor_tensor(out=latT[:, i, :], in0=latT[:, i, :], scalar=vec_g[:, i:i + 1], in1=lat_r[:, i // 2, :],
                                          op0=ALU.mult, op1=ALU.mult)
        last.then_inc(lat_ready, 1)
        dve.wait_ge(even_unit_used, 5)
        v.tensor_copy(kT2[:, 0:2, :], ps[:, 6, :]).then_inc(proj_dve, 1)
        for i in range(2):
            ada(GATE0 + i, ADA_UNITS + i)
        dve.wait_ge(even_unit_used, 7)
        v.tensor_copy(qT[0:QK, 0:4, :], ps[0:QK, 4:6, :]).then_inc(proj_dve, 1)
        dve.wait_ge(knope_ps, 1)
        v.tensor_copy(kT[0:NOPE, 0:4, :], ps[0:NOPE, 0:2, :]).then_inc(proj_dve, 1)
        dve.wait_ge(even_unit_used, 8)
        v.tensor_copy(v1[:, 0, :], ps[:, 1, :]).then_inc(proj_dve, 1)
        R = slice(NOPE, QK)
        sin8 = k_sin[R, :].unsqueeze(1).to_broadcast([ROPE, MLA_H, S])
        cos8 = k_cos[R, :].unsqueeze(1).to_broadcast([ROPE, MLA_H, S])
        dve.wait_ge(rot_ps, 1)
        v.tensor_tensor(lat_v[R, 2, :], latT[R, 3, :], k_cos[R, :], ALU.mult)
        v.tensor_tensor(rope_t[R], ps[R, 4:8, :].rearrange("p b (h t) -> p (b h) t", h=2), sin8, ALU.mult)
        chain.link(v.tensor_tensor(lat_v[R, 3, :], ps[R, 0, 0:S], k_sin[R, :], ALU.mult))
        v.tensor_tensor(kT[R], lat_v[R, 2, :].unsqueeze(1).to_broadcast([ROPE, MLA_H, S]),
                        lat_v[R, 3, :].unsqueeze(1).to_broadcast([ROPE, MLA_H, S]), ALU.add)
        chain.link(v.tensor_tensor(qT[R], qT[R], cos8, ALU.mult))
        v.tensor_tensor(qT[R], qT[R], rope_t[R], ALU.add).then_inc(rope_ready, 1)
        for i in range(2, 4):
            ada(GATE0 + i, ADA_UNITS + i)
        dve.wait_ge(even_unit_used, 9)
        v.tensor_copy(v2[:, :, 0:S], ps[:, 3, :]).then_inc(proj_dve, 1)

        SEG = ((0, S), (S, TRI))
        H0 = DIL_H + MLA_H

        def scores(i, b0, biases, scale, first):
            dve.wait_ge(s_ps, i + 1)
            if i >= first + 2:
                dve.wait_ge(p_exp, i - 1)
            for m, b in enumerate(biases):
                last = v.scalar_tensor_tensor(out=sc[:, i % 2, m, :], in0=ps[:, b0 + m, 0:TRI], scalar=scale, in1=b,
                                              op0=ALU.mult, op1=ALU.add)
            last.then_inc(s_free, 1)
            dve.wait_ge(s_free, i + 1)
            for m in range(len(biases)):
                for g, (a, b) in enumerate(SEG):
                    last = v.tensor_reduce(nmax[:, i % 2, m, g:g + 1], sc[:, i % 2, m, a:b], AX.X, ALU.max, negate=True)
            last.then_inc(s_max, 1)

        def normalised(i):
            dve.wait_ge(p_exp, i + 1)
            r = rden[:, i % 2, 0, :]
            chain.link(v.reciprocal(r, den[:, i % 2, 0, :]))
            for g, (a, b) in enumerate(SEG):
                last = v.tensor_scalar(pr[:, i % 2, 0, a:b], pr[:, i % 2, 0, a:b], r[:, g:g + 1], None, ALU.mult)
            last.then_inc(p_ready, 1)

        for i in range(H0 + 1):
            if i < H0:
                if i == 0:
                    dve.wait_ge(bias_in, 32)
                b = bias[:, i, :] if i < DIL_H else k_causal[:]
                scores(i, i % 2, [b], (HD if i < DIL_H else QK) ** -0.5, 0)
            if i >= 1:
                normalised(i - 1)

        def gated_columns(used, n0, squared, after=None):
            for n in range(4):
                dve.wait_ge(used, n0 + n + 1)
                dve.wait_ge(y_squared, squared + n + 1)
                w = slice(n * UCOL, (n + 1) * UCOL)
                last = v.tensor_tensor(y_sb[:, :, w], ps[:, n, :].rearrange("p (c n) -> p c n", c=2),
                                       gate_row[:, w].unsqueeze(1).to_broadcast([P, 2, UCOL]), ALU.mult)
                if n == 3:
                    last.then_inc(y_gated, 1)
                if after:
                    after(n)

        def residual(m, gated, parts):
            if parts:
                chain.link(v.tensor_reduce(ssq[:], y_ssq[:], AX.X, ALU.add))
            normalise(m, ready=parts)
            dve.wait_ge(y_gated, m + 1)
            for c in range(2):
                v.scalar_tensor_tensor(out=x_sb[:, c, :], in0=gated[:, c, :], scalar=rs_r[:, c:c + 1], in1=x_sb[:, c, :],
                                       op0=ALU.mult, op1=ALU.add).then_inc(x_new, 1)
            dve.wait_ge(x_new, 2 * (m + 1))

        def next_input(m):
            residual(m - 1, y_sb, m != 2)
            prenorm(m)
            shift_scale(m)
            modulated(m)

        gate(0)

        def ffn(f, u0, nb, flag=None, e=None, between=None, added=None):
            blk0 = 0 if e is None else e * nb
            un0 = 0 if e is None else e * (3 * nb)

            def lo(t, idx, it=0):
                dve.wait_ge(f.w_hi, un0 + 6 * it + (idx + CREDIT + 1))
                v.tensor_tensor(w_lo[t][:], ring[(u0 + idx) % RING][:], w_hi[t][:].bitcast(F32), ALU.subtract).then_inc(f.w_lo, 1)

            def product(blk):
                def chunk(c):
                    dve.wait_ge(f.silu[c], blk + (CREDIT + 1))
                    dve.wait_ge(f.hT_ps[c], blk + CREDIT)
                    v.tensor_tensor(prod[:, c, :], ps[:, c, FB:2 * FB], g_silu[:, c, :], ALU.mult).then_inc(f.prod[c], 1)
                with_second(dve, flag, lambda: chunk(1), [f.prod[1]])
                chunk(0)

            def hidden(blk):
                def chunk(c):
                    dve.wait_ge(f.h_hi[c], blk + (CREDIT + 1))
                    v.tensor_tensor(h_lo[:, c, :], ps[:, 2 + c, 0:FB], h_hi[:, c, :].bitcast(F32), ALU.subtract).then_inc(f.h_lo[c], 1)
                with_second(dve, flag, lambda: chunk(1), [f.h_lo[1]])
                chunk(0)

            def step(s, idx, it=0, added=None):
                lo(0, idx, it)
                product(blk0 + s)
                lo(1, idx + 1, it)
                if added:
                    added()
                hidden(blk0 + s)
                lo(2, idx + 2, it)

            if e is not None:
                lo(0, 0)
                lo(1, 1)
            if between:
                between()
            step(0, 2, added=added)
            turns = (nb - 2) // 2
            with dve.Fori(0, turns) as it:
                step(2 * it + 1, 5, it)
                step(2 * it + 2, 8, it)
            for s in range(1 + 2 * turns, nb - 1):
                step(s, 2 + 3 * s)
            product(blk0 + nb - 1)
            hidden(blk0 + nb - 1)
            lo(2, 3 * nb - 1)

        def first_weights(n):
            if 1 <= n < 3:
                dve.wait_ge(dense_s.w_hi, CREDIT + n)
                v.tensor_tensor(w_lo[n - 1][:], ring[(DENSE0 + n - 1) % RING][:], w_hi[n - 1][:].bitcast(F32),
                                ALU.subtract).then_inc(dense_s.w_lo, 1)

        gated_columns(even_unit_used, 10, 0, first_weights)
        next_input(1)
        dve.wait_ge(dense_s.x_hi[0], CREDIT + 1)
        v.tensor_tensor(x_lo[:], hT[:], x_hi[:].bitcast(F32), ALU.subtract).then_inc(dense_s.x_lo[0], 1)
        gate(1)
        ffn(dense_s, DENSE0, DENSE_NB)
        dve.wait_ge(dense_s.down[0], CREDIT + DENSE_NB)
        dve.wait_ge(dense_s.down[1], CREDIT + DENSE_NB)
        v.tensor_tensor(y_sb[:, 1, :], ps[:, 6:8, :].rearrange("p b n -> p (b n)"), gate_row[:], ALU.mult).then_inc(y_half, 1)
        dve.wait_ge(y_squared, 5)
        v.tensor_tensor(y_sb[:, 0, :], ps[:, 4:6, :].rearrange("p b n -> p (b n)"), gate_row[:], ALU.mult).then_inc(y_gated, 1)
        next_input(2)
        gate(2)

        for i in range(0, 12, 2):
            dve.wait_ge(odd_unit_used, i + 1)
            bank = ps[:, i % 8, :]
            if i in (4, 10):
                v.tensor_copy((v1 if i == 4 else v2)[:, :, 0:S], bank).then_inc(proj_dve, 1)
            elif i == 6:
                v.tensor_scalar(qT2[:, 0:2, :], bank, HD ** -0.5, None, ALU.mult).then_inc(proj_dve, 1)
            else:
                v.tensor_copy({0: qT, 2: kT, 8: kT2}[i][:, 0:2, :], bank).then_inc(proj_dve, 1)
        chain.link(v.tensor_tensor(lam_p[:], lam_in[:, 0::2, :], lam_in[:, 1::2, :], ALU.mult))
        v.tensor_reduce(lam_s[:], lam_p[:], AX.X, ALU.add).then_inc(lam_sum, 1)
        dve.wait_ge(lam_exp, 1)
        v.tensor_scalar(sub_scaled[:], vec_g[:, 3:4], 1.0 - LAM_INIT, None, ALU.mult)
        chain.link(v.scalar_tensor_tensor(out=lam[:], in0=lam_e[:, 0:1], scalar=LAM_INIT, in1=lam_e[:, 1:2],
                                          op0=ALU.add, op1=ALU.subtract))

        def difference(i):
            dve.wait_ge(p_exp, i + 1)
            chain.link(v.reciprocal(rden[:, i % 2, :, :], den[:, i % 2, :, :]))
            chain.link(v.tensor_scalar(rden[:, i % 2, 1, :], rden[:, i % 2, 1, :], lam[:], None, ALU.mult))
            for g, (a, b) in enumerate(SEG):
                chain.mark(v.tensor_scalar(pr[:, i % 2, 1, a:b], pr[:, i % 2, 1, a:b], rden[:, i % 2, 1, g:g + 1], None, ALU.mult))
            chain.wait()
            for g, (a, b) in enumerate(SEG):
                last = v.scalar_tensor_tensor(out=pr[:, i % 2, 0, a:b], in0=pr[:, i % 2, 0, a:b], scalar=rden[:, i % 2, 0, g:g + 1],
                                              in1=pr[:, i % 2, 1, a:b], op0=ALU.mult, op1=ALU.subtract)
            last.then_inc(p_ready, 1)

        dve.wait_ge(bias_in, 64)
        for j in range(DIFF_H + 1):
            i = H0 + j
            if j < DIFF_H:
                scores(i, 2 * (i % 2), [bias[:, 2 * j, :], bias[:, 2 * j + 1, :]], HD ** -0.5, H0)
            if j >= 1:
                difference(i - 1)
        dve.wait_ge(dn_ps, 1)
        rsqrt_dve(dve, chain, [(ps[:, 4:6, :].rearrange("p b (h t) -> p (b h) t", h=2), 2 * HD, lat_v[:, 0:4, :])],
                  lat_v[:, 0:4, :], lat_t[:, 0:4, :], lat_r[:, 0:4, :])
        v.scalar_tensor_tensor(out=oT[:, 0:4, :], in0=latT[:, 0:4, :], scalar=sub_scaled[:], in1=lat_r[:, 0:4, :],
                               op0=ALU.mult, op1=ALU.mult).then_inc(dn_done, 1)

        for i in range(SB_H + 1):
            if i < SB_H:
                dve.wait_ge(z_ln, i + 1)
                if i >= 2:
                    dve.wait_ge(a_ps, i - 1)
                chain.link(v.scalar_tensor_tensor(out=sc[:, i % 2, 0, :], in0=ps[:, i % 2, 0:TRI], scalar=0.0, in1=sc[:, i % 2, 1, :],
                                                  op0=ALU.max, op1=ALU.add))
                v.tensor_tensor(sc[:, i % 2, 0, :], sc[:, i % 2, 0, :], k_strict01[:], ALU.mult).then_inc(z_sp, 1)
            if i >= 1:
                h = i - 1
                dve.wait_ge(a_ps, h + 1)
                if h >= 2:
                    dve.wait_ge(w_sb, h - 1)
                v.tensor_tensor(pr[:, h % 2, 1, :], ps[:, 2 + h % 2, 0:TRI], k_strict[:], ALU.add).then_inc(a_sb, 1)

        gated_columns(odd_unit_used, 12, 5)
        next_input(3)
        gate(3)

        dve.wait_ge(router_ps, 1)
        v.memset(slot_of[:], 0.0)
        v.memset(gate_of[:], 0.0)
        v.memset(two_chunks[:], 0)
        v.memset(y_sb[:], 0.0).then_inc(y_added, 1)
        dve.wait_ge(y_added, 1)
        chain.link(v.tensor_tensor(r_log[:], ps[:, 0, 0:2 * NE].rearrange("p (c n) -> p c n", c=2),
                                   rb_row[:].unsqueeze(1).to_broadcast([P, 2, NE]), ALU.add))
        for c in range(2):
            chain.mark(v.max(r_max[:, c, :], r_log[:, c, :]))
        chain.wait()
        for c in range(2):
            chain.mark(v.max_index(r_idx[:, c, :], r_max[:, c, :], r_log[:, c, :]))
        v.tensor_tensor(r_e[:], r_max[:, :, 1], r_max[:, :, 0], ALU.subtract).then_inc(router_sub, 1)
        chain.wait()
        chain.link(v.tensor_copy(r_idxf[:], r_idx[:]))
        for c in range(2):
            for m, mask in enumerate((r_m0, r_m1)):
                chain.mark(v.tensor_scalar(mask[:, c, :], k_iota[:, 0:NE], r_idxf[:, c, m:m + 1], None, ALU.is_equal))
        chain.wait()
        v.tensor_tensor(r_mask[:], r_m0[:], r_m1[:], ALU.add).then_inc(router_mask, 1)
        dve.wait_ge(router_exp, 1)
        chain.link(v.tensor_scalar(r_w0[:], r_e[:], 1.0, None, ALU.add))
        chain.link(v.reciprocal(r_w0[:], r_w0[:]))
        chain.link(v.tensor_tensor(r_w1[:], r_e[:], r_w0[:], ALU.mult))
        for c in range(2):
            chain.mark(v.tensor_scalar(r_m0[:, c, :], r_m0[:, c, :], r_w0[:, c:c + 1], None, ALU.mult))
        chain.wait()
        for c in range(2):
            chain.mark(v.scalar_tensor_tensor(out=gate_of[:, c, 1:1 + NE], in0=r_m1[:, c, :], scalar=r_w1[:, c:c + 1], in1=r_m0[:, c, :],
                                              op0=ALU.mult, op1=ALU.add))
        chain.wait()
        dve.wait_ge(router_mask, 1)
        dve.wait_ge(pos_ps, 1)
        chain.mark(v.scalar_tensor_tensor(out=slot_of[:, :, 1:1 + NE], in0=ps[:, 1, 0:2 * NE].rearrange("p (c n) -> p c n", c=2),
                                          scalar=1.0, in1=r_mask[:], op0=ALU.add, op1=ALU.mult))
        chain.mark(v.tensor_scalar(two_chunks[0:1, 1:1 + NE], ps[0:1, 1, 2 * NE:3 * NE], P + 0.5, None, ALU.is_gt))
        chain.wait()
        v.tensor_scalar(slot_of[:], slot_of[:], -1.0, None, ALU.add).then_inc(route_ready, 1)
        dve.wait_ge(route_ready, 1)

        def picks(col):
            for c in range(2):
                last = v.tensor_scalar(pick[:, c, :], k_iota[:], slot_of[:, c, col], None, ALU.is_equal)
            last.then_inc(pick_ready, 1)

        def last_picks(n, col):
            dve.wait_ge(pick_gT_ps, n + CREDIT)
            for c in range(2):
                last = v.tensor_scalar(pick_g[:, c, :], k_iota[:], slot_of[:, c, col], gate_of[:, c, col], ALU.is_equal, ALU.mult)
            last.then_inc(pick_g_ready, 1)

        def gathered(s, n):
            own, other = ((x_tok_dve, x_tok_act), (x_tok_dve1, x_tok_act1))[s]
            dve.wait_ge(gath_ps[s], n + (CREDIT + 1))
            dve.wait_ge(moe_s.x_lo[0], n + (CREDIT + s))
            dve.wait_ge(moe_s.x_lo[1], n + CREDIT)
            t = x_tok[:, 0:4, :]
            v.tensor_tensor(t, ps[:, 0, :].rearrange("p (j n) -> p j n", j=4), mod_scale[:, 3, 0:4].unsqueeze(2).to_broadcast([P, 4, P]),
                            ALU.mult).then_inc(x_tok_mul[s], 1)
            dve.wait_ge(x_tok_mul[s], n + 1)
            v.tensor_tensor(t, t, mod_shift[:, 3, 0:4].unsqueeze(2).to_broadcast([P, 4, P]), ALU.add).then_inc(own, 1)
            dve.wait_ge(own, n + 1)
            dve.wait_ge(other, n + 1)
            dve.wait_ge(moe_s.x_hi[s], n + (CREDIT + 1))
            v.tensor_tensor(x_lo[:, :, s * P:(s + 1) * P], x_tok[:], x_hi[:, :, s * P:(s + 1) * P].bitcast(F32),
                            ALU.subtract).then_inc(moe_s.x_lo[s], 1)

        def gathered_second(flag, n):
            with_second(dve, flag, lambda: gathered(1, n), [x_tok_mul[1], x_tok_dve1, moe_s.x_lo[1]])

        def last_outputs(flag, n):
            def chunk(c):
                dve.wait_ge(moe_s.down[c], n * MOE_NB + CREDIT)
                dve.wait_ge(scat_ps, n + CREDIT)
                v.tensor_copy(y_tok[:, c, 0:512], ps[:, 4 + 2 * c, :]).then_inc(ytok_dve[c], 1)
            with_second(dve, flag, lambda: chunk(1), [ytok_dve[1]])
            chunk(0)

        def add_scattered(n):
            dve.wait_ge(scat_ps, n + (CREDIT + 1))
            dve.wait_ge(y_added, n + 1)
            for c in range(2):
                last = v.tensor_tensor(y_sb[:, c, :], ps[:, 4 + 2 * c:6 + 2 * c, :].rearrange("p b n -> p (b n)"), y_sb[:, c, :], ALU.add)
            last.then_inc(y_added, 1)

        def flag_at(i):
            return dve.value_load(two_chunks[0:1, i], min_val=0, max_val=1)

        picks(slice(1, 2))
        gathered(0, 0)
        gathered_second(flag_at(slice(1, 2)), 0)
        with dve.Fori(0, NE) as e:
            last_flag, flag, next_flag = (flag_at(bass.ds(e + i, 1)) for i in range(3))
            last_picks(e, bass.ds(e, 1))
            picks(bass.ds(e + 2, 1))
            ffn(moe_s, MOE0, MOE_NB, flag, e, between=lambda: last_outputs(last_flag, e), added=lambda: add_scattered(e))
            gathered(0, e + 1)
            gathered_second(next_flag, e + 1)
        last_picks(NE, slice(NE, NE + 1))
        last_outputs(flag_at(slice(NE, NE + 1)), NE)
        add_scattered(NE)
        dve.wait_ge(y_added, NE + 2)
        for c in range(2):
            last = v.tensor_tensor(xn[:, c, :], y_sb[:, c, :], gate_row[:], ALU.mult)
        last.then_inc(y_gated, 1)
        residual(3, xn, False)

    ctx.close()


def kernel(**inputs):
    import concourse.bacc as bacc
    from concourse.bass_utils import run_bass_kernel_spmd

    nc = bacc.Bacc("TRN2", target_bir_lowering=False, num_devices=1)
    arrays = {name: np.ascontiguousarray(inputs[name]) for name in _INS}
    for name, mix, ffn in (("ada_w", "ada_mix_w", "ada_ffn_w"), ("ada_b", "ada_mix_b", "ada_ffn_b"),
                           ("pre_g", "mix_pre_g", "ffn_pre_g"), ("post_g", "mix_post_g", "ffn_post_g")):
        a, b = np.asarray(inputs[mix]), np.asarray(inputs[ffn])
        arrays[name] = np.stack([a[0], b[0], a[1], b[1]])
    def columns(a, lead=0):
        a = np.asarray(a)
        a = a.reshape(a.shape[:lead] + (a.shape[lead] // P, P) + a.shape[lead + 1:])
        return np.ascontiguousarray(np.moveaxis(a, lead + 1, 0))

    arrays["c_cols"] = columns(inputs["c"][0])
    arrays["ada_b_cols"] = columns(arrays["ada_b"][:, 0:2 * D], 1)
    arrays["pre_cols"] = columns(arrays["pre_g"], 1)
    arrays["vec_cols"] = np.concatenate([columns(inputs[n][0]) for n in ("e_q_norm_g", "e_kv_norm_g", "diff_sub_g")], 1)
    arrays["router_cols"] = columns(inputs["router_w"][0])
    del arrays["pre_g"]
    arrays.update(shape_constants())
    aps = {}
    for name, a in arrays.items():
        aps[name] = nc.dram_tensor(f"in_{name}", a.shape, mybir.dt.from_np(a.dtype), kind="ExternalInput").ap()
    out = nc.dram_tensor("out_0", (1, S, D), F32, kind="ExternalOutput").ap()
    build(nc, aps, out)
    r = run_bass_kernel_spmd(nc, [{f"in_{name}": a for name, a in arrays.items()}], core_ids=[0])
    return r.results[0]["out_0"]
```

```python
import math
from contextlib import ExitStack

import numpy as np

import concourse.bass as bass
from concourse import mybir

F32 = mybir.dt.float32
F32R = mybir.dt.float32r
I32 = mybir.dt.int32
U32 = mybir.dt.uint32
ACT = mybir.ActivationFunctionType
ALU = mybir.AluOpType
AX = mybir.AxisListType

P = 128
D = 1024
S = 256
KT = D // P
EPS = 1e-6
HD = 64
MLA_H, DIL_H, DIFF_H, SB_H = 8, 8, 4, 8
NOPE, ROPE = 64, 32
PAIRS = SB_H // 2
DN_NORM = 7
QK = NOPE + ROPE
Q_RANK, KV_RANK = 256, 128
MLA_IN = Q_RANK + KV_RANK + ROPE
D_FF, D_FFE, NE = 2816, 3584, 8
FB = 256
RING = 6
UNIT = 2048
UCOL = UNIT // KT
LAM_INIT = 0.8 - 0.6 * math.exp(-0.3 * 1)
NEG = -1e30
TRI = S + P

ADA_UNITS = 8
EVEN_IN0 = ADA_UNITS
GATE0 = EVEN_IN0 + 6
EVEN_UP0 = GATE0 + 4
EVEN_OUT0 = EVEN_UP0 + 4
DENSE0 = EVEN_OUT0 + 4
DENSE_NB = D_FF // FB
ODD_IN0 = DENSE0 + 3 * DENSE_NB
ODD_OUT0 = ODD_IN0 + 12
MOE0 = ODD_OUT0 + 4
MOE_NB = D_FFE // FB
PIECES = 3 * KT
ACT_PIECES = 15
NARROW = P // 2
CREDIT = 8


def shape_constants():
    f32 = np.float32
    k, m = np.arange(P)[:, None], np.arange(P)[None, :]
    c = {"ident": (k == m).astype(f32), "ones": np.ones((P, P), f32)}
    c["neg_suffix"] = -(k >= m).astype(f32)
    c["neg_ones"] = -np.ones((P, P), f32)
    c["before"] = (k < m).astype(f32)
    q, j = np.arange(P)[:, None], np.arange(S)[None, :]
    causal = np.where(j <= q + P, 0.0, NEG)
    c["causal"] = np.concatenate([causal, causal[:, P:]], 1).astype(f32)
    strict0 = np.where(np.arange(P)[:, None] < np.arange(S)[None, :], 0.0, NEG)
    c["strict"] = np.concatenate([strict0, strict0[:, :P]], 1).astype(f32)
    c["strict01"] = (c["strict"] == 0).astype(f32)
    c["iota"] = np.broadcast_to(np.arange(S, dtype=f32), (P, S)).copy()
    half = ROPE // 2
    freqs = (f32(10000.0) ** (-np.arange(half, dtype=f32) / f32(half))).astype(f32)
    ang = (np.arange(S, dtype=f32)[:, None] * freqs[None, :]).astype(f32)
    cos, sin, rot = np.zeros((P, S), f32), np.zeros((P, S), f32), np.zeros((P, ROPE), f32)
    for r in range(ROPE):
        cos[NOPE + r], sin[NOPE + r] = np.cos(ang[:, r % half]), np.sin(ang[:, r % half])
        rot[NOPE + (r + half if r < half else r - half), r] = -1.0 if r < half else 1.0
    c["cos"], c["sin"], c["rot"] = cos, sin, rot
    dist = 255 - np.arange(TRI)
    d = np.maximum(dist, 1).astype(f32)
    log_b = 16 + (np.log(d / f32(16)) / f32(math.log(2048 / 16)) * f32(16)).astype(np.int32)
    bucket = np.where(dist < 16, np.maximum(dist, 0), np.minimum(log_b, 31))
    hot = (np.arange(32)[:, None] == bucket[None, :]) & (dist >= 0)[None, :]
    count = ((dist >= 0) & (dist <= 128)).astype(int) + ((dist >= 0) & (dist % 4 == 0)) + ((dist >= 0) & (dist % 16 == 0))
    dil = np.where(count > 0, np.log(np.maximum(count, 1).astype(np.float64)), NEG)
    dif = np.where(dist >= 0, 0.0, NEG)
    c["bias_hot"] = np.stack([np.vstack([hot, x[None]]) for x in (dil, dif)]).astype(f32)
    return c


_INS = ["x", "rel_bias", "e_w_in", "e_w_uq", "e_w_ukv", "e_w_out",
        "ffn_w_gate", "ffn_w_up", "ffn_w_down", "o_w_in", "diff_lq1", "diff_lk1", "diff_lq2", "diff_lk2",
        "o_w_out", "router_b", "moe_w_gate", "moe_w_up", "moe_w_down"]


def build(nc, A, out):
    ctx = ExitStack()

    def sb(name, shape, dt=F32, scope=None):
        return (scope or ctx).enter_context(nc.sbuf_tensor(name, shape, dt))

    def sem(name):
        return ctx.enter_context(nc.semaphore(name))

    ring = [sb(f"ring{i}", [P, UNIT]) for i in range(RING)]
    k_ident, k_ones = sb("k_ident", [P, P]), sb("k_ones", [P, P])
    k_neg_suffix, k_neg_ones, k_before = sb("k_neg_suffix", [P, P]), sb("k_neg_ones", [P, P]), sb("k_before", [P, P])
    k_causal, k_strict, k_iota = sb("k_causal", [P, TRI]), sb("k_strict", [P, TRI]), sb("k_iota", [P, S])
    k_strict01 = sb("k_strict01", [P, TRI])
    k_cos, k_sin, k_rot = sb("k_cos", [P, S]), sb("k_sin", [P, S]), sb("k_rot", [P, ROPE])
    x_sb = sb("x_sb", [P, 2, D])
    y_sb = sb("y_sb", [P, 2, D])
    xn = sb("xn", [P, 2, D])
    hT = sb("hT", [P, KT, S])
    gate_row = sb("gate_row", [P, D])
    post_row = sb("post_row", [P, D])
    ada_bg = sb("ada_bg", [P, 3 * D])
    ada_w2 = [sb(f"ada_w{i}", [P, D]) for i in range(2)]
    c_col, c_silu = sb("c_col", [P, KT]), sb("c_silu", [P, KT])
    ada_b_col, pre_col = sb("ada_b_col", [P, 4, 16]), sb("pre_col", [P, 4, KT])
    mod_scale, mod_shift = sb("mod_scale", [P, 4, KT]), sb("mod_shift", [P, 4, KT])
    ssq, rs_v, rs_t, rs_r = (sb(n, [P, 2]) for n in ("ssq", "rs_v", "rs_t", "rs_r"))
    y_ssq, table = sb("y_ssq", [P, 2, 4]), sb("table", [P, 1])
    vec_g = sb("vec_g", [P, 4])
    rw_sb, rb_row = sb("rw_sb", [P, KT, NE]), sb("rb_row", [P, NE])
    lam_in, lam_p = sb("lam_in", [P, 4, HD]), sb("lam_p", [P, 2, HD])
    lam_s, lam_e, lam, sub_scaled = sb("lam_s", [P, 2]), sb("lam_e", [P, 2]), sb("lam", [P, 1]), sb("sub_scaled", [P, 1])

    at = ExitStack()
    ada_fg = sb("ada_fg", [P, 3 * D], scope=at)
    qT, kT = sb("qT", [P, 8, S], scope=at), sb("kT", [P, 8, S], scope=at)
    qT2, kT2 = sb("qT2", [P, 4, S], scope=at), sb("kT2", [P, 4, S], scope=at)
    v1, v2 = sb("v1", [P, 2, 512], scope=at), sb("v2", [P, 2, 512], scope=at)
    oT = sb("oT", [P, 8, S], scope=at)
    latT = sb("latT", [P, 4, S], scope=at)
    lat_sq, lat_v = (y_sb[:, c, :].rearrange("p (i t) -> p i t", i=4) for c in range(2))
    lat_t, lat_r = (xn[:, c, :].rearrange("p (i t) -> p i t", i=4) for c in range(2))
    rope_t = ada_fg[:, 0:8 * S].rearrange("p (h t) -> p h t", h=8)
    bias = sb("bias", [P, 8, TRI], scope=at)
    bias_w = sb("bias_w", [33, 8], scope=at)
    hT_flat = hT[:].rearrange("p k t -> p (k t)")
    sc = sb("sc", [P, 2, 2, TRI], scope=at)
    bias_hot, bias_v = sc[0:33, 0, :, :], sc[0:8, 1, :, :]
    pr = sb("pr", [P, 2, 2, TRI], scope=at)
    pt = sb("pt", [P, 2, TRI], scope=at)
    nmax, den, rden = (sb(n, [P, 2, 2, 2], scope=at) for n in ("nmax", "den", "rden"))
    at.close()

    ff = ExitStack()
    w_hi = [sb(f"w_hi{i}", [P, UNIT], F32R, ff) for i in range(3)]
    w_lo = [sb(f"w_lo{i}", [P, UNIT], F32R, ff) for i in range(3)]
    x_hi, x_lo = sb("x_hi", [P, KT, S], F32R, ff), sb("x_lo", [P, KT, S], F32R, ff)
    g_silu, prod = sb("g_silu", [P, 2, FB], scope=ff), sb("prod", [P, 2, FB], scope=ff)
    h_hi, h_lo = sb("h_hi", [P, 2, FB], F32R, ff), sb("h_lo", [P, 2, FB], F32R, ff)
    x_tok = sb("x_tok", [P, KT, P], scope=ff)
    pick, pick_g = sb("pick", [P, 2, S], scope=ff), sb("pick_g", [P, 2, S], scope=ff)
    pick_gT = sb("pick_gT", [P, 2, S], scope=ff)
    y_tok = hT_flat.rearrange("p (c d) -> p c d", c=2)
    r_log, r_m0, r_m1, r_mask = (sb(n, [P, 2, NE], scope=ff) for n in ("r_log", "r_m0", "r_m1", "r_mask"))
    r_max, r_idxf = sb("r_max", [P, 2, 8], scope=ff), sb("r_idxf", [P, 2, 8], scope=ff)
    r_idx = sb("r_idx", [P, 2, 8], U32, ff)
    r_e, r_w0, r_w1 = sb("r_e", [P, 2], scope=ff), sb("r_w0", [P, 2], scope=ff), sb("r_w1", [P, 2], scope=ff)
    slot_of, gate_of = sb("slot_of", [P, 2, 12], scope=ff), sb("gate_of", [P, 2, 12], scope=ff)
    slot2_of = sb("slot2_of", [P, 2, 12], scope=ff)
    r_many = sb("r_many", [P, 2, NE], scope=ff)
    second = sb("second", [1, 12], I32, ff)
    folded = sb("folded", [NARROW, 2 * FB], scope=ff)
    ff.close()

    ps = ctx.enter_context(nc.psum_tensor("ps", [P, 8, 512], F32))
    MOD_BANK, GATE_BANK, XT_BANK = (0, 5, 1, 5), (6, 6, 2, 6), (4, 0, 4, 0)
    bias_dram = nc.dram_tensor("bias_dram", (2, 8, P, TRI), F32, kind="Internal").ap()

    landed = [sem(f"landed{i}") for i in range(RING)]
    consts_in, x_in, rows_in = sem("consts_in"), sem("x_in"), sem("rows_in")
    c_ready = sem("c_ready")
    ada_unit_used, even_unit_used, odd_unit_used = sem("ada_unit_used"), sem("even_unit_used"), sem("odd_unit_used")
    ada_fg_ready, ada_bg_step, ada_bg_ready = sem("ada_fg_ready"), sem("ada_bg_step"), sem("ada_bg_ready")
    ada_bg_in = [sem(f"ada_bg_in{i}") for i in range(2)]
    mod_ps, mod_used, mod_ready, gate_ps, gate_sb = (sem(n) for n in ("mod_ps", "mod_used", "mod_ready", "gate_ps", "gate_sb"))
    c_in, early_in, ada_multiplied = sem("c_in"), sem("early_in"), sem("ada_multiplied")
    rs_var, rs_ln, rs_estimate, ssq_ready, rs_done = sem("rs_var"), sem("rs_ln"), sem("rs_estimate"), sem("ssq_ready"), sem("rs_done")
    xn_dve, xn_act, xT_ps, hT_dve, hT_act = sem("xn_dve"), sem("xn_act"), sem("xT_ps"), sem("hT_dve"), sem("hT_act")
    dve_chain, act_chain = sem("dve_chain"), sem("act_chain")
    bias_ps, bias_sb, bias_out, bias_in = sem("bias_ps"), sem("bias_sb"), sem("bias_out"), sem("bias_in")
    knope_ps, proj_dve, proj_act = sem("knope_ps"), sem("proj_dve"), sem("proj_act")
    lat_act, lat_ps, lat_ready, rot_ps, rope_ready = sem("lat_act"), sem("lat_ps"), sem("lat_ready"), sem("rot_ps"), sem("rope_ready")
    s_ps, s_free, s_max, p_exp, p_ready, pT_ps, pT_sb, o_ps, o_sb = (
        sem(n) for n in ("s_ps", "s_free", "s_max", "p_exp", "p_ready", "pT_ps", "pT_sb", "o_ps", "o_sb"))
    z_ps, z_ln, z_sp, a_ps, a_sb, w_sb, so_ps, so_sb = (
        sem(n) for n in ("z_ps", "z_ln", "z_sp", "a_ps", "a_sb", "w_sb", "so_ps", "so_sb"))
    dn_sq, dn_ps, dn_done, lam_sum, lam_exp = sem("dn_sq"), sem("dn_ps"), sem("dn_done"), sem("lam_sum"), sem("lam_exp")
    y_gated, y_squared, y_half = sem("y_gated"), sem("y_squared"), sem("y_half")
    x_new, out_done = sem("x_new"), sem("out_done")
    router_ps, router_sub, router_exp, router_mask, pos_ps, route_ready = (
        sem(n) for n in ("router_ps", "router_sub", "router_exp", "router_mask", "pos_ps", "route_ready"))

    class FfnSems:
        def __init__(self, name):
            self.x_hi, self.x_lo = ([sem(f"{name}_{n}{c}") for c in range(2)] for n in ("x_hi", "x_lo"))
            self.w_hi, self.w_lo, self.half_used = (sem(f"{name}_{n}") for n in ("w_hi", "w_lo", "half_used"))
            self.gu, self.silu, self.prod, self.hT_ps, self.h_hi, self.h_lo, self.down = (
                [sem(f"{name}_{n}{c}") for c in range(2)]
                for n in ("gu", "silu", "prod", "hT_ps", "h_hi", "h_lo", "down"))

    dense_s, moe_s = FfnSems("dense"), FfnSems("moe")
    fold_moved, fold_added = sem("fold_moved"), sem("fold_added")
    pick_ready, pick_g_ready, pick_gT_ps, pick_gT_sb = sem("pick_ready"), sem("pick_g_ready"), sem("pick_gT_ps"), sem("pick_gT_sb")
    gath_ps, ytok_dve, ytok_act = ([sem(f"{n}{c}") for c in range(2)] for n in ("gath_ps", "ytok_dve", "ytok_act"))
    x_tok_dve, x_tok_act, x_tok_dve1, x_tok_act1 = (sem(n) for n in ("x_tok_dve", "x_tok_act", "x_tok_dve1", "x_tok_act1"))
    x_tok_mul = [sem(f"x_tok_mul{c}") for c in range(2)]
    scat_ps, y_added = sem("scat_ps"), sem("y_added")

    class Chain:
        def __init__(self, eng, s):
            self.eng, self.s, self.n = eng, s, 0

        def mark(self, ins):
            self.n += 1
            return ins.then_inc(self.s, 1)

        def wait(self):
            self.eng.wait_ge(self.s, self.n)

        def link(self, ins):
            self.mark(ins)
            self.wait()

    class Unit:
        def __init__(self, n):
            self.n, self.slot = n, ring[n % RING]

        def wait(self, eng, more_uses=0):
            eng.wait_ge(landed[self.n % RING], 32 * (self.n // RING + 1) + 32 * more_uses)

    def with_second(eng, flag, work, skipped, narrow=None, narrow_only=None):
        if flag is None:
            work()
            return

        def skip():
            with eng.Else():
                for s in skipped + ([narrow_only] if narrow_only else []):
                    eng.sem_inc(s, 1)

        if narrow is None:
            with eng.If(flag > 0):
                work()
            skip()
            return
        with eng.If(flag > 1):
            work()
            if narrow_only:
                eng.sem_inc(narrow_only, 1)
        with eng.Else():
            with eng.If(flag > 0):
                narrow()
            skip()

    def bias_tiles(eng, v):
        src = bias_dram[v, 0, 0, :]
        for dst0, src0, n in ((0, P - 1, S), (S, 2 * P - 1, P)):
            skew = bass.AP(src.tensor, src.offset + src0, [[TRI - 1, P], [P * TRI, 8], [1, n]])
            eng.dma_start(bias[:, :, dst0:dst0 + n], skew).then_inc(bias_in, 16)

    rs_count = {"dve": 0, "act": 0, "wide": 0}

    def rsqrt_act(v, r):
        rs_count["act"] += 1
        nc.scalar.wait_ge(rs_var, rs_count["act"])
        nc.scalar.activation(r, v, ACT.Sqrt).then_inc(rs_estimate, 1)

    def wide_rsqrt_act(v, l, r, first):
        if first:
            rs_count["act"] += 1
            nc.scalar.wait_ge(rs_var, rs_count["act"])
            nc.scalar.activation(l, v, ACT.Ln).then_inc(rs_ln, 1)
        else:
            nc.scalar.wait_ge(rs_ln, rs_count["wide"] + 1)
            rs_count["wide"] += 1
            nc.scalar.activation(r, l, ACT.Exp, scale=-0.5).then_inc(rs_estimate, 1)

    def mean_dve(sums):
        rs_count["dve"] += 1
        for squares, n, mean in sums:
            last = nc.vector.tensor_scalar(mean, squares, 1.0 / n, EPS, ALU.mult, ALU.add)
        last.then_inc(rs_var, 1)

    def rsqrt_dve(dve, chain, v, t, r, wide=False):
        dve.wait_ge(rs_var, rs_count["dve"])
        dve.wait_ge(rs_estimate, rs_count["dve"])
        if not wide:
            chain.link(nc.vector.reciprocal(r, r))
        chain.link(nc.vector.tensor_tensor(t, r, r, ALU.mult))
        chain.link(nc.vector.tensor_tensor(t, t, v, ALU.mult))
        chain.link(nc.vector.tensor_scalar(t, t, -0.5, 1.5, ALU.mult, ALU.add))
        nc.vector.tensor_tensor(r, r, t, ALU.mult).then_inc(rs_done, 1)
        dve.wait_ge(rs_done, rs_count["dve"])

    EARLY_LOADS = [(k_ident[:], A["ident"]), (k_ones[:], A["ones"]), (ada_b_col[:], A["ada_b_cols"]), (pre_col[:], A["pre_cols"])]
    CONST_LOADS = []
    for name, dst in (("neg_suffix", k_neg_suffix), ("neg_ones", k_neg_ones),
                      ("before", k_before), ("causal", k_causal), ("strict", k_strict), ("strict01", k_strict01),
                      ("iota", k_iota), ("cos", k_cos), ("sin", k_sin), ("rot", k_rot), ("vec_cols", vec_g), ("router_cols", rw_sb)):
        CONST_LOADS.append((dst[:], A[name]))
    EARLY_LOADS += [
        (bias_hot, A["bias_hot"].rearrange("m b i -> b m i")),
        (bias_w[0:32, :], A["rel_bias"]), (bias_w[32:33, :], A["ones"][0:1, 0:8]),
    ]
    CONST_LOADS += [
        (rb_row[:], A["router_b"].partition_broadcast(P)),
    ]
    for i, name in enumerate(("diff_lq1", "diff_lk1", "diff_lq2", "diff_lk2")):
        CONST_LOADS.append((lam_in[:, i, :], A[name].partition_broadcast(P)))
    N_EARLY = 16 * len(EARLY_LOADS)
    N_CONSTS = 16 * len(CONST_LOADS)

    block = ctx.enter_context(nc.Block())

    w_in, wo_in = A["e_w_in"][0], A["o_w_in"][0]

    def cols(w, c0, n=UCOL):
        return w.rearrange("(k p) n -> p k n", p=P)[:, :, c0:c0 + n]

    @block.sync
    def _(sp):
        sp.dma_start(c_col[:], A["c_cols"]).then_inc(c_in, 16)

        def slot_free(n):
            old = n - RING
            if old < 0:
                return
            for lo, hi, s, before in ((0, EVEN_IN0, ada_unit_used, 0), (EVEN_IN0, GATE0, even_unit_used, 0),
                                      (GATE0, EVEN_UP0, ada_unit_used, ADA_UNITS), (EVEN_UP0, DENSE0, even_unit_used, 6),
                                      (ODD_IN0, MOE0, odd_unit_used, 0)):
                if lo <= old < hi:
                    sp.wait_ge(s, before + old - lo + 1)
            if DENSE0 <= old < ODD_IN0:
                sp.wait_ge(dense_s.w_lo, CREDIT + old - DENSE0 + 1)

        def load(n, src, k):
            slot_free(n)
            w = src.shape[-1]
            dst = ring[n % RING][:, 0:k * w].rearrange("p (k n) -> p k n", k=k)
            for a in (0, k // 2):
                b = a + k // 2
                sp.dma_start(dst[:, a:b, :], src[:, a:b, :]).then_inc(landed[n % RING], 16)

        def ada(n, u):
            g, kp = u // 4, u % 4
            src = A["ada_w"][0].rearrange("(k p) n -> p k n", p=P)[:, 2 * kp:2 * kp + 2, g * D:(g + 1) * D]
            load(n, src, 2)

        for u in range(ADA_UNITS):
            ada(u, u)
            if u == 2:
                sp.dma_start(x_sb[:], A["x"][0].rearrange("(c p) d -> p c d", p=P)).then_inc(x_in, 16)

        mla = cols(w_in, 0, MLA_IN)
        load(EVEN_IN0, mla[:, 0:4, :], 4)
        load(EVEN_IN0 + 1, mla[:, 4:8, :], 4)
        for i in range(4):
            load(EVEN_IN0 + 2 + i, cols(w_in, MLA_IN + i * UCOL), KT)
        for i in range(4):
            ada(GATE0 + i, ADA_UNITS + i)
        load(EVEN_UP0, A["e_w_uq"][0].rearrange("(k p) n -> p k n", p=P), 2)
        load(EVEN_UP0 + 1, A["e_w_ukv"][0].rearrange("p (k n) -> p k n", k=2), 2)
        for i in range(2):
            load(EVEN_UP0 + 2 + i, cols(w_in, MLA_IN + (4 + i) * UCOL), KT)
        sp.wait_ge(bias_sb, 1)
        for i in range(2):
            copies = bias_v[:, i, :].unsqueeze(1).to_broadcast([8, P, TRI])
            sp.dma_start(bias_dram[i], copies).then_inc(bias_out, 16)
        sp.wait_ge(bias_out, 32)
        bias_tiles(sp, 0)
        for i in range(4):
            load(EVEN_OUT0 + i, cols(A["e_w_out"][0], i * UCOL), KT)

        def ffn_loads(u0, nb, w_gate, w_up, w_down, lo_done, older, e=None):
            more = 0 if e is None else e * (3 * nb)
            gate = w_gate.rearrange("o (k p) f -> (o p) k f", p=P)
            up = w_up.rearrange("o (k p) f -> (o p) k f", p=P)
            down = w_down.rearrange("o (g k p) d -> (o p) g k d", p=P, k=2)

            def free(idx, it):
                sp.wait_ge(lo_done, more + it * 6 + (CREDIT + idx + 1 - RING))

            def gate_up(idx, b, half, it=0):
                r = ring[(u0 + idx) % RING][:].rearrange("p (k n) -> p k n", k=4)
                s = landed[(u0 + idx) % RING]
                c0 = b * FB
                k0 = 4 * half
                src_g, src_u = gate[:, k0:k0 + 4, bass.ds(c0, FB)], up[:, k0:k0 + 4, bass.ds(c0, FB)]
                free(idx, it)
                sp.dma_start(r[:, :, 0:FB], src_g).then_inc(s, 16)
                sp.dma_start(r[:, :, FB:2 * FB], src_u).then_inc(s, 16)

            def down_rows(idx, b, it=0):
                r = ring[(u0 + idx) % RING][:].rearrange("p (k n) -> p k n", k=2)
                s = landed[(u0 + idx) % RING]
                src = down[:, bass.ds(b, 1), :, :].rearrange("p o k d -> p (o k) d")
                free(idx, it)
                for k in range(2):
                    sp.dma_start(r[:, k:k + 1, :], src[:, k:k + 1, :]).then_inc(s, 16)

            def step(s, idx, it=0):
                gate_up(idx, s + 1, 0, it)
                gate_up(idx + 1, s + 1, 1, it)
                down_rows(idx + 2, s, it)

            older(1)
            gate_up(0, 0, 0)
            older(2)
            gate_up(1, 0, 1)
            older(6)
            step(0, 2)
            turns = (nb - 2) // 2
            with sp.Fori(0, turns) as it:
                step(2 * it + 1, 5, it)
                step(2 * it + 2, 8, it)
            for s in range(1 + 2 * turns, nb - 1):
                step(s, 2 + 3 * s)
            down_rows(3 * nb - 1, nb - 1)

        ffn_loads(DENSE0, DENSE_NB, A["ffn_w_gate"], A["ffn_w_up"], A["ffn_w_down"], dense_s.w_lo,
                  lambda i: sp.wait_ge(even_unit_used, 6 + DENSE0 - EVEN_UP0 - 6 + i))

        for i in range(12):
            load(ODD_IN0 + i, cols(wo_in, i * UCOL), KT)
        for i in range(4):
            load(ODD_OUT0 + i, cols(A["o_w_out"][0], i * UCOL), KT)

        with sp.Fori(0, NE) as e:
            ex = [A[n][0][bass.ds(e, 1)] for n in ("moe_w_gate", "moe_w_up", "moe_w_down")]
            ffn_loads(MOE0, MOE_NB, *ex, moe_s.w_lo, lambda i: sp.wait_ge(odd_unit_used, MOE0 - ODD_IN0 - 6 + i), e)

        for c in range(2):
            sp.wait_ge(x_new, 7 + c)
            sp.dma_start(out[0, c * P:(c + 1) * P, :], x_sb[:, c, :]).then_inc(out_done, 16)
        sp.wait_ge(out_done, 32)

    @block.gpsimd
    def _(pool):
        pool.wait_ge(c_ready, 1)
        ada_w_k = A["ada_w"].rearrange("m (k p) n -> m p k n", p=P)

        def sub_layer(m, i, by_act):
            for n in range(PIECES + 1):
                if n < PIECES:
                    g, k = n // KT, n % KT
                    src = ada_w_k[m, :, k:k + 1, g * D:(g + 1) * D].rearrange("m p k n -> (m p) (k n)")
                    if n >= 2:
                        pool.wait_ge(ada_bg_step, 2 * PIECES * i + 2 * (n - 1))
                    nc.gpsimd.dma_start(ada_w2[n % 2][:], src).then_inc(ada_bg_in[n % 2], 16)
                if n >= 1:
                    p = n - 1
                    g, k = p // KT, p % KT
                    acc = ada_bg[:, g * D:(g + 1) * D]
                    w = ada_w2[p % 2][:]
                    ck = c_silu[:, k:k + 1].to_broadcast([P, D])
                    done = 2 * PIECES * i + 2 * p
                    if p < by_act:
                        pool.wait_ge(ada_multiplied, p + 1)
                        if k == 0:
                            pool.sem_inc(ada_bg_step, 2)
                        else:
                            nc.gpsimd.tensor_tensor(acc, acc, w, ALU.add).then_inc(ada_bg_step, 2)
                    else:
                        pool.wait_ge(ada_bg_in[p % 2], 8 * PIECES * i + 16 * (p // 2 + 1))
                        if k == 0:
                            nc.gpsimd.tensor_tensor(acc, w, ck, ALU.mult).then_inc(ada_bg_step, 2)
                        else:
                            nc.gpsimd.tensor_tensor(w, w, ck, ALU.mult).then_inc(ada_bg_step, 1)
                            pool.wait_ge(ada_bg_step, done + 1)
                            nc.gpsimd.tensor_tensor(acc, acc, w, ALU.add).then_inc(ada_bg_step, 1)
                    pool.wait_ge(ada_bg_step, done + 2)
            pool.sem_inc(ada_bg_ready, 1)

        pool.wait_ge(mod_used, 1)
        sub_layer(slice(1, 2), 0, ACT_PIECES)
        with pool.Fori(0, 2) as i:
            pool.wait_ge(mod_used, i + 2)
            sub_layer(bass.ds(i + 2, 1), i + 1, 0)

    @block.tensor
    def _(pe):
        mm = nc.tensor.matmul
        for f in (dense_s, moe_s):
            for s in (f.half_used, *f.gu, *f.hT_ps, *f.down):
                pe.sem_inc(s, CREDIT)
        for s in (pick_gT_ps, scat_ps, *gath_ps):
            pe.sem_inc(s, CREDIT)

        def shift_scale(m):
            if m > 0:
                pe.wait_ge(ada_bg_ready, m)
            acc = ada_fg if m == 0 else ada_bg
            for j in range(16):
                if m == 0 and j % KT == 0:
                    pe.wait_ge(ada_fg_ready, j // KT + 1)
                last = mm(ps[:, MOD_BANK[m], j:j + 1], acc[:, j * P:(j + 1) * P], k_ones[:, 0:1], start=True, stop=True)
            last.then_inc(mod_ps, 1)
            if m == 0:
                pe.sem_inc(mod_used, 1)

        def gate(m):
            acc = ada_fg if m == 0 else ada_bg
            if m == 0:
                pe.wait_ge(ada_fg_ready, 3)
            for n in range(2):
                last = mm(ps[:, GATE_BANK[m] + n, :], k_ones[:], acc[:, 2 * D + n * 512:2 * D + (n + 1) * 512], start=True, stop=True)
            last.then_inc(gate_ps, 1)
            if m > 0:
                pe.wait_ge(gate_ps, m + 1)
                pe.sem_inc(mod_used, 1)

        def modulation(m):
            shift_scale(m)
            gate(m)

        def transposes(m):
            pe.wait_ge(xn_dve, m + 1)
            pe.wait_ge(xn_act, m + 1)
            for j in range(KT):
                for c in range(2):
                    o = (j % 2) * S + c * P
                    last = nc.tensor.transpose(ps[:, XT_BANK[m] + j // 2, o:o + P], xn[:, c, j * P:(j + 1) * P], k_ident[:])
            last.then_inc(xT_ps, 1)

        def wait_hT(m):
            pe.wait_ge(hT_dve, m + 1)
            pe.wait_ge(hT_act, m + 1)

        def unit(n, k):
            u = Unit(n)
            u.wait(pe)
            return u.slot[:].rearrange("p (k n) -> p k n", k=k)

        def features(n, bank):
            w = unit(n, KT)
            for i in range(2):
                for k in range(KT):
                    last = mm(ps[:, bank, i * S:(i + 1) * S], w[:, k, i * P:(i + 1) * P], hT[:, k, :],
                              start=(k == 0), stop=(k == KT - 1))
            return last

        def tokens(n, bank, lhs):
            w = unit(n, KT)
            for c in range(2):
                for k in range(KT):
                    last = mm(ps[:, bank, c * UCOL:(c + 1) * UCOL], lhs[:, k, c * P:(c + 1) * P], w[:, k, :],
                              start=(k == 0), stop=(k == KT - 1))
            return last

        pe.wait_ge(early_in, N_EARLY)
        for v in range(2):
            last = mm(ps[0:8, 1 + v, 0:TRI], bias_w[:], bias_hot[:, v, :], start=True, stop=True)
        last.then_inc(bias_ps, 1)
        transposes(0)
        shift_scale(0)
        pe.wait_ge(bias_sb, 1)
        wait_hT(0)
        pe.wait_ge(consts_in, N_CONSTS)

        for h in range(2):
            w = Unit(EVEN_IN0 + h)
            w.wait(pe)
            wv = w.slot[:, 0:4 * MLA_IN].rearrange("p (k n) -> p k n", k=4)
            for k in range(4):
                kt = 4 * h + k
                for i in range(3):
                    mm(ps[:, i, 0:S], wv[:, k, i * P:(i + 1) * P], hT[:, kt, :], start=(kt == 0), stop=(kt == KT - 1))
                last = mm(ps[NOPE:QK, 3, 0:S], wv[:, k, 3 * P:3 * P + ROPE], hT[:, kt, :], start=(kt == 0), stop=(kt == KT - 1))
            last.then_inc(even_unit_used, 1)
        for i in range(4):
            if i == 2:
                pe.wait_ge(lat_act, 1)
                mm(ps[:, 2, 0:S], k_ones[:], lat_sq[:, 0, :], start=True, stop=False)
                mm(ps[:, 2, 0:S], k_ones[:], lat_sq[:, 1, :], start=False, stop=True)
                mm(ps[:, 2, S:2 * S], k_ones[:], lat_sq[:, 2, :], start=True, stop=True).then_inc(lat_ps, 1)
            features(EVEN_IN0 + 2 + i, 4 + i).then_inc(even_unit_used, 1)
        wq = Unit(EVEN_UP0)
        wq.wait(pe)
        wqv = wq.slot[:, 0:2 * MLA_H * QK].rearrange("p (k n) -> p k n", k=2)
        pe.wait_ge(lat_ready, 1)
        pe.wait_ge(proj_dve, 2)
        pe.wait_ge(proj_act, 2)
        for h in range(MLA_H):
            for k in range(2):
                last = mm(ps[0:QK, 4 + h // 2, (h % 2) * S:(h % 2 + 1) * S], wqv[:, k, h * QK:(h + 1) * QK], latT[:, k, :],
                          start=(k == 0), stop=(k == 1))
        last.then_inc(even_unit_used, 1)
        wkv = Unit(EVEN_UP0 + 1)
        wkv.wait(pe)
        wkvv = wkv.slot[:, 0:MLA_H * 2 * HD].rearrange("p (h n) -> p h n", h=MLA_H)
        for h in range(MLA_H):
            last = mm(ps[0:NOPE, h // 2, (h % 2) * S:(h % 2 + 1) * S], wkvv[:, h, 0:NOPE], latT[:, 2, :], start=True, stop=True)
        last.then_inc(knope_ps, 1)
        pe.wait_ge(proj_dve, 4)
        pe.wait_ge(proj_act, 4)
        for i in range(4):
            mm(ps[NOPE:QK, 4 + i, :], k_rot[NOPE:QK, :], qT[NOPE:QK, 2 * i:2 * i + 2, :], start=True, stop=True)
        mm(ps[NOPE:QK, 0, 0:S], k_rot[NOPE:QK, :], latT[NOPE:QK, 3, :], start=True, stop=True).then_inc(rot_ps, 1)
        for c in range(2):
            last = mm(ps[:, 1 + c, :], latT[:, 2, c * P:(c + 1) * P], wkvv[:, :, NOPE:2 * HD], start=True, stop=True)
        last.then_inc(even_unit_used, 1)
        tokens(EVEN_UP0 + 2, 3, hT).then_inc(even_unit_used, 1)
        pe.wait_ge(proj_dve, 5)
        tokens(EVEN_UP0 + 3, 1, hT).then_inc(even_unit_used, 1)

        def softmax_head(i, maps, n_maps):
            b0 = (i % 2) * n_maps
            if i >= first_head[0] + 2:
                pe.wait_ge(s_free, i - 1)
            for m, (q, k) in enumerate(maps):
                mm(ps[:, b0 + m, 0:S], q[:, P:S], k[:, 0:S], start=True, stop=True)
                last = mm(ps[:, b0 + m, S:TRI], q[:, 0:P], k[:, 0:P], start=True, stop=True)
            last.then_inc(s_ps, 1)

        def transpose_head(i, bank):
            pe.wait_ge(p_ready, i + 1)
            if i >= first_head[0] + 2:
                pe.wait_ge(pT_sb, i - 1)
            p = pr[:, i % 2, 0, :]
            for src, dst in ((0, P), (P, S), (S, 0)):
                last = nc.tensor.transpose(ps[:, bank + i % 2, dst:dst + P], p[:, src:src + P], k_ident[:])
            last.then_inc(pT_ps, 1)

        def values(i, bank, rows, v, signal=True):
            pe.wait_ge(pT_sb, i + 1)
            if i >= first_head[0] + 2:
                pe.wait_ge(o_sb, i - 1)
            o = ps[rows, bank + i % 2, :]
            mm(o[:, 0:S], v[:, 0, :], pt[:, i % 2, 0:S], start=True, stop=False)
            mm(o[:, P:S], v[:, 1, :], pt[:, i % 2, S:TRI], start=False, stop=True).then_inc(o_ps, 1)

        first_head = [0]
        pe.wait_ge(proj_dve, 6)
        pe.wait_ge(proj_act, 6)
        pe.wait_ge(rope_ready, 1)

        def even_maps(i):
            if i < DIL_H:
                r = slice(64 * (i % 2), 64 * (i % 2) + HD)
                return [(qT2[r, i // 2, :], kT2[r, i // 2, :])]
            return [(qT[0:QK, i - DIL_H, :], kT[0:QK, i - DIL_H, :])]

        H0 = DIL_H + MLA_H
        for i in range(H0 + 3):
            if i < H0:
                softmax_head(i, even_maps(i), 1)
            if 2 <= i < H0 + 2:
                transpose_head(i - 2, 2)
            if i >= 3:
                h = i - 3
                v = v2 if h < DIL_H else v1
                values(h, 4, slice(64 * (h % 2), 64 * (h % 2) + HD), v[:, :, (h % 8) * HD:(h % 8 + 1) * HD])

        def out_projection(u0, used):
            for n in range(4):
                tokens(u0 + n, n, oT).then_inc(used, 1)
        gate(0)
        pe.wait_ge(o_sb, H0)
        out_projection(EVEN_OUT0, even_unit_used)
        shift_scale(1)
        transposes(1)
        pe.wait_ge(gate_sb, 1)
        gate(1)

        def ffn(f, u0, nb, flag=None, e=None, between=None, y_free=None, fetch_next=None, fetched=None):
            blk0 = 0 if e is None else e * nb
            un0 = 0 if e is None else e * (3 * nb)

            def w_ready(un):
                pe.wait_ge(f.w_hi, un + (CREDIT + 1))
                pe.wait_ge(f.w_lo, un + (CREDIT + 1))

            def gate_up(un, blk):
                def chunk(c):
                    pe.wait_ge(f.prod[c], blk + CREDIT)
                    for k in range(KT):
                        t = k // 4
                        if k % 4 == 0:
                            w_ready(un + t)
                        wh = w_hi[t][:, (k % 4) * 512:(k % 4 + 1) * 512]
                        wl = w_lo[t][:, (k % 4) * 512:(k % 4 + 1) * 512]
                        xh, xl = x_hi[:, k, c * P:(c + 1) * P], x_lo[:, k, c * P:(c + 1) * P]
                        mm(ps[:, c, :], xh, wh, start=(k == 0), stop=False)
                        mm(ps[:, c, :], xl, wh, start=False, stop=False)
                        last = mm(ps[:, c, :], xh, wl, start=False, stop=(k == KT - 1))
                        if c == 0 and k == 3:
                            last.then_inc(f.half_used, 1)
                    return last

                def narrow():
                    pe.wait_ge(f.prod[1], blk + CREDIT)
                    for k in range(KT):
                        t = k // 4
                        if k % 4 == 0:
                            w_ready(un + t)
                        w = slice((k % 4) * 512, (k % 4 + 1) * 512)

                        def hi(start, stop):
                            return mm(ps[:, 1, :], x_hi[:, k, P:S], w_hi[t][:, w], start=start, stop=stop, skip_group_check=True)

                        def lo():
                            mm(ps[0:NARROW, 1, :], x_hi[:, k, P:P + NARROW], w_lo[t][:, w], start=False, stop=False, skip_group_check=True)

                        if k == 0:
                            hi(True, False)
                            lo()
                        else:
                            lo()
                            last = hi(False, k == KT - 1)
                    last.then_inc(f.gu[1], 1)
                with_second(pe, flag, lambda: chunk(1).then_inc(f.gu[1], 1), [f.gu[1]], narrow)
                chunk(0).then_inc(f.gu[0], 1)

            def hidden_T(blk):
                def chunk(c):
                    pe.wait_ge(f.prod[c], blk + (CREDIT + 1))
                    pe.wait_ge(f.h_lo[c], blk + CREDIT)
                    for i in range(2):
                        last = nc.tensor.transpose(ps[:, 2 + c, i * P:(i + 1) * P], prod[:, c, i * P:(i + 1) * P], k_ident[:])
                    last.then_inc(f.hT_ps[c], 1)
                with_second(pe, flag, lambda: chunk(1), [f.hT_ps[1]])
                chunk(0)

            def down(un, blk, first=False, final=False):
                if first and y_free:
                    y_free()
                def chunk(c):
                    pe.wait_ge(f.h_hi[c], blk + (CREDIT + 1))
                    pe.wait_ge(f.h_lo[c], blk + (CREDIT + 1))
                    w_ready(un)
                    for i in range(2):
                        hh, hl = h_hi[:, c, i * P:(i + 1) * P], h_lo[:, c, i * P:(i + 1) * P]
                        for n in range(2):
                            o = ps[:, 4 + 2 * c + n, :]
                            wh = w_hi[2][:, i * D + n * 512:i * D + (n + 1) * 512]
                            wl = w_lo[2][:, i * D + n * 512:i * D + (n + 1) * 512]
                            mm(o, hh, wh, start=(first and i == 0), stop=False, skip_group_check=True)
                            mm(o, hl, wh, start=False, stop=False, skip_group_check=True)
                            last = mm(o, hh, wl, start=False, stop=(final and i == 1), skip_group_check=True)
                    return last

                def narrow():
                    pe.wait_ge(f.h_hi[1], blk + (CREDIT + 1))
                    pe.wait_ge(f.h_lo[1], blk + (CREDIT + 1))
                    w_ready(un)
                    for i in range(2):
                        for n in range(2):
                            w = slice(i * D + n * 512, i * D + (n + 1) * 512)

                            def hi(start, stop):
                                return mm(ps[:, 6 + n, :], h_hi[:, 1, i * P:(i + 1) * P], w_hi[2][:, w], start=start, stop=stop,
                                          skip_group_check=True)

                            def lo():
                                mm(ps[0:NARROW, 6 + n, :], h_hi[:, 1, i * P:i * P + NARROW], w_lo[2][:, w], start=False, stop=False,
                                   skip_group_check=True)

                            if i == 0:
                                hi(first, False)
                                lo()
                            else:
                                lo()
                                last = hi(False, final)
                    last.then_inc(f.down[1], 1)
                with_second(pe, flag, lambda: chunk(1).then_inc(f.down[1], 1), [f.down[1]], narrow)
                chunk(0).then_inc(f.down[0], 1)

            def step(s, idx, it=0, first=False):
                gate_up(un0 + 6 * it + idx, blk0 + s + 1)
                down(un0 + 6 * it + idx + 2, blk0 + s, first)
                hidden_T(blk0 + s + 1)

            gate_up(un0, blk0)
            if between:
                between()
            hidden_T(blk0)
            step(0, 2, first=True)
            turns = (nb - 3) // 2
            with pe.Fori(0, turns) as it:
                step(2 * it + 1, 5, it)
                step(2 * it + 2, 8, it)
            for s in range(1 + 2 * turns, nb - 2):
                step(s, 2 + 3 * s)
            s = nb - 2
            if fetch_next:
                fetch_next()
                down(un0 + 3 * s + 4, blk0 + s)
                fetched()
                gate_up(un0 + 3 * s + 2, blk0 + s + 1)
            else:
                gate_up(un0 + 3 * s + 2, blk0 + s + 1)
                down(un0 + 3 * s + 4, blk0 + s)
            hidden_T(blk0 + s + 1)
            down(un0 + 3 * nb - 1, blk0 + nb - 1, final=True)

        pe.wait_ge(dense_s.x_hi[0], CREDIT + 1)
        pe.wait_ge(dense_s.x_lo[0], CREDIT + 1)
        ffn(dense_s, DENSE0, DENSE_NB, y_free=lambda: pe.wait_ge(gate_sb, 2))
        modulation(2)
        transposes(2)
        wait_hT(2)

        for i in range(12):
            bank = i % 8
            if i == 2:
                pe.wait_ge(gate_sb, 3)
            if i >= 8:
                pe.wait_ge(proj_dve, 6 + (i - 8) // 2 + 1)
                pe.wait_ge(proj_act, 6 + (i - 8) // 2 + 1)
            (tokens(ODD_IN0 + i, bank, hT) if i in (4, 5, 10, 11) else features(ODD_IN0 + i, bank)).then_inc(odd_unit_used, 1)
        pe.wait_ge(proj_dve, 12)
        pe.wait_ge(proj_act, 12)

        first_head[0] = H0
        for j in range(DIFF_H + 3):
            i = H0 + j
            if j < DIFF_H:
                softmax_head(i, [(qT[64 * m:64 * m + HD, j, :], kT[64 * m:64 * m + HD, j, :]) for m in range(2)], 2)
            if 2 <= j < DIFF_H + 2:
                transpose_head(i - 2, 4)
            if j >= 3:
                values(i - 3, 6, slice(0, P), v1[:, :, (j - 3) * P:(j - 2) * P])

        def sb_qk(h):
            r = slice(64 * (h % 2), 64 * (h % 2) + HD)
            return qT2[r, h // 2, :], kT2[r, h // 2, :]

        for p in range(PAIRS + 2):
            if p < PAIRS:
                if p == 1:
                    pe.wait_ge(rs_var, DN_NORM)
                if p >= 2:
                    pe.wait_ge(z_sp, p - 1)
                for i in range(2):
                    q, k = sb_qk(2 * p + i)
                    z = ps[:, 4 * (p % 2) + i, :]
                    mm(z[:, 0:S], k[:, 0:P], q[:, 0:S], start=True, stop=True)
                    last = mm(z[:, S:TRI], k[:, P:S], q[:, P:S], start=True, stop=True)
                last.then_inc(z_ps, 1)
            if p == 0:
                pe.wait_ge(dn_sq, DIFF_H)
                for i in range(2):
                    last = mm(ps[:, 4 + i, :], k_ones[:], lat_sq[:, 2 * i:2 * i + 2, :], start=True, stop=True)
                last.then_inc(dn_ps, 1)
            if 1 <= p <= PAIRS:
                if p >= 2:
                    pe.wait_ge(a_sb, p - 1)
                pe.wait_ge(z_sp, p)
                for i in range(2):
                    q, k = sb_qk(2 * (p - 1) + i)
                    softplus, o = sc[:, (p - 1) % 2, i, :], ps[:, 2 + i, :]
                    mm(o[:, 0:S], k[:, 0:P], q[:, 0:S], start=True, stop=False)
                    mm(o[:, 0:S], k_neg_suffix[:], softplus[:, 0:S], start=False, stop=False)
                    mm(o[:, P:S], k_neg_ones[:], softplus[:, S:TRI], start=False, stop=True)
                    mm(o[:, S:TRI], k[:, P:S], q[:, P:S], start=True, stop=False)
                    last = mm(o[:, S:TRI], k_neg_suffix[:], softplus[:, S:TRI], start=False, stop=True)
                last.then_inc(a_ps, 1)
            if p >= 2:
                pe.wait_ge(w_sb, p - 1)
                if p >= 3:
                    pe.wait_ge(so_sb, p - 2)
                for i in range(2):
                    h = 2 * (p - 2) + i
                    o = ps[64 * i:64 * i + HD, 6 + i, :]
                    w, v = pr[:, p % 2, i, :], v2[:, :, h * HD:(h + 1) * HD]
                    mm(o[:, 0:S], v[:, 0, :], w[:, 0:S], start=True, stop=False)
                    last = mm(o[:, P:S], v[:, 1, :], w[:, S:TRI], start=False, stop=True)
                last.then_inc(so_ps, 1)

        pe.wait_ge(so_sb, PAIRS)
        pe.wait_ge(dn_done, 1)
        out_projection(ODD_OUT0, odd_unit_used)
        modulation(3)
        transposes(3)
        wait_hT(3)

        for c in range(2):
            for k in range(KT):
                last = mm(ps[:, 0, c * NE:(c + 1) * NE], hT[:, k, c * P:(c + 1) * P], rw_sb[:, k, :], start=(k == 0), stop=(k == KT - 1))
        last.then_inc(router_ps, 1)
        pe.wait_ge(router_mask, 1)
        mm(ps[:, 1, 0:NE], k_before[:], r_mask[:, 0, :], start=True, stop=True)
        mm(ps[:, 1, NE:2 * NE], k_ones[:], r_mask[:, 0, :], start=True, stop=False)
        mm(ps[:, 1, NE:2 * NE], k_before[:], r_mask[:, 1, :], start=False, stop=True)
        mm(ps[:, 1, 2 * NE:3 * NE], k_ones[:], r_mask[:, 0, :], start=True, stop=False)
        mm(ps[:, 1, 2 * NE:3 * NE], k_ones[:], r_mask[:, 1, :], start=False, stop=True).then_inc(pos_ps, 1)

        pe.wait_ge(gate_sb, 4)

        def gather(s):
            for j in range(KT):
                for c in range(2):
                    last = mm(ps[:, j // 4, (j % 4) * P:(j % 4 + 1) * P], xn[:, c, j * P:(j + 1) * P],
                              pick[:, c, s * P:(s + 1) * P], start=(c == 0), stop=(c == 1))
            last.then_inc(gath_ps[s], 1)

        def gather_second(flag, n):
            def work():
                pe.wait_ge(x_tok_dve, n + 1)
                pe.wait_ge(x_tok_act, n + 1)
                gather(1)
            with_second(pe, flag, work, [gath_ps[1]])

        def pick_gates_T(n):
            pe.wait_ge(pick_g_ready, n + 1)
            for s in range(2):
                for c in range(2):
                    last = nc.tensor.transpose(ps[:, 2, s * S + c * P:s * S + (c + 1) * P], pick_g[:, c, s * P:(s + 1) * P], k_ident[:])
            last.then_inc(pick_gT_ps, 1)

        def scatter(flag, n):
            pe.wait_ge(pick_gT_sb, n + 1)
            for s in (ytok_dve[0], ytok_act[0]):
                pe.wait_ge(s, n + (CREDIT + 1))

            def out(chunks):
                for c in range(2):
                    for half in range(2):
                        for s in chunks:
                            last = mm(ps[:, 4 + 2 * c + half, :], pick_gT[:, s, c * P:(c + 1) * P],
                                      y_tok[:, s, half * 512:(half + 1) * 512], start=(s == chunks[0]), stop=(s == chunks[-1]))
                last.then_inc(scat_ps, 1)

            with pe.If(flag > 0):
                for s in (ytok_dve[1], ytok_act[1]):
                    pe.wait_ge(s, n + (CREDIT + 1))
                out([0, 1])
            with pe.Else():
                out([0])

        def flag_at(i):
            return pe.value_load(second[0:1, i], min_val=0, max_val=2)

        pe.wait_ge(route_ready, 1)
        pe.wait_ge(pick_ready, 1)
        gather(0)
        gather_second(flag_at(slice(1, 2)), 0)
        with pe.Fori(0, NE) as e:
            last_flag, flag, next_flag = (flag_at(bass.ds(e + i, 1)) for i in range(3))
            pe.wait_ge(moe_s.h_lo[0], e * MOE_NB + CREDIT)
            pick_gates_T(e)
            for s in (moe_s.x_hi[0], moe_s.x_lo[0], moe_s.x_hi[1], moe_s.x_lo[1]):
                pe.wait_ge(s, e + (CREDIT + 1))

            def fetch_next():
                pe.wait_ge(pick_ready, e + 2)
                gather(0)

            def fetched():
                pe.wait_ge(x_tok_dve, e + 2)
                pe.wait_ge(x_tok_act, e + 2)

            ffn(moe_s, MOE0, MOE_NB, flag, e, between=lambda: scatter(last_flag, e),
                y_free=lambda: pe.wait_ge(y_added, e + 2), fetch_next=fetch_next, fetched=fetched)
            gather_second(next_flag, e + 1)
        pe.wait_ge(moe_s.h_lo[0], NE * MOE_NB + CREDIT)
        pick_gates_T(NE)
        scatter(flag_at(slice(NE, NE + 1)), NE)

    @block.scalar
    def _(act):
        chain = Chain(act, act_chain)
        do = nc.scalar.activation
        for f in (dense_s, moe_s):
            for s in (f.w_hi, *f.silu, *f.h_hi, *f.x_hi):
                act.sem_inc(s, CREDIT)
        for s in (*ytok_act, fold_moved):
            act.sem_inc(s, CREDIT)

        for dst, src in EARLY_LOADS:
            act.dma_start(dst, src).then_inc(early_in, 16)

        def load_rows(m):
            act.dma_start(gate_row[:], A["ada_b"][m:m + 1, 2 * D:3 * D].partition_broadcast(P)).then_inc(rows_in, 16)
            act.dma_start(post_row[:], A["post_g"][m:m + 1, :].partition_broadcast(P)).then_inc(rows_in, 16)

        def sqrt_table():
            do(table[:], k_ones[:, 0:1], ACT.Sqrt)

        def prenorm(m):
            for c in range(2):
                if m > 0:
                    act.wait_ge(x_new, 2 * (m - 1) + c + 1)
                last = do(xn[:, c, :], x_sb[:, c, :], ACT.Square, accum_out=ssq[:, c:c + 1])
            last.then_inc(ssq_ready, 1)
            rsqrt_act(rs_v[:], rs_r[:])
            act.wait_ge(rs_done, rs_count["act"])
            do(xn[:, 1, :], x_sb[:, 1, :], ACT.Copy, scale=rs_r[:, 1:2]).then_inc(xn_act, 1)

        def modulated(m):
            act.wait_ge(xT_ps, m + 1)
            act.wait_ge(mod_ready, m + 1)
            for j in (2, 3, 6, 7):
                last = do(hT[:, j, :], ps[:, XT_BANK[m] + j // 2, (j % 2) * S:(j % 2 + 1) * S], ACT.Identity,
                          scale=mod_scale[:, m, j:j + 1], bias=mod_shift[:, m, j:j + 1])
            last.then_inc(hT_act, 1)

        def multiply_pieces(a, b):
            for n in range(a, b):
                g, k = n // KT, n % KT
                act.wait_ge(ada_bg_in[n % 2], 16 * (n // 2 + 1))
                w = ada_w2[n % 2][:]
                do(ada_bg[:, g * D:(g + 1) * D] if k == 0 else w, w, ACT.Copy, scale=c_silu[:, k:k + 1]).then_inc(ada_multiplied, 1)

        act.wait_ge(c_in, 16)
        do(c_silu[:], c_col[:], ACT.Silu).then_inc(c_ready, 1)
        for dst, src in CONST_LOADS:
            act.dma_start(dst, src).then_inc(consts_in, 16)
        act.wait_ge(x_in, 16)
        prenorm(0)
        act.wait_ge(bias_ps, 1)
        do(bias_v, ps[0:8, 1:3, 0:TRI], ACT.Copy).then_inc(bias_sb, 1)
        modulated(0)
        load_rows(0)
        multiply_pieces(0, 4)

        act.wait_ge(even_unit_used, 2)
        for i in range(3):
            do(latT[:, i, :], ps[:, i, 0:S], ACT.Copy)
            last = do(lat_sq[:, i, :], ps[:, i, 0:S], ACT.Square)
        last.then_inc(lat_act, 1)
        multiply_pieces(4, 7)
        act.wait_ge(even_unit_used, 4)
        do(qT2[:, 2:4, :], ps[:, 5, :], ACT.Copy).then_inc(proj_act, 1)
        for first in (True, False):
            wide_rsqrt_act(lat_v[:, 0:2, :], lat_t[:, 2:4, :], lat_r[:, 0:2, :], first)
        multiply_pieces(7, 10)
        act.wait_ge(even_unit_used, 6)
        do(kT2[:, 2:4, :], ps[:, 7, :], ACT.Copy).then_inc(proj_act, 1)
        multiply_pieces(10, 12)
        act.wait_ge(even_unit_used, 7)
        do(qT[0:QK, 4:8, :], ps[0:QK, 6:8, :], ACT.Copy).then_inc(proj_act, 1)
        act.wait_ge(knope_ps, 1)
        do(kT[0:NOPE, 4:8, :], ps[0:NOPE, 2:4, :], ACT.Copy).then_inc(proj_act, 1)
        act.wait_ge(even_unit_used, 8)
        do(v1[:, 1, :], ps[:, 2, :], ACT.Copy).then_inc(proj_act, 1)
        multiply_pieces(12, ACT_PIECES)
        act.wait_ge(even_unit_used, 10)
        do(v2[:, :, S:2 * S], ps[:, 1, :], ACT.Copy).then_inc(proj_act, 1)

        SEG = ((0, S), (S, TRI))

        def exps(i, maps):
            act.wait_ge(s_max, i + 1)
            if i >= 2:
                act.wait_ge(pT_ps, i - 1)
            for m in range(maps):
                for g, (a, b) in enumerate(SEG):
                    last = do(pr[:, i % 2, m, a:b], sc[:, i % 2, m, a:b], ACT.Exp, bias=nmax[:, i % 2, m, g:g + 1],
                              accum_out=den[:, i % 2, m, g:g + 1])
            last.then_inc(p_exp, 1)

        def pT_copy(i, bank):
            act.wait_ge(pT_ps, i + 1)
            do(pt[:, i % 2, :], ps[:, bank + i % 2, 0:TRI], ACT.Copy).then_inc(pT_sb, 1)

        H0 = DIL_H + MLA_H
        for i in range(H0 + 3):
            if i < H0:
                exps(i, 1)
            if 2 <= i < H0 + 2:
                pT_copy(i - 2, 2)
            if i >= 3:
                h = i - 3
                act.wait_ge(o_ps, h + 1)
                rows = slice(64 * (h % 2), 64 * (h % 2) + HD)
                chunk = 4 + h // 2 if h < DIL_H else (h - DIL_H) // 2
                do(oT[rows, chunk, :], ps[rows, 4 + h % 2, 0:S], ACT.Copy).then_inc(o_sb, 1)

        def out_squares(used, n0, after=None):
            sqrt_table()
            for n in range(4):
                act.wait_ge(used, n0 + n + 1)
                for c in range(2):
                    last = do(xn[:, c, n * UCOL:(n + 1) * UCOL], ps[:, n, c * UCOL:(c + 1) * UCOL], ACT.Square,
                              accum_out=y_ssq[:, c, n:n + 1])
                last.then_inc(y_squared, 1)
                if after:
                    after(n)
            rsqrt_act(rs_v[:], rs_r[:])

        def next_input(m):
            act.wait_ge(y_gated, m)
            load_rows(m)
            prenorm(m)
            modulated(m)


        def ffn(f, u0, nb, flag=None, e=None, between=None, fetch_next=None):
            blk0 = 0 if e is None else e * nb
            uses = 0 if e is None else e * (3 * nb // RING)

            def hi(t, idx, blk, it=0):
                Unit(u0 + idx).wait(act, uses + it)
                act.wait_ge((f.half_used, f.gu[0], f.down[0])[t], blk + CREDIT)
                do(w_hi[t][:], ring[(u0 + idx) % RING][:], ACT.Copy).then_inc(f.w_hi, 1)

            def silu(blk):
                def chunk(c):
                    act.wait_ge(f.gu[c], blk + (CREDIT + 1))
                    act.wait_ge(f.prod[c], blk + CREDIT)
                    do(g_silu[:, c, :], ps[:, c, 0:FB], ACT.Silu).then_inc(f.silu[c], 1)

                def narrow():
                    act.wait_ge(f.gu[1], blk + (CREDIT + 1))
                    act.wait_ge(f.prod[1], blk + CREDIT)
                    do(folded[:], ps[NARROW:P, 1, :], ACT.Copy).then_inc(fold_moved, 1)
                    act.wait_ge(fold_added, blk + (CREDIT + 1))
                    do(g_silu[0:NARROW, 1, :], folded[:, 0:FB], ACT.Silu).then_inc(f.silu[1], 1)
                with_second(act, flag, lambda: chunk(1), [f.silu[1]], narrow, fold_moved)
                chunk(0)

            def hidden(blk):
                def chunk(c):
                    act.wait_ge(f.hT_ps[c], blk + (CREDIT + 1))
                    act.wait_ge(f.down[c], blk + CREDIT)
                    do(h_hi[:, c, :], ps[:, 2 + c, 0:FB], ACT.Copy).then_inc(f.h_hi[c], 1)

                def narrow():
                    act.wait_ge(f.hT_ps[1], blk + (CREDIT + 1))
                    act.wait_ge(f.down[1], blk + CREDIT)
                    parts = h_hi[:, 1, :].rearrange("p (i n) -> p i n", i=2)
                    src = ps[:, 3, 0:FB].rearrange("p (i n) -> p i n", i=2)
                    do(parts[:, :, 0:NARROW], src[:, :, 0:NARROW], ACT.Copy).then_inc(f.h_hi[1], 1)
                with_second(act, flag, lambda: chunk(1), [f.h_hi[1]], narrow)
                chunk(0)

            def step(s, idx, it=0):
                hi(0, idx, blk0 + s + 1, it)
                silu(blk0 + s)
                hi(1, idx + 1, blk0 + s + 1, it)
                hidden(blk0 + s)
                hi(2, idx + 2, blk0 + s, it)

            if e is not None:
                hi(0, 0, blk0)
                hi(1, 1, blk0)
            if between:
                flag = between()
            step(0, 2)
            turns = (nb - 2) // 2
            with act.Fori(0, turns) as it:
                step(2 * it + 1, 5, it)
                step(2 * it + 2, 8, it)
            for s in range(1 + 2 * turns, nb - 1):
                step(s, 2 + 3 * s)
            if fetch_next:
                fetch_next()
            hi(2, 3 * nb - 1, blk0 + nb - 1)
            silu(blk0 + nb - 1)
            hidden(blk0 + nb - 1)

        def first_weights(n):
            if n < 2:
                Unit(DENSE0 + n).wait(act)
                do(w_hi[n][:], ring[(DENSE0 + n) % RING][:], ACT.Copy).then_inc(dense_s.w_hi, 1)

        out_squares(even_unit_used, 10, first_weights)
        next_input(1)
        act.wait_ge(hT_dve, 2)
        act.wait_ge(hT_act, 2)
        do(x_hi[:], hT[:], ACT.Copy).then_inc(dense_s.x_hi[0], 1)
        ffn(dense_s, DENSE0, DENSE_NB)
        sqrt_table()
        act.wait_ge(dense_s.down[0], CREDIT + DENSE_NB)
        act.wait_ge(dense_s.down[1], CREDIT + DENSE_NB)
        do(xn[:, 0, :], ps[:, 4:6, :], ACT.Square, accum_out=ssq[:, 0:1]).then_inc(y_squared, 1)
        act.wait_ge(y_half, 1)
        do(xn[:, 1, :], ps[:, 6:8, :], ACT.Square, accum_out=ssq[:, 1:2]).then_inc(ssq_ready, 1)
        rsqrt_act(rs_v[:], rs_r[:])
        bias_tiles(act, 1)
        next_input(2)

        for i in range(1, 12, 2):
            act.wait_ge(odd_unit_used, i + 1)
            bank = ps[:, i % 8, :]
            if i in (5, 11):
                do((v1 if i == 5 else v2)[:, :, S:2 * S], bank, ACT.Copy).then_inc(proj_act, 1)
            else:
                dst = {1: qT, 3: kT, 7: qT2, 9: kT2}[i]
                do(dst[:, 2:4, :], bank, ACT.Copy, scale=HD ** -0.5 if i == 7 else 1.0).then_inc(proj_act, 1)
        act.wait_ge(lam_sum, 1)
        do(lam_e[:], lam_s[:], ACT.Exp).then_inc(lam_exp, 1)

        for j in range(DIFF_H + 3):
            i = H0 + j
            if j < DIFF_H:
                exps(i, 2)
            if 2 <= j < DIFF_H + 2:
                pT_copy(i - 2, 4)
            if j >= 3:
                h = j - 3
                act.wait_ge(o_ps, H0 + h + 1)
                do(latT[:, h, :], ps[:, 6 + h % 2, 0:S], ACT.Copy).then_inc(o_sb, 1)
                act.wait_ge(o_sb, H0 + h + 1)
                do(lat_sq[:, h, :], latT[:, h, :], ACT.Square).then_inc(dn_sq, 1)

        for p in range(PAIRS + 2):
            if p < PAIRS:
                t, b0 = sc[:, p % 2, :, :], 4 * (p % 2)
                act.wait_ge(z_ps, p + 1)
                if p >= 2:
                    act.wait_ge(a_ps, p - 1)
                chain.link(do(t, ps[:, b0:b0 + 2, 0:TRI], ACT.Abs))
                chain.link(do(t, t, ACT.Exp, scale=-1.0))
                do(t, t, ACT.Ln, bias=1.0).then_inc(z_ln, 1)
            if p == 0:
                for first in (True, False):
                    wide_rsqrt_act(lat_v[:, 0:4, :], lat_t[:, 0:4, :], lat_r[:, 0:4, :], first)
            if 1 <= p <= PAIRS:
                act.wait_ge(a_sb, p)
                w = pr[:, (p - 1) % 2, :, :]
                do(w, w, ACT.Exp).then_inc(w_sb, 1)
            if p >= 2:
                act.wait_ge(so_ps, p - 1)
                for i in range(2):
                    rows = slice(64 * i, 64 * i + HD)
                    last = do(oT[rows, 4 + p - 2, :], ps[rows, 6 + i, 0:S], ACT.Copy)
                last.then_inc(so_sb, 1)

        out_squares(odd_unit_used, 12)
        next_input(3)

        act.wait_ge(router_sub, 1)
        do(r_e[:], r_e[:], ACT.Exp).then_inc(router_exp, 1)

        def gathered(s, n):
            own = (x_tok_act, x_tok_act1)[s]
            act.wait_ge(gath_ps[s], n + (CREDIT + 1))
            act.wait_ge(moe_s.x_lo[0], n + (CREDIT + s))
            act.wait_ge(moe_s.x_lo[1], n + CREDIT)
            for j in range(4, KT):
                last = do(x_tok[:, j, :], ps[:, 1, (j - 4) * P:(j - 3) * P], ACT.Identity,
                          scale=mod_scale[:, 3, j:j + 1], bias=mod_shift[:, 3, j:j + 1])
            last.then_inc(own, 1)

        def split(s, n):
            own, other = ((x_tok_act, x_tok_dve), (x_tok_act1, x_tok_dve1))[s]
            act.wait_ge(moe_s.gu[0], n * MOE_NB + CREDIT)
            act.wait_ge(own, n + 1)
            act.wait_ge(other, n + 1)
            do(x_hi[:, :, s * P:(s + 1) * P], x_tok[:], ACT.Copy).then_inc(moe_s.x_hi[s], 1)

        def gathered_second(flag, n):
            def work():
                gathered(1, n)
                split(1, n)

            def narrow():
                gathered(1, n)
                act.wait_ge(moe_s.gu[0], n * MOE_NB + CREDIT)
                act.wait_ge(x_tok_act1, n + 1)
                act.wait_ge(x_tok_dve1, n + 1)
                do(x_hi[:, :, P:P + NARROW], x_tok[:, :, 0:NARROW], ACT.Copy).then_inc(moe_s.x_hi[1], 1)
            with_second(act, flag, work, [x_tok_act1, moe_s.x_hi[1]], narrow)

        def last_outputs(flag, n):
            act.wait_ge(pick_gT_ps, n + (CREDIT + 1))
            act.wait_ge(scat_ps, n + CREDIT)
            do(pick_gT[:], ps[:, 2, :], ACT.Copy).then_inc(pick_gT_sb, 1)

            def chunk(c):
                act.wait_ge(moe_s.down[c], n * MOE_NB + CREDIT)
                do(y_tok[:, c, 512:D], ps[:, 5 + 2 * c, :], ACT.Copy).then_inc(ytok_act[c], 1)
            with_second(act, flag, lambda: chunk(1), [ytok_act[1]])
            chunk(0)

        def flag_at(i):
            return act.value_load(second[0:1, i], min_val=0, max_val=2)

        act.wait_ge(route_ready, 1)
        gathered(0, 0)
        split(0, 0)
        gathered_second(flag_at(slice(1, 2)), 0)
        with act.Fori(0, NE) as e:
            next_flag = []

            def fetch_next():
                next_flag.append(flag_at(bass.ds(e + 2, 1)))
                gathered(0, e + 1)

            def between():
                last_flag, flag = (flag_at(bass.ds(e + i, 1)) for i in range(2))
                last_outputs(last_flag, e)
                return flag

            ffn(moe_s, MOE0, MOE_NB, None, e, between=between,
                fetch_next=fetch_next)
            split(0, e + 1)
            gathered_second(next_flag[0], e + 1)
        last_outputs(flag_at(slice(NE, NE + 1)), NE)
        sqrt_table()
        act.wait_ge(y_added, NE + 2)
        for c in range(2):
            last = do(y_tok[:, c, :], y_sb[:, c, :], ACT.Square, accum_out=ssq[:, c:c + 1])
        last.then_inc(ssq_ready, 1)
        rsqrt_act(rs_v[:], rs_r[:])

    @block.vector
    def _(dve):
        chain = Chain(dve, dve_chain)
        v = nc.vector
        for f in (dense_s, moe_s):
            for s in (f.w_lo, *f.prod, *f.h_lo, *f.x_lo):
                dve.sem_inc(s, CREDIT)
        for s in (*ytok_dve, fold_added):
            dve.sem_inc(s, CREDIT)

        def normalise(m, ready=False):
            if not ready:
                ssq_count[0] += 1
                dve.wait_ge(ssq_ready, ssq_count[0])
            mean_dve([(ssq[:], D, rs_v[:])])
            rsqrt_dve(dve, chain, rs_v[:], rs_t[:], rs_r[:])

        ssq_count = [0]

        def prenorm(m):
            normalise(m)
            v.tensor_scalar(xn[:, 0, :], x_sb[:, 0, :], rs_r[:, 0:1], None, ALU.mult).then_inc(xn_dve, 1)

        def shift_scale(m):
            dve.wait_ge(mod_ps, m + 1)
            o = ps[:, MOD_BANK[m], :]
            v.tensor_tensor(mod_shift[:, m, :], o[:, 0:KT], ada_b_col[:, m, 0:KT], ALU.add)
            chain.link(v.tensor_tensor(mod_scale[:, m, :], o[:, KT:2 * KT], ada_b_col[:, m, KT:2 * KT], ALU.add))
            v.scalar_tensor_tensor(out=mod_scale[:, m, :], in0=mod_scale[:, m, :], scalar=1.0, in1=pre_col[:, m, :],
                                   op0=ALU.add, op1=ALU.mult).then_inc(mod_ready, 1)

        def gate(m):
            dve.wait_ge(gate_ps, m + 1)
            dve.wait_ge(rows_in, 32 * (m + 1))
            o = ps[:, GATE_BANK[m]:GATE_BANK[m] + 2, :].rearrange("p b n -> p (b n)")
            v.tensor_tensor(gate_row[:], o, gate_row[:], ALU.add).then_inc(gate_sb, 1)
            dve.wait_ge(gate_sb, m + 1)
            chain.link(v.tensor_tensor(gate_row[:], gate_row[:], post_row[:], ALU.mult))

        def modulated(m):
            dve.wait_ge(xT_ps, m + 1)
            dve.wait_ge(mod_ready, m + 1)
            for j in (0, 1, 4, 5):
                last = v.tensor_scalar(hT[:, j, :], ps[:, XT_BANK[m] + j // 2, (j % 2) * S:(j % 2 + 1) * S],
                                       mod_scale[:, m, j:j + 1], mod_shift[:, m, j:j + 1], ALU.mult, ALU.add)
            last.then_inc(hT_dve, 1)

        dve.wait_ge(c_ready, 1)
        def ada(n, u):
            g, kp = u // 4, u % 4
            un = Unit(n)
            un.wait(dve)
            acc = ada_fg[:, g * D:(g + 1) * D]
            for i in range(2):
                k = 2 * kp + i
                w = un.slot[:, i * D:(i + 1) * D]
                if k == 0:
                    ins = v.tensor_scalar(acc, w, c_silu[:, k:k + 1], None, ALU.mult)
                else:
                    ins = v.scalar_tensor_tensor(out=acc, in0=w, scalar=c_silu[:, k:k + 1], in1=acc, op0=ALU.mult, op1=ALU.add)
                if i == 0:
                    chain.link(ins)
            ins.then_inc(ada_unit_used, 1)
            dve.wait_ge(ada_unit_used, u + 1)
            if kp == 3:
                dve.sem_inc(ada_fg_ready, 1)

        for u in range(ADA_UNITS):
            if u == 4:
                prenorm(0)
            ada(u, u)
        dve.wait_ge(early_in, N_EARLY)
        shift_scale(0)
        modulated(0)
        dve.wait_ge(consts_in, N_CONSTS)

        dve.wait_ge(even_unit_used, 2)
        chain.link(v.tensor_copy(latT[NOPE:QK, 3, :], ps[NOPE:QK, 3, 0:S]))
        dve.wait_ge(even_unit_used, 3)
        v.tensor_copy(qT2[:, 0:2, :], ps[:, 4, :]).then_inc(proj_dve, 1)
        dve.wait_ge(lat_act, 1)
        dve.wait_ge(lat_ps, 1)
        mean_dve([(ps[:, 2, 0:S], Q_RANK, lat_v[:, 0, :]), (ps[:, 2, S:2 * S], KV_RANK, lat_v[:, 1, :])])
        rsqrt_dve(dve, chain, lat_v[:, 0:2, :], lat_t[:, 0:2, :], lat_r[:, 0:2, :], wide=True)
        for i in range(3):
            last = v.scalar_tensor_tensor(out=latT[:, i, :], in0=latT[:, i, :], scalar=vec_g[:, i:i + 1], in1=lat_r[:, i // 2, :],
                                          op0=ALU.mult, op1=ALU.mult)
        last.then_inc(lat_ready, 1)
        dve.wait_ge(even_unit_used, 5)
        v.tensor_copy(kT2[:, 0:2, :], ps[:, 6, :]).then_inc(proj_dve, 1)
        for i in range(2):
            ada(GATE0 + i, ADA_UNITS + i)
        dve.wait_ge(even_unit_used, 7)
        v.tensor_copy(qT[0:QK, 0:4, :], ps[0:QK, 4:6, :]).then_inc(proj_dve, 1)
        dve.wait_ge(knope_ps, 1)
        v.tensor_copy(kT[0:NOPE, 0:4, :], ps[0:NOPE, 0:2, :]).then_inc(proj_dve, 1)
        dve.wait_ge(even_unit_used, 8)
        v.tensor_copy(v1[:, 0, :], ps[:, 1, :]).then_inc(proj_dve, 1)
        R = slice(NOPE, QK)
        sin8 = k_sin[R, :].unsqueeze(1).to_broadcast([ROPE, MLA_H, S])
        cos8 = k_cos[R, :].unsqueeze(1).to_broadcast([ROPE, MLA_H, S])
        dve.wait_ge(rot_ps, 1)
        v.tensor_tensor(lat_v[R, 2, :], latT[R, 3, :], k_cos[R, :], ALU.mult)
        v.tensor_tensor(rope_t[R], ps[R, 4:8, :].rearrange("p b (h t) -> p (b h) t", h=2), sin8, ALU.mult)
        chain.link(v.tensor_tensor(lat_v[R, 3, :], ps[R, 0, 0:S], k_sin[R, :], ALU.mult))
        v.tensor_tensor(kT[R], lat_v[R, 2, :].unsqueeze(1).to_broadcast([ROPE, MLA_H, S]),
                        lat_v[R, 3, :].unsqueeze(1).to_broadcast([ROPE, MLA_H, S]), ALU.add)
        chain.link(v.tensor_tensor(qT[R], qT[R], cos8, ALU.mult))
        v.tensor_tensor(qT[R], qT[R], rope_t[R], ALU.add).then_inc(rope_ready, 1)
        for i in range(2, 4):
            ada(GATE0 + i, ADA_UNITS + i)
        dve.wait_ge(even_unit_used, 9)
        v.tensor_copy(v2[:, :, 0:S], ps[:, 3, :]).then_inc(proj_dve, 1)

        SEG = ((0, S), (S, TRI))
        H0 = DIL_H + MLA_H

        def scores(i, b0, biases, scale, first):
            dve.wait_ge(s_ps, i + 1)
            if i >= first + 2:
                dve.wait_ge(p_exp, i - 1)
            for m, b in enumerate(biases):
                last = v.scalar_tensor_tensor(out=sc[:, i % 2, m, :], in0=ps[:, b0 + m, 0:TRI], scalar=scale, in1=b,
                                              op0=ALU.mult, op1=ALU.add)
            last.then_inc(s_free, 1)
            dve.wait_ge(s_free, i + 1)
            for m in range(len(biases)):
                for g, (a, b) in enumerate(SEG):
                    last = v.tensor_reduce(nmax[:, i % 2, m, g:g + 1], sc[:, i % 2, m, a:b], AX.X, ALU.max, negate=True)
            last.then_inc(s_max, 1)

        def normalised(i):
            dve.wait_ge(p_exp, i + 1)
            r = rden[:, i % 2, 0, :]
            chain.link(v.reciprocal(r, den[:, i % 2, 0, :]))
            for g, (a, b) in enumerate(SEG):
                last = v.tensor_scalar(pr[:, i % 2, 0, a:b], pr[:, i % 2, 0, a:b], r[:, g:g + 1], None, ALU.mult)
            last.then_inc(p_ready, 1)

        for i in range(H0 + 1):
            if i < H0:
                if i == 0:
                    dve.wait_ge(bias_in, 32)
                b = bias[:, i, :] if i < DIL_H else k_causal[:]
                scores(i, i % 2, [b], (HD if i < DIL_H else QK) ** -0.5, 0)
            if i >= 1:
                normalised(i - 1)

        def gated_columns(used, n0, squared, after=None):
            for n in range(4):
                dve.wait_ge(used, n0 + n + 1)
                dve.wait_ge(y_squared, squared + n + 1)
                w = slice(n * UCOL, (n + 1) * UCOL)
                last = v.tensor_tensor(y_sb[:, :, w], ps[:, n, :].rearrange("p (c n) -> p c n", c=2),
                                       gate_row[:, w].unsqueeze(1).to_broadcast([P, 2, UCOL]), ALU.mult)
                if n == 3:
                    last.then_inc(y_gated, 1)
                if after:
                    after(n)

        def residual(m, gated, parts):
            if parts:
                chain.link(v.tensor_reduce(ssq[:], y_ssq[:], AX.X, ALU.add))
            normalise(m, ready=parts)
            dve.wait_ge(y_gated, m + 1)
            for c in range(2):
                v.scalar_tensor_tensor(out=x_sb[:, c, :], in0=gated[:, c, :], scalar=rs_r[:, c:c + 1], in1=x_sb[:, c, :],
                                       op0=ALU.mult, op1=ALU.add).then_inc(x_new, 1)
            dve.wait_ge(x_new, 2 * (m + 1))

        def next_input(m):
            residual(m - 1, y_sb, m != 2)
            prenorm(m)
            shift_scale(m)
            modulated(m)

        gate(0)

        def ffn(f, u0, nb, flag=None, e=None, between=None, added=None, fetch_next=None):
            blk0 = 0 if e is None else e * nb
            un0 = 0 if e is None else e * (3 * nb)

            def lo(t, idx, it=0):
                dve.wait_ge(f.w_hi, un0 + 6 * it + (idx + CREDIT + 1))
                v.tensor_tensor(w_lo[t][:], ring[(u0 + idx) % RING][:], w_hi[t][:].bitcast(F32), ALU.subtract).then_inc(f.w_lo, 1)

            def product(blk):
                def chunk(c):
                    dve.wait_ge(f.silu[c], blk + (CREDIT + 1))
                    dve.wait_ge(f.hT_ps[c], blk + CREDIT)
                    v.tensor_tensor(prod[:, c, :], ps[:, c, FB:2 * FB], g_silu[:, c, :], ALU.mult).then_inc(f.prod[c], 1)

                def narrow():
                    dve.wait_ge(fold_moved, blk + (CREDIT + 1))
                    v.tensor_tensor(folded[:], ps[0:NARROW, 1, :], folded[:], ALU.add).then_inc(fold_added, 1)
                    dve.wait_ge(fold_added, blk + (CREDIT + 1))
                    dve.wait_ge(f.silu[1], blk + (CREDIT + 1))
                    dve.wait_ge(f.hT_ps[1], blk + CREDIT)
                    v.tensor_tensor(prod[0:NARROW, 1, :], folded[:, FB:2 * FB], g_silu[0:NARROW, 1, :], ALU.mult).then_inc(f.prod[1], 1)
                with_second(dve, flag, lambda: chunk(1), [f.prod[1]], narrow, fold_added)
                chunk(0)

            def hidden(blk):
                def chunk(c):
                    dve.wait_ge(f.h_hi[c], blk + (CREDIT + 1))
                    v.tensor_tensor(h_lo[:, c, :], ps[:, 2 + c, 0:FB], h_hi[:, c, :].bitcast(F32), ALU.subtract).then_inc(f.h_lo[c], 1)

                def narrow():
                    dve.wait_ge(f.h_hi[1], blk + (CREDIT + 1))
                    parts = h_hi[:, 1, :].rearrange("p (i n) -> p i n", i=2)
                    src = ps[:, 3, 0:FB].rearrange("p (i n) -> p i n", i=2)
                    v.tensor_tensor(parts[:, :, NARROW:P], src[:, :, 0:NARROW], parts[:, :, 0:NARROW].bitcast(F32),
                                    ALU.subtract).then_inc(f.h_lo[1], 1)
                with_second(dve, flag, lambda: chunk(1), [f.h_lo[1]], narrow)
                chunk(0)

            def step(s, idx, it=0, added=None):
                lo(0, idx, it)
                product(blk0 + s)
                lo(1, idx + 1, it)
                if added:
                    added()
                hidden(blk0 + s)
                lo(2, idx + 2, it)

            if e is not None:
                lo(0, 0)
                lo(1, 1)
            if between:
                flag = between()
            step(0, 2, added=added)
            turns = (nb - 2) // 2
            with dve.Fori(0, turns) as it:
                step(2 * it + 1, 5, it)
                step(2 * it + 2, 8, it)
            for s in range(1 + 2 * turns, nb - 1):
                step(s, 2 + 3 * s)
            if fetch_next:
                fetch_next()
            lo(2, 3 * nb - 1)
            product(blk0 + nb - 1)
            hidden(blk0 + nb - 1)

        def first_weights(n):
            if 1 <= n < 3:
                dve.wait_ge(dense_s.w_hi, CREDIT + n)
                v.tensor_tensor(w_lo[n - 1][:], ring[(DENSE0 + n - 1) % RING][:], w_hi[n - 1][:].bitcast(F32),
                                ALU.subtract).then_inc(dense_s.w_lo, 1)

        gated_columns(even_unit_used, 10, 0, first_weights)
        next_input(1)
        dve.wait_ge(dense_s.x_hi[0], CREDIT + 1)
        v.tensor_tensor(x_lo[:], hT[:], x_hi[:].bitcast(F32), ALU.subtract).then_inc(dense_s.x_lo[0], 1)
        gate(1)
        ffn(dense_s, DENSE0, DENSE_NB)
        dve.wait_ge(dense_s.down[0], CREDIT + DENSE_NB)
        dve.wait_ge(dense_s.down[1], CREDIT + DENSE_NB)
        v.tensor_tensor(y_sb[:, 1, :], ps[:, 6:8, :].rearrange("p b n -> p (b n)"), gate_row[:], ALU.mult).then_inc(y_half, 1)
        dve.wait_ge(y_squared, 5)
        v.tensor_tensor(y_sb[:, 0, :], ps[:, 4:6, :].rearrange("p b n -> p (b n)"), gate_row[:], ALU.mult).then_inc(y_gated, 1)
        next_input(2)
        gate(2)

        for i in range(0, 12, 2):
            dve.wait_ge(odd_unit_used, i + 1)
            bank = ps[:, i % 8, :]
            if i in (4, 10):
                v.tensor_copy((v1 if i == 4 else v2)[:, :, 0:S], bank).then_inc(proj_dve, 1)
            elif i == 6:
                v.tensor_scalar(qT2[:, 0:2, :], bank, HD ** -0.5, None, ALU.mult).then_inc(proj_dve, 1)
            else:
                v.tensor_copy({0: qT, 2: kT, 8: kT2}[i][:, 0:2, :], bank).then_inc(proj_dve, 1)
        chain.link(v.tensor_tensor(lam_p[:], lam_in[:, 0::2, :], lam_in[:, 1::2, :], ALU.mult))
        v.tensor_reduce(lam_s[:], lam_p[:], AX.X, ALU.add).then_inc(lam_sum, 1)
        dve.wait_ge(lam_exp, 1)
        v.tensor_scalar(sub_scaled[:], vec_g[:, 3:4], 1.0 - LAM_INIT, None, ALU.mult)
        chain.link(v.scalar_tensor_tensor(out=lam[:], in0=lam_e[:, 0:1], scalar=LAM_INIT, in1=lam_e[:, 1:2],
                                          op0=ALU.add, op1=ALU.subtract))

        def difference(i):
            dve.wait_ge(p_exp, i + 1)
            chain.link(v.reciprocal(rden[:, i % 2, :, :], den[:, i % 2, :, :]))
            chain.link(v.tensor_scalar(rden[:, i % 2, 1, :], rden[:, i % 2, 1, :], lam[:], None, ALU.mult))
            for g, (a, b) in enumerate(SEG):
                chain.mark(v.tensor_scalar(pr[:, i % 2, 1, a:b], pr[:, i % 2, 1, a:b], rden[:, i % 2, 1, g:g + 1], None, ALU.mult))
            chain.wait()
            for g, (a, b) in enumerate(SEG):
                last = v.scalar_tensor_tensor(out=pr[:, i % 2, 0, a:b], in0=pr[:, i % 2, 0, a:b], scalar=rden[:, i % 2, 0, g:g + 1],
                                              in1=pr[:, i % 2, 1, a:b], op0=ALU.mult, op1=ALU.subtract)
            last.then_inc(p_ready, 1)

        dve.wait_ge(bias_in, 64)
        for j in range(DIFF_H + 1):
            i = H0 + j
            if j < DIFF_H:
                scores(i, 2 * (i % 2), [bias[:, 2 * j, :], bias[:, 2 * j + 1, :]], HD ** -0.5, H0)
            if j >= 1:
                difference(i - 1)
        for p in range(PAIRS + 1):
            if p == 0:
                dve.wait_ge(dn_ps, 1)
                mean_dve([(ps[:, 4:6, :].rearrange("p b (h t) -> p (b h) t", h=2), 2 * HD, lat_v[:, 0:4, :])])
            if p < PAIRS:
                t, b0 = sc[:, p % 2, :, :], 4 * (p % 2)
                dve.wait_ge(z_ln, p + 1)
                chain.link(v.scalar_tensor_tensor(out=t, in0=ps[:, b0:b0 + 2, 0:TRI], scalar=0.0, in1=t, op0=ALU.max, op1=ALU.add))
                v.tensor_tensor(t, t, k_strict01[:].unsqueeze(1).to_broadcast([P, 2, TRI]), ALU.mult).then_inc(z_sp, 1)
            if p >= 1:
                dve.wait_ge(a_ps, p)
                if p >= 3:
                    dve.wait_ge(so_ps, p - 2)
                v.tensor_tensor(pr[:, (p - 1) % 2, :, :], ps[:, 2:4, 0:TRI], k_strict[:].unsqueeze(1).to_broadcast([P, 2, TRI]),
                                ALU.add).then_inc(a_sb, 1)
            if p == 1:
                rsqrt_dve(dve, chain, lat_v[:, 0:4, :], lat_t[:, 0:4, :], lat_r[:, 0:4, :], wide=True)
                v.scalar_tensor_tensor(out=oT[:, 0:4, :], in0=latT[:, 0:4, :], scalar=sub_scaled[:], in1=lat_r[:, 0:4, :],
                                       op0=ALU.mult, op1=ALU.mult).then_inc(dn_done, 1)

        gated_columns(odd_unit_used, 12, 5)
        next_input(3)
        gate(3)

        v.memset(slot_of[:], 0.0)
        v.memset(gate_of[:], 0.0)
        v.memset(slot2_of[:], 0.0)
        v.memset(second[:], 0)
        v.memset(prod[:], 0.0)
        v.memset(y_sb[:], 0.0).then_inc(y_added, 1)
        dve.wait_ge(y_added, 1)
        dve.wait_ge(router_ps, 1)
        chain.link(v.tensor_tensor(r_log[:], ps[:, 0, 0:2 * NE].rearrange("p (c n) -> p c n", c=2),
                                   rb_row[:].unsqueeze(1).to_broadcast([P, 2, NE]), ALU.add))
        for c in range(2):
            chain.mark(v.max(r_max[:, c, :], r_log[:, c, :]))
        chain.wait()
        for c in range(2):
            chain.mark(v.max_index(r_idx[:, c, :], r_max[:, c, :], r_log[:, c, :]))
        v.tensor_tensor(r_e[:], r_max[:, :, 1], r_max[:, :, 0], ALU.subtract).then_inc(router_sub, 1)
        chain.wait()
        chain.link(v.tensor_copy(r_idxf[:], r_idx[:]))
        for c in range(2):
            for m, mask in enumerate((r_m0, r_m1)):
                chain.mark(v.tensor_scalar(mask[:, c, :], k_iota[:, 0:NE], r_idxf[:, c, m:m + 1], None, ALU.is_equal))
        chain.wait()
        v.tensor_tensor(r_mask[:], r_m0[:], r_m1[:], ALU.add).then_inc(router_mask, 1)
        dve.wait_ge(router_mask, 1)
        dve.wait_ge(pos_ps, 1)
        chain.mark(v.scalar_tensor_tensor(out=slot_of[:, :, 1:1 + NE], in0=ps[:, 1, 0:2 * NE].rearrange("p (c n) -> p c n", c=2),
                                          scalar=1.0, in1=r_mask[:], op0=ALU.add, op1=ALU.mult))
        for i, most in enumerate((P, P + NARROW)):
            chain.mark(v.tensor_scalar(r_many[:, i, :], ps[:, 1, 2 * NE:3 * NE], most + 0.5, None, ALU.is_gt))
        chain.wait()
        chain.mark(v.tensor_scalar(slot_of[:], slot_of[:], -1.0, None, ALU.add))
        chain.link(v.tensor_tensor(second[0:1, 1:1 + NE], r_many[0:1, 0, :], r_many[0:1, 1, :], ALU.add))
        chain.link(v.tensor_tensor(r_many[:, 0, :], r_many[:, 0, :], r_many[:, 1, :], ALU.subtract))
        v.scalar_tensor_tensor(out=slot2_of[:, :, 1:1 + NE], in0=r_many[:, 0, :].unsqueeze(1).to_broadcast([P, 2, NE]),
                               scalar=float(NARROW), in1=slot_of[:, :, 1:1 + NE], op0=ALU.mult, op1=ALU.add).then_inc(route_ready, 1)
        dve.wait_ge(route_ready, 1)

        def picks(col):
            for c in range(2):
                last = v.tensor_scalar(pick[:, c, :], k_iota[:], slot_of[:, c, col], None, ALU.is_equal)
            last.then_inc(pick_ready, 1)

        def last_picks(n, col):
            dve.wait_ge(pick_gT_ps, n + CREDIT)
            both = P + NARROW
            for c in range(2):
                v.tensor_scalar(pick_g[:, c, 0:both], k_iota[:, 0:both], slot_of[:, c, col], gate_of[:, c, col], ALU.is_equal, ALU.mult)
                last = v.tensor_scalar(pick_g[:, c, both:S], k_iota[:, both:S], slot2_of[:, c, col], gate_of[:, c, col],
                                       ALU.is_equal, ALU.mult)
            last.then_inc(pick_g_ready, 1)

        def gathered(s, n):
            own = (x_tok_dve, x_tok_dve1)[s]
            dve.wait_ge(gath_ps[s], n + (CREDIT + 1))
            dve.wait_ge(moe_s.x_lo[0], n + (CREDIT + s))
            dve.wait_ge(moe_s.x_lo[1], n + CREDIT)
            t = x_tok[:, 0:4, :]
            v.tensor_tensor(t, ps[:, 0, :].rearrange("p (j n) -> p j n", j=4), mod_scale[:, 3, 0:4].unsqueeze(2).to_broadcast([P, 4, P]),
                            ALU.mult).then_inc(x_tok_mul[s], 1)
            dve.wait_ge(x_tok_mul[s], n + 1)
            v.tensor_tensor(t, t, mod_shift[:, 3, 0:4].unsqueeze(2).to_broadcast([P, 4, P]), ALU.add).then_inc(own, 1)

        def split(s, n):
            own, other = ((x_tok_dve, x_tok_act), (x_tok_dve1, x_tok_act1))[s]
            dve.wait_ge(own, n + 1)
            dve.wait_ge(other, n + 1)
            dve.wait_ge(moe_s.x_hi[s], n + (CREDIT + 1))
            v.tensor_tensor(x_lo[:, :, s * P:(s + 1) * P], x_tok[:], x_hi[:, :, s * P:(s + 1) * P].bitcast(F32),
                            ALU.subtract).then_inc(moe_s.x_lo[s], 1)

        def gathered_second(flag, n):
            def work():
                gathered(1, n)
                split(1, n)

            def narrow():
                gathered(1, n)
                dve.wait_ge(x_tok_dve1, n + 1)
                dve.wait_ge(x_tok_act1, n + 1)
                dve.wait_ge(moe_s.x_hi[1], n + (CREDIT + 1))
                v.tensor_tensor(x_hi[:, :, P + NARROW:S], x_tok[:, :, 0:NARROW], x_hi[:, :, P:P + NARROW].bitcast(F32),
                                ALU.subtract).then_inc(moe_s.x_lo[1], 1)
            with_second(dve, flag, work, [x_tok_mul[1], x_tok_dve1, moe_s.x_lo[1]], narrow)

        def last_outputs(flag, n):
            def chunk(c):
                dve.wait_ge(moe_s.down[c], n * MOE_NB + CREDIT)
                dve.wait_ge(scat_ps, n + CREDIT)
                v.tensor_copy(y_tok[:, c, 0:512], ps[:, 4 + 2 * c, :]).then_inc(ytok_dve[c], 1)
            with_second(dve, flag, lambda: chunk(1), [ytok_dve[1]])
            chunk(0)

        def add_scattered(n):
            dve.wait_ge(scat_ps, n + (CREDIT + 1))
            dve.wait_ge(y_added, n + 1)
            for c in range(2):
                last = v.tensor_tensor(y_sb[:, c, :], ps[:, 4 + 2 * c:6 + 2 * c, :].rearrange("p b n -> p (b n)"), y_sb[:, c, :], ALU.add)
            last.then_inc(y_added, 1)

        def flag_at(i):
            return dve.value_load(second[0:1, i], min_val=0, max_val=2)

        picks(slice(1, 2))
        dve.wait_ge(router_exp, 1)
        chain.link(v.tensor_scalar(r_w0[:], r_e[:], 1.0, None, ALU.add))
        chain.link(v.reciprocal(r_w0[:], r_w0[:]))
        chain.link(v.tensor_tensor(r_w1[:], r_e[:], r_w0[:], ALU.mult))
        for c in range(2):
            chain.mark(v.tensor_scalar(r_m0[:, c, :], r_m0[:, c, :], r_w0[:, c:c + 1], None, ALU.mult))
        chain.wait()
        for c in range(2):
            chain.mark(v.scalar_tensor_tensor(out=gate_of[:, c, 1:1 + NE], in0=r_m1[:, c, :], scalar=r_w1[:, c:c + 1], in1=r_m0[:, c, :],
                                              op0=ALU.mult, op1=ALU.add))
        chain.wait()
        gathered(0, 0)
        split(0, 0)
        gathered_second(flag_at(slice(1, 2)), 0)
        with dve.Fori(0, NE) as e:
            next_flag = []

            def fetch_next():
                next_flag.append(flag_at(bass.ds(e + 2, 1)))
                gathered(0, e + 1)

            def between():
                last_flag, flag = (flag_at(bass.ds(e + i, 1)) for i in range(2))
                last_outputs(last_flag, e)
                picks(bass.ds(e + 2, 1))
                return flag

            last_picks(e, bass.ds(e, 1))
            ffn(moe_s, MOE0, MOE_NB, None, e, between=between, added=lambda: add_scattered(e),
                fetch_next=fetch_next)
            split(0, e + 1)
            gathered_second(next_flag[0], e + 1)
        last_picks(NE, slice(NE, NE + 1))
        last_outputs(flag_at(slice(NE, NE + 1)), NE)
        add_scattered(NE)
        dve.wait_ge(y_added, NE + 2)
        for c in range(2):
            last = v.tensor_tensor(xn[:, c, :], y_sb[:, c, :], gate_row[:], ALU.mult)
        last.then_inc(y_gated, 1)
        residual(3, xn, False)

    ctx.close()


def kernel(**inputs):
    import concourse.bacc as bacc
    from concourse.bass_utils import run_bass_kernel_spmd

    nc = bacc.Bacc("TRN2", target_bir_lowering=False, num_devices=1)
    arrays = {name: np.ascontiguousarray(inputs[name]) for name in _INS}
    for name, mix, ffn in (("ada_w", "ada_mix_w", "ada_ffn_w"), ("ada_b", "ada_mix_b", "ada_ffn_b"),
                           ("pre_g", "mix_pre_g", "ffn_pre_g"), ("post_g", "mix_post_g", "ffn_post_g")):
        a, b = np.asarray(inputs[mix]), np.asarray(inputs[ffn])
        arrays[name] = np.stack([a[0], b[0], a[1], b[1]])
    def columns(a, lead=0):
        a = np.asarray(a)
        a = a.reshape(a.shape[:lead] + (a.shape[lead] // P, P) + a.shape[lead + 1:])
        return np.ascontiguousarray(np.moveaxis(a, lead + 1, 0))

    arrays["c_cols"] = columns(inputs["c"][0])
    arrays["ada_b_cols"] = columns(arrays["ada_b"][:, 0:2 * D], 1)
    arrays["pre_cols"] = columns(arrays["pre_g"], 1)
    arrays["vec_cols"] = np.concatenate([columns(inputs[n][0]) for n in ("e_q_norm_g", "e_kv_norm_g", "diff_sub_g")], 1)
    arrays["router_cols"] = columns(inputs["router_w"][0])
    del arrays["pre_g"]
    arrays.update(shape_constants())
    aps = {}
    for name, a in arrays.items():
        aps[name] = nc.dram_tensor(f"in_{name}", a.shape, mybir.dt.from_np(a.dtype), kind="ExternalInput").ap()
    out = nc.dram_tensor("out_0", (1, S, D), F32, kind="ExternalOutput").ap()
    build(nc, aps, out)
    r = run_bass_kernel_spmd(nc, [{f"in_{name}": a for name, a in arrays.items()}], core_ids=[0])
    return r.results[0]["out_0"]
```
